# Optimizing a Trainium2 kernel written in Bass

```python
import functools
import jax, jax.numpy as jnp
from jax import lax
import numpy as np

D_MODEL = 1024
BATCH = 1
SEQ = 512
DEPTH = 2
DEC_BATCH = 8
DEC_SEQ = 4
PAST_LEN = 512
PAGE_SIZE = 128

MIX_WIDTH = D_MODEL
W_A = MIX_WIDTH // 4
W_B = MIX_WIDTH // 4
W_C = MIX_WIDTH // 4
W_D = MIX_WIDTH - W_A - W_B - W_C

A_HEADS = 4
A_HEAD_DIM = W_A // A_HEADS
ROT_DIM = A_HEAD_DIM // 4
ROPE_THETA = 500000.0
IDX_HEADS = 4
IDX_DIM = 32
IDX_ROT_DIM = IDX_DIM // 4
TOPK_MAX = 256
Q_BLOCK = 128

B_HEAD = 64
B_HEADS = W_B // B_HEAD
DECAY_LORA = 32
AAA_LORA = 32
GATE_LORA = 64
B_PROJ = 3 * W_B + DECAY_LORA + AAA_LORA + GATE_LORA
LNX_EPS = 64e-5

C_CONV = 3

D_HEADS = 4
D_BLOCK = W_D // D_HEADS
D_CONV = 4
LRU_C = 8.0

N_EXPERTS = 16
N_GROUPS = 4
EXPERTS_PER_GROUP = N_EXPERTS // N_GROUPS
TOP_K_EXPERTS = 2
D_EXPERT = 256

LN_EPS = 1e-5
DEEPNORM_ALPHA = (2 * DEPTH) ** 0.25
DEEPNORM_BETA = (8 * DEPTH) ** -0.25

A_Q = 0
A_K = A_Q + W_A
A_V = A_K + W_A
A_QI = A_V + W_A
A_KI = A_QI + IDX_HEADS * IDX_DIM
A_WI = A_KI + IDX_DIM
A_END = A_WI + IDX_HEADS
B_START = A_END
B_END = B_START + B_PROJ
C_START = B_END
C_END = C_START + 3 * W_C
D_START = C_END
D_END = D_START + 2 * W_D
IN_COLS = D_END

kernel_name = 'hymba_dsa_rwkv7_conv_rglru_moe_step'

def layer_norm(x, g, b):
    xf = x.astype(jnp.float32)
    mu = jnp.mean(xf, -1, keepdims=True)
    var = jnp.mean(jnp.square(xf - mu), -1, keepdims=True)
    return ((xf - mu) * lax.rsqrt(var + LN_EPS) * g + b).astype(x.dtype)

def rope_partial(x, pos, rot_dim):
    half = rot_dim // 2
    inv_freq = ROPE_THETA ** (-jnp.arange(half, dtype=jnp.float32) / half)
    ang = pos.astype(jnp.float32)[:, None] * inv_freq[None, :]
    cos = jnp.cos(ang)[:, None, :].astype(x.dtype)
    sin = jnp.sin(ang)[:, None, :].astype(x.dtype)
    x1, x2, rest = x[..., :half], x[..., half:rot_dim], x[..., rot_dim:]
    return jnp.concatenate([x1 * cos - x2 * sin, x2 * cos + x1 * sin, rest], axis=-1)

def causal_dwconv(x, buf, w):
    width = w.shape[0]
    t = x.shape[1]
    xx = jnp.concatenate([buf.astype(x.dtype), x], axis=1)
    out = w[0] * xx[:, 0:t]
    for j in range(1, width):
        out = out + w[j] * xx[:, j:j + t]
    return out, xx[:, t:]

def gather_pages(pool, layer, page_table):
    g = pool[layer, page_table]
    return g.reshape((page_table.shape[0], -1) + pool.shape[3:])

def dsa_attend(q, qi, wi, k, v, ki, q_pos, topk):
    f32 = jnp.float32
    n_keys = k.shape[1]
    dots = jnp.einsum('bthd,bsd->bths', qi.astype(f32), ki.astype(f32)) * IDX_DIM ** -0.5
    score = jnp.einsum('bth,bths->bts', wi.astype(f32), jax.nn.relu(dots))
    admissible = jnp.arange(n_keys)[None, :] <= q_pos[:, None]
    score = jnp.where(admissible[None], score, -jnp.inf)
    _, sel = lax.top_k(score, topk)
    valid = sel <= q_pos[None, :, None]
    take = jax.vmap(lambda arr, ix: arr[ix])
    k_sel = take(k, sel)
    v_sel = take(v, sel)
    logits = jnp.einsum('bthd,btkhd->bthk', q.astype(f32), k_sel.astype(f32)) * A_HEAD_DIM ** -0.5
    logits = jnp.where(valid[:, :, None, :], logits, -jnp.inf)
    p = jax.nn.softmax(logits, axis=-1)
    return jnp.einsum('bthk,btkhd->bthd', p.astype(v.dtype), v_sel)

def dsa_prompt(q, k, v, qi, ki, wi):
    b, t = q.shape[0], q.shape[1]
    nb = t // Q_BLOCK
    topk = min(TOPK_MAX, t // 4)

    def blockify(a):
        return jnp.swapaxes(a.reshape((b, nb, Q_BLOCK) + a.shape[2:]), 0, 1)

    pos = jnp.arange(t).reshape(nb, Q_BLOCK)
    out = lax.map(lambda a: dsa_attend(a[0], a[1], a[2], k, v, ki, a[3], topk),
                  (blockify(q), blockify(qi), blockify(wi), pos))
    return jnp.swapaxes(out, 0, 1).reshape(b, t, A_HEADS, A_HEAD_DIM)

def dsa_sample(q, k, v, qi, ki, wi, past):
    past_k, past_v, past_ki = past
    k_all = jnp.concatenate([past_k.astype(k.dtype), k], axis=1)
    v_all = jnp.concatenate([past_v.astype(v.dtype), v], axis=1)
    ki_all = jnp.concatenate([past_ki.astype(ki.dtype), ki], axis=1)
    n_keys = k_all.shape[1]
    q_pos = past_k.shape[1] + jnp.arange(q.shape[1])
    return dsa_attend(q, qi, wi, k_all, v_all, ki_all, q_pos, min(TOPK_MAX, n_keys // 4))

def rwkv7_scan(r, w, k, v, a_vec, b_vec, state):
    def step(s, inp):
        r_t, w_t, k_t, v_t, a_t, b_t = inp
        sa = jnp.einsum('bhvk,bhk->bhv', s, a_t)
        s = s * w_t[:, :, None, :] + sa[..., None] * b_t[:, :, None, :] + v_t[..., None] * k_t[:, :, None, :]
        return s, jnp.einsum('bhvk,bhk->bhv', s, r_t)
    xs = tuple(jnp.moveaxis(z, 1, 0) for z in (r, w, k, v, a_vec, b_vec))
    s, ys = lax.scan(step, state, xs)
    return jnp.moveaxis(ys, 0, 1), s

def rwkv7_mix(p, shift_buf, state, lp):
    f32 = jnp.float32
    b, t = p.shape[0], p.shape[1]
    prev = jnp.concatenate([shift_buf.astype(p.dtype), p[:, :-1]], axis=1)
    z = p + (prev - p) * lp['rwkv_mu']
    r, k, v, wl, al, gl = jnp.split(z, [W_B, 2 * W_B, 3 * W_B, 3 * W_B + DECAY_LORA,
                                        3 * W_B + DECAY_LORA + AAA_LORA], axis=-1)
    w_log = -jax.nn.softplus(-(lp['rwkv_w0'] + jnp.tanh(wl) @ lp['rwkv_w2']).astype(f32)) - 0.5
    decay = jnp.exp(-jnp.exp(w_log))
    a = jax.nn.sigmoid((lp['rwkv_a0'] + al @ lp['rwkv_a2']).astype(f32))
    g = (jax.nn.sigmoid(gl) @ lp['rwkv_g2']).astype(f32)

    def heads(u):
        return u.astype(f32).reshape(b, t, B_HEADS, B_HEAD)

    kk = heads(k * lp['rwkv_kk'])
    kk = kk / jnp.maximum(jnp.sqrt(jnp.sum(kk * kk, -1, keepdims=True)), 1e-12)
    kf = k.astype(f32) * (1.0 + (a - 1.0) * lp['rwkv_ka'].astype(f32))
    rh, kh, vh, ah = heads(r), heads(kf), heads(v), heads(a)
    y, s_new = rwkv7_scan(rh, heads(decay), kh, vh, -kk, kk * ah, state.astype(f32))
    mu = jnp.mean(y, -1, keepdims=True)
    var = jnp.mean(jnp.square(y - mu), -1, keepdims=True)
    y = ((y - mu) * lax.rsqrt(var + LNX_EPS)).reshape(b, t, W_B) * lp['rwkv_lnx_g'] + lp['rwkv_lnx_b']
    bonus = jnp.sum(rh * kh * lp['rwkv_rk'].astype(f32), -1, keepdims=True) * vh
    y = (y + bonus.reshape(b, t, W_B)) * g
    return y.astype(p.dtype), s_new.astype(state.dtype), p[:, -1:]

def gated_short_conv(p, buf, conv_w):
    bg, cg, xin = jnp.split(p, 3, axis=-1)
    y, new_buf = causal_dwconv(cg * xin, buf, conv_w)
    return bg * y, new_buf

def lru_scan(a, u, h0):
    def step(h, inp):
        h = inp[0] * h + inp[1]
        return h, h
    h, hs = lax.scan(step, h0, (jnp.moveaxis(a, 1, 0), jnp.moveaxis(u, 1, 0)))
    return jnp.moveaxis(hs, 0, 1), h

def rglru_block(p, buf, h0, lp):
    f32 = jnp.float32
    b, t = p.shape[0], p.shape[1]
    xb, gb = jnp.split(p, 2, axis=-1)
    xc, new_buf = causal_dwconv(xb, buf, lp['convd_w'])
    xc = xc + lp['convd_b']
    xh = xc.reshape(b, t, D_HEADS, D_BLOCK)
    gate_x = jax.nn.sigmoid((jnp.einsum('bthi,hij->bthj', xh, lp['lru_gx_w']).reshape(b, t, W_D)
                             + lp['lru_gx_b']).astype(f32))
    gate_a = jax.nn.sigmoid((jnp.einsum('bthi,hij->bthj', xh, lp['lru_ga_w']).reshape(b, t, W_D)
                             + lp['lru_ga_b']).astype(f32))
    log_a = -LRU_C * gate_a * jax.nn.softplus(-lp['lru_lam'].astype(f32))
    u = jnp.sqrt(-jnp.expm1(2.0 * log_a)) * gate_x * xc.astype(f32)
    hs, h = lru_scan(jnp.exp(log_a), u, h0.astype(f32))
    y = hs * jax.nn.gelu(gb.astype(f32))
    return y.astype(p.dtype), new_buf, h.astype(h0.dtype)

def moe(x, w_router, router_bias, w_gate, w_up, w_down):
    f32 = jnp.float32
    shp = x.shape
    xf = x.reshape(-1, shp[-1])
    n = xf.shape[0]
    s = jax.nn.sigmoid((xf @ w_router).astype(f32))
    sel = (s + router_bias.astype(f32)).reshape(n, N_GROUPS, EXPERTS_PER_GROUP)
    group_score = jnp.sum(lax.top_k(sel, TOP_K_EXPERTS)[0], -1)
    g_idx = jnp.argmax(group_score, -1)
    in_grp = jnp.take_along_axis(sel, g_idx[:, None, None], axis=1)[:, 0]
    _, local = lax.top_k(in_grp, TOP_K_EXPERTS)
    e_idx = g_idx[:, None] * EXPERTS_PER_GROUP + local
    w_sel = jnp.take_along_axis(s, e_idx, axis=1)
    w_sel = w_sel / jnp.sum(w_sel, -1, keepdims=True)
    gates = jnp.sum(jax.nn.one_hot(e_idx, N_EXPERTS, dtype=f32) * w_sel[..., None], axis=1)
    h = jax.nn.silu(jnp.einsum('nd,edf->nef', xf, w_gate)) * jnp.einsum('nd,edf->nef', xf, w_up)
    y = jnp.einsum('nef,efd->nd', h * gates[:, :, None].astype(h.dtype), w_down)
    return y.reshape(shp)

def layer_step(x, pos, lp, attn, rwkv_state, shift_buf, convc_buf, convd_buf, lru_h, w_router, router_bias):
    b, t = x.shape[0], x.shape[1]
    cols = x @ lp['w_in']
    q = rope_partial(cols[..., A_Q:A_K].reshape(b, t, A_HEADS, A_HEAD_DIM), pos, ROT_DIM)
    k = rope_partial(cols[..., A_K:A_V].reshape(b, t, A_HEADS, A_HEAD_DIM), pos, ROT_DIM)
    v = cols[..., A_V:A_QI].reshape(b, t, A_HEADS, A_HEAD_DIM)
    qi = rope_partial(cols[..., A_QI:A_KI].reshape(b, t, IDX_HEADS, IDX_DIM), pos, IDX_ROT_DIM)
    ki = layer_norm(cols[..., A_KI:A_WI], lp['idx_ln_g'], lp['idx_ln_b'])
    ki = rope_partial(ki[:, :, None, :], pos, IDX_ROT_DIM)[:, :, 0]
    wi = cols[..., A_WI:A_END] * IDX_HEADS ** -0.5
    y_a = attn(q, k, v, qi, ki, wi).reshape(b, t, W_A)
    y_b, rwkv_state, shift_buf = rwkv7_mix(cols[..., B_START:B_END], shift_buf, rwkv_state, lp)
    y_c, convc_buf = gated_short_conv(cols[..., C_START:C_END], convc_buf, lp['convc_w'])
    y_d, convd_buf, lru_h = rglru_block(cols[..., D_START:D_END], convd_buf, lru_h, lp)
    mix = jnp.concatenate([y_a, y_b, y_c, y_d], axis=-1) @ lp['w_out']
    x = layer_norm(DEEPNORM_ALPHA * x + mix, lp['ln1_g'], lp['ln1_b'])
    ffn = moe(x, w_router, router_bias, lp['moe_w_gate'], lp['moe_w_up'], lp['moe_w_down'])
    x = layer_norm(DEEPNORM_ALPHA * x + ffn, lp['ln2_g'], lp['ln2_b'])
    return x, (k, v, ki, rwkv_state, shift_buf, convc_buf, convd_buf, lru_h)

def setup_inputs(seed: int = 0) -> dict:
    key = jax.random.key(seed)
    keys = iter(jax.random.split(key, 64))

    def nrm(shape, scale=1.0):
        return jax.random.normal(next(keys), shape, jnp.float32) * scale

    def unif(shape, lo, hi):
        return jax.random.uniform(next(keys), shape, jnp.float32, lo, hi)

    n_pages = PAST_LEN // PAGE_SIZE
    n_phys = (DEC_BATCH * n_pages * 5) // 4
    page_table = jax.random.permutation(next(keys), n_phys)[:DEC_BATCH * n_pages]
    page_table = page_table.reshape(DEC_BATCH, n_pages).astype(jnp.int32)
    lam_base = unif((DEPTH, W_D), 0.81, 0.998) ** (1.0 / LRU_C)
    lru_lam = jnp.log(lam_base) - jnp.log1p(-lam_base)
    return {
        'x_prompt': nrm((BATCH, SEQ, D_MODEL)),
        'x_sample': nrm((DEC_BATCH, DEC_SEQ, D_MODEL)),
        'cache_k': nrm((DEPTH, n_phys, PAGE_SIZE, A_HEADS, A_HEAD_DIM)),
        'cache_v': nrm((DEPTH, n_phys, PAGE_SIZE, A_HEADS, A_HEAD_DIM)),
        'cache_ik': nrm((DEPTH, n_phys, PAGE_SIZE, IDX_DIM)),
        'page_table': page_table,
        'state_rwkv': nrm((DEPTH, DEC_BATCH, B_HEADS, B_HEAD, B_HEAD), 0.3),
        'state_rwkv_shift': nrm((DEPTH, DEC_BATCH, 1, B_PROJ)),
        'state_conv_c': nrm((DEPTH, DEC_BATCH, C_CONV - 1, W_C)),
        'state_conv_d': nrm((DEPTH, DEC_BATCH, D_CONV - 1, W_D)),
        'state_lru': nrm((DEPTH, DEC_BATCH, W_D), 0.5),
        'w_in': nrm((DEPTH, D_MODEL, IN_COLS), D_MODEL ** -0.5),
        'w_out': nrm((DEPTH, MIX_WIDTH, D_MODEL), MIX_WIDTH ** -0.5 * DEEPNORM_BETA),
        'idx_ln_g': 1.0 + nrm((DEPTH, IDX_DIM), 0.01),
        'idx_ln_b': nrm((DEPTH, IDX_DIM), 0.01),
        'rwkv_mu': unif((DEPTH, B_PROJ), 0.0, 1.0),
        'rwkv_w0': unif((DEPTH, W_B), -4.0, 0.0),
        'rwkv_w2': nrm((DEPTH, DECAY_LORA, W_B), 0.1),
        'rwkv_a0': nrm((DEPTH, W_B), 0.1),
        'rwkv_a2': nrm((DEPTH, AAA_LORA, W_B), 0.1),
        'rwkv_g2': nrm((DEPTH, GATE_LORA, W_B), GATE_LORA ** -0.5),
        'rwkv_kk': 0.85 + nrm((DEPTH, W_B), 0.05),
        'rwkv_ka': 1.0 + nrm((DEPTH, W_B), 0.05),
        'rwkv_rk': nrm((DEPTH, B_HEADS, B_HEAD), 0.1),
        'rwkv_lnx_g': 1.0 + nrm((DEPTH, W_B), 0.01),
        'rwkv_lnx_b': nrm((DEPTH, W_B), 0.01),
        'convc_w': nrm((DEPTH, C_CONV, W_C), C_CONV ** -0.5),
        'convd_w': nrm((DEPTH, D_CONV, W_D), D_CONV ** -0.5),
        'convd_b': nrm((DEPTH, W_D), 0.01),
        'lru_gx_w': nrm((DEPTH, D_HEADS, D_BLOCK, D_BLOCK), D_BLOCK ** -0.5),
        'lru_gx_b': nrm((DEPTH, W_D), 0.01),
        'lru_ga_w': nrm((DEPTH, D_HEADS, D_BLOCK, D_BLOCK), D_BLOCK ** -0.5),
        'lru_ga_b': nrm((DEPTH, W_D), 0.01),
        'lru_lam': lru_lam,
        'ln1_g': 1.0 + nrm((DEPTH, D_MODEL), 0.01),
        'ln1_b': nrm((DEPTH, D_MODEL), 0.01),
        'ln2_g': 1.0 + nrm((DEPTH, D_MODEL), 0.01),
        'ln2_b': nrm((DEPTH, D_MODEL), 0.01),
        'w_router': nrm((D_MODEL, N_EXPERTS), D_MODEL ** -0.5),
        'router_bias': nrm((N_EXPERTS,), 0.01),
        'moe_w_gate': nrm((DEPTH, N_EXPERTS, D_MODEL, D_EXPERT), D_MODEL ** -0.5),
        'moe_w_up': nrm((DEPTH, N_EXPERTS, D_MODEL, D_EXPERT), D_MODEL ** -0.5),
        'moe_w_down': nrm((DEPTH, N_EXPERTS, D_EXPERT, D_MODEL), D_EXPERT ** -0.5 * DEEPNORM_BETA),
    }

def reference(x_prompt, x_sample, cache_k, cache_v, cache_ik, page_table, state_rwkv, state_rwkv_shift,
              state_conv_c, state_conv_d, state_lru, w_in, w_out, idx_ln_g, idx_ln_b, rwkv_mu, rwkv_w0,
              rwkv_w2, rwkv_a0, rwkv_a2, rwkv_g2, rwkv_kk, rwkv_ka, rwkv_rk, rwkv_lnx_g, rwkv_lnx_b,
              convc_w, convd_w, convd_b, lru_gx_w, lru_gx_b, lru_ga_w, lru_ga_b, lru_lam,
              ln1_g, ln1_b, ln2_g, ln2_b, w_router, router_bias, moe_w_gate, moe_w_up, moe_w_down):
    bp, tp = x_prompt.shape[0], x_prompt.shape[1]
    ts = x_sample.shape[1]
    dt = x_prompt.dtype
    pos_p = jnp.arange(tp)
    pos_s = PAST_LEN + jnp.arange(ts)
    xp, xs = x_prompt, x_sample
    new_p = [[] for _ in range(8)]
    new_s = [[] for _ in range(8)]
    for l in range(DEPTH):
        lp = {
            'w_in': w_in[l], 'w_out': w_out[l], 'idx_ln_g': idx_ln_g[l], 'idx_ln_b': idx_ln_b[l],
            'rwkv_mu': rwkv_mu[l], 'rwkv_w0': rwkv_w0[l], 'rwkv_w2': rwkv_w2[l], 'rwkv_a0': rwkv_a0[l],
            'rwkv_a2': rwkv_a2[l], 'rwkv_g2': rwkv_g2[l], 'rwkv_kk': rwkv_kk[l], 'rwkv_ka': rwkv_ka[l],
            'rwkv_rk': rwkv_rk[l], 'rwkv_lnx_g': rwkv_lnx_g[l], 'rwkv_lnx_b': rwkv_lnx_b[l],
            'convc_w': convc_w[l], 'convd_w': convd_w[l], 'convd_b': convd_b[l],
            'lru_gx_w': lru_gx_w[l], 'lru_gx_b': lru_gx_b[l], 'lru_ga_w': lru_ga_w[l], 'lru_ga_b': lru_ga_b[l],
            'lru_lam': lru_lam[l], 'ln1_g': ln1_g[l], 'ln1_b': ln1_b[l], 'ln2_g': ln2_g[l], 'ln2_b': ln2_b[l],
            'moe_w_gate': moe_w_gate[l], 'moe_w_up': moe_w_up[l], 'moe_w_down': moe_w_down[l],
        }
        xp, st_p = layer_step(xp, pos_p, lp, dsa_prompt,
                              jnp.zeros((bp, B_HEADS, B_HEAD, B_HEAD), dt), jnp.zeros((bp, 1, B_PROJ), dt),
                              jnp.zeros((bp, C_CONV - 1, W_C), dt), jnp.zeros((bp, D_CONV - 1, W_D), dt),
                              jnp.zeros((bp, W_D), dt), w_router, router_bias)
        past = (gather_pages(cache_k, l, page_table), gather_pages(cache_v, l, page_table),
                gather_pages(cache_ik, l, page_table))
        attn_s = functools.partial(dsa_sample, past=past)
        xs, st_s = layer_step(xs, pos_s, lp, attn_s, state_rwkv[l], state_rwkv_shift[l], state_conv_c[l],
                              state_conv_d[l], state_lru[l], w_router, router_bias)
        for i in range(8):
            new_p[i].append(st_p[i])
            new_s[i].append(st_s[i])
    return (xp, xs,
            jnp.stack(new_p[0]), jnp.stack(new_p[1]), jnp.stack(new_p[2]), jnp.stack(new_p[3]),
            jnp.stack(new_p[4]), jnp.stack(new_p[5]), jnp.stack(new_p[6]), jnp.stack(new_p[7]),
            jnp.stack(new_s[0]), jnp.stack(new_s[1]), jnp.stack(new_s[2]), jnp.stack(new_s[3]),
            jnp.stack(new_s[4]), jnp.stack(new_s[5]), jnp.stack(new_s[6]), jnp.stack(new_s[7]))


_drawn_inputs = setup_inputs


def setup_inputs(seed=0):
    import zlib

    import numpy as np

    out = dict(_drawn_inputs(seed))
    spreads = {}
    factors = {'idx_ln_g': 96.747,
     'idx_ln_b': 124.945,
     'rwkv_lnx_g': 12.167,
     'rwkv_lnx_b': 10.024,
     'lru_gx_b': 8.0,
     'lru_ga_b': 23.612}
    for name, (base, spread) in spreads.items():
        noise = np.random.default_rng([zlib.crc32(name.encode()), seed]).standard_normal(out[name].shape)
        drawn = base * np.exp(spread * noise) if base else spread * noise
        out[name] = __import__('jax').numpy.asarray(drawn.astype(out[name].dtype))
    for name, factor in factors.items():
        out[name] = (out[name] * factor).astype(out[name].dtype)
    return out
```

```python
from contextlib import ExitStack

import numpy as np

import concourse.bass as bass
from concourse import mybir

F32 = mybir.dt.float32
I32 = mybir.dt.int32
ALU = mybir.AluOpType
ACT = mybir.ActivationFunctionType
AX = mybir.AxisListType

DM = 1024
SEQ = 512
DEPTH = 2
DB, DS = 8, 4
PAST, PAGE = 512, 128
NPAGE = PAST // PAGE
NPHYS = 5 * DB * NPAGE // 4
NS = DB * DS
T = SEQ + NS
TP = SEQ + 64
P = 128
KC = DM // P
NT = SEQ // P
WA = 256
ACOLS = 932
C_QI, C_KI, C_WI = 768, 896, 928
NCH = 17
TOPK_P, TOPK_S = 128, 129
CH = 64
NEXP, DEXP = 16, 256
BLOCKS = NEXP + 2 * T // P
ALPHA = (2 * DEPTH) ** 0.25
DECAY = float(np.exp(-0.5))
NEG = -1e30
GELU_C = float(np.sqrt(2.0 / np.pi))


def offsets(spec):
    at, out = 0, {}
    for name, width in spec:
        out[name] = (at, width)
        at += width
    return out, at


CONST, CONST_W = offsets([
    ("ident", 128), ("causal", 128), ("ones_head", 128),
    ("strict_near", 128), ("strict_near_t", 128), ("strict_far", 128), ("strict", 128), ("incl", 64),
    ("s_strict", 128), ("s_strict_t", 128), ("s_incl", 64), ("s_rows", 8), ("spread", 256),
    ("new_bias", 32), ("cos_q", 40), ("sin_q", 40), ("cos_i", 20), ("sin_i", 20), ("reset", TP),
    ("ones", 1), ("group_order", 4), ("expert_order", 16), ("eps", 2),
])

PARAM, PARAM_W = offsets([
    ("mu", 7), ("w0", 2), ("a0", 2), ("kkw", 2), ("ka", 2), ("rk", 2), ("lnxg", 2), ("lnxb", 2),
    ("cw", 6), ("dw", 8), ("db", 2), ("gxb", 2), ("gab", 2), ("lam", 2),
    ("shift", 56), ("convc", 32), ("convd", 48), ("lru", 16),
    ("lora", 256), ("gxw", 256), ("gaw", 256), ("idxg", 32), ("idxb", 32),
])

SMALL, SMALL_W = offsets([("shift", 63), ("convc", 36), ("convd", 54), ("lru", 18)])


def constants():
    c = np.zeros((P, CONST_W), np.float32)

    def put(name, a):
        at, w = CONST[name]
        a = np.asarray(a, np.float32)
        c[:a.shape[0], at:at + w] = a.reshape(a.shape[0], w)

    i = np.arange(P)
    put("ident", np.eye(P))
    put("causal", np.where(i[None] <= i[:, None], 0.0, NEG))
    put("ones_head", (i[:, None] // 64 == i[None] // 64))
    s, t, same = i[:, None] % 64, i[None] % 64, i[:, None] // 64 == i[None] // 64
    near = (s < t) & same & (s // 16 == t // 16)
    far = (s < t) & same & (s // 16 != t // 16)
    put("strict_near", near)
    put("strict_near_t", near.T)
    put("strict_far", far)
    put("strict", (s < t) & same)
    tc = np.arange(64)[None]
    put("incl", i[:, None] % 64 <= tc)
    ss = (s < t) & same & (s // DS == t // DS) & (s < NS) & (t < NS)
    put("s_strict", ss)
    put("s_strict_t", ss.T)
    put("s_incl", (i[:, None] % 64 <= tc) & (i[:, None] % 64 // DS == tc // DS) & (i[:, None] % 64 < NS) & (tc < NS))
    put("s_rows", (i[:, None] % 64) // DS == np.arange(8)[None])
    spread = np.zeros((NS, 2, P), np.float32)
    for g in range(2):
        for j in range(4):
            for h in range(4):
                for q in range(DS):
                    spread[(4 * g + j) * DS + q, g, 32 * j + h * DS + q] = 1.0
    put("spread", spread)
    a = np.arange(NS)
    put("new_bias", np.where((a[None] // DS == a[:, None] // DS) & (a[None] % DS <= a[:, None] % DS), 0.0, NEG))
    pos = np.zeros((5 * P,), np.float32)
    pos[:SEQ] = np.arange(SEQ)
    pos[SEQ:T] = PAST + a % DS
    for name, half in (("q", 8), ("i", 4)):
        freq = (np.float32(500000.0) ** (-np.arange(half, dtype=np.float32) / np.float32(half))).astype(np.float32)
        ang = pos[:, None] * freq[None]
        put("cos_" + name, np.cos(ang).reshape(5, P, half).transpose(1, 0, 2))
        put("sin_" + name, np.sin(ang).reshape(5, P, half).transpose(1, 0, 2))
    reset = np.ones(TP, np.float32)
    reset[0:SEQ:CH] = 0
    reset[SEQ:T:DS] = 0
    reset[T:] = 0
    put("reset", np.broadcast_to(reset, (P, TP)))
    put("ones", np.ones((P, 1)))
    put("group_order", np.broadcast_to(4.0 - np.arange(4), (P, 4)))
    put("expert_order", np.broadcast_to(16.0 - np.arange(16), (P, 16)))
    put("eps", np.broadcast_to(np.array([1e-5, 64e-5], np.float32), (P, 2)))
    return c


RW_PE, RW_DVE, RW_ACT = 21, 16, 5
PER_LAYER = dict(
    params_in=16, wa_in=16, wf0_in=96, wf1_in=96, wf2_in=80, ln_in=32, ik_in=16 * DB * NPAGE, k_in=16 * DB * NPAGE, v_in=16 * DB * NPAGE,
    state_in=64, wout_in=16, moe0_in=16 * BLOCKS, moe1_in=16 * BLOCKS,
    rows_mm=10, rows_copied=10, fm_mm=NCH, fm_copied=NCH, fm_used=NCH, rows_ready=1, rows_stored=96, lora_act=1, ki_var=1, ki_std=1,
    lam_abs=1, lam_exp=1, lam_sum=1, lam_log=1, job_mm=14, job_out=14, conv_done=2, kk_in=1, cum_ready=1, bonus_in=1,
    dz_ready=1, d_tanh=1, gelu_in=1, gelu_tanh=1, om_ready=1, om_sqrt=1, exps_ready=1, cols_ready=1, states_zeroed=1,
    rwc_v=24, rw_in=4, rw_mm=4 * RW_PE, rw_v=4 * RW_DVE, rw_a=4 * RW_ACT,
    rws_in=1, rws_mm=9, rws_v=9, rws_a=2, yn_in=1, yn_mm=2, yn_std=1, rw_done=1, state_out=128,
    kr_ready=1, tr_mm=1, tr_copied=1, idx_mm=3, relu_done=12, rl_used=12, lg_mm=16, lg_ready=16, p_exp=16, p_ready=16,
    pt_mm=16, pt_copied=16, pv_mm=16, ya_copied=4,
    s_prep=1, s_wb_mm=1, s_wb=1, s_idx_mm=1, s_relu=1, s_sums=1, s_tr_mm=1, s_score=1, s_bias=1,
    s_lg_mm=2, s_lg=2, s_max=2, s_exp=2, s_p=2, s_pt_mm=2, s_pt=2, s_pv_mm=2, attn_done=1, small_ready=1, small_out=16,
    mix_mm=5, ln_var=10, ln_std=10, ln_mid=10, ln_done=10, xt_mm=10, xt_copied=10,
    router_mm=1, router_sig=1, chosen=1, slots_mm=1, idx_ready=1, x_scattered=160,
    xg0_in=8 * BLOCKS, xg1_in=8 * BLOCKS, xgt_mm=BLOCKS, xgt_copied=BLOCKS, gu_mm=BLOCKS, silu_done=BLOCKS, h_ready=BLOCKS,
    ht_mm=BLOCKS, ht_copied=BLOCKS, down_mm=BLOCKS, y_copied_a=BLOCKS, y_copied_v=BLOCKS,
    y0_stored=8 * BLOCKS, y1_stored=8 * BLOCKS, yg0_in=32, yg1_in=32, yg2_in=32, yg3_in=32, yg4_in=32,
)
ONCE = ("const_in", "x_in", "zeroed", "y_out", "zeros_out")


START = dict(mix_mm=1, rw_mm=1, xt_copied=1, h_ready=1, ln_done=5, xgt_copied=1, ht_copied=1,
             y_copied_a=1, y_copied_v=1, y0_stored=1, y1_stored=1)


def nth(l, name, n):
    return l * PER_LAYER[name] + (n + START.get(name, 0))


ARENA = 52100


class Map:
    pass


def memory(arena):
    m = Map()
    end = 0

    def region(n):
        nonlocal end
        end += n
        return end - n

    def view(at, *shape):
        n = int(np.prod(shape))
        assert at + n <= ARENA, (at, shape)
        v = arena[:, at:at + n]
        if len(shape) == 1:
            return v
        names = "abcd"[:len(shape)]
        return v.rearrange(f"p ({' '.join(names)}) -> p {' '.join(names)}", **dict(zip(names[1:], shape[1:])))

    C0, WR0, X0, A0 = region(CONST_W), region(KC * NEXP + NEXP), region(5 * DM), region(5 * ACOLS)
    PV0, YT0, LN0, OS0, XT0 = region(PARAM_W), region(8 * T), region(2 * DM), region(SMALL_W), region(8 * T)
    SM0, R1, R2, R4 = region(680), region(8 * DM), region(12288), region(13 * 512)
    assert end <= ARENA, end

    m.consts = view(C0, CONST_W)
    m.const = lambda name: view(C0 + CONST[name][0], CONST[name][1])
    m.param = lambda name: view(PV0 + PARAM[name][0], PARAM[name][1])
    m.small = lambda name: view(OS0 + SMALL[name][0], SMALL[name][1])
    m.params, m.smalls = view(PV0, PARAM_W), view(OS0, SMALL_W)
    m.w_router, m.router_bias = view(WR0, KC, NEXP), view(WR0 + KC * NEXP, NEXP)
    m.x = view(X0, 5, DM)
    m.A = view(A0, 5, ACOLS)
    m.yT = view(YT0, 8, T)
    m.xT = view(XT0, 8, T)
    m.ln = view(LN0, 2, DM)

    st = view(SM0, 680)
    m.nmax, m.ssum, m.rsum = st[:, 0:4], st[:, 4:8], st[:, 8:12]
    m.top8, m.cnt = st[:, 12:20], st[:, 20:22]
    m.lam = [st[:, 24 + 2 * k:26 + 2 * k] for k in range(8)]
    m.bn, m.mv, m.std = [view(SM0 + 44, 2, 6), view(SM0 + 666, 2, 6)], [st[:, 56:58], st[:, 58:60]], [st[:, 664:665], st[:, 665:666]]
    m.pc = view(SM0 + 60, 2, 2)
    m.kist = [view(SM0 + 64 + 5 * k, 5) for k in range(4)]
    m.gsig, m.gsel, m.gates = (view(SM0 + 84 + 80 * k, 5, NEXP) for k in range(3))
    m.g16 = [view(SM0 + 324 + 80 * k, 5, NEXP) for k in range(3)]
    m.g4 = [view(SM0 + 564 + 20 * k, 5, 4) for k in range(4)]
    m.g1 = [view(SM0 + 644 + 5 * k, 5) for k in range(3)]
    m.omka, m.turn = st[:, 660:662], st[:, 678:679]
    m.rks = st[:, 662:664]

    m.wa, m.wout = view(R1, KC, ACOLS), view(R1, KC, DM)
    m.Z = view(R1, 7, TP)
    m.gate, m.bonus, m.yb = (view(R1 + 7 * TP + 2 * TP * k, 2, TP) for k in range(3))
    assert 13 * TP <= 8 * DM
    m.gb = view(R1 + 11 * TP, 2, T)

    FMW = 3 + SEQ + DB * 7
    m.wf = [view(R4 + 1024 * k, KC, P) for k in range(3)]
    fm = [view(R4 + 3072 + FMW * k, FMW) for k in range(4)]
    m.fm_p = [f[:, 0:3 + SEQ] for f in fm]
    m.fm_s = [f[:, 3 + SEQ:FMW].rearrange("p (b t) -> p b t", t=7) for f in fm]
    m.diff = view(R4 + 3072 + 4 * FMW, T)
    m.conv = view(R4 + 3072 + 4 * FMW + T, T)
    m.za_tanh, m.a_lru = view(R4 + 3072, 2, T), view(R4 + 3072 + 2 * T, 2, T)
    m.hs, m.gelu = view(XT0, 2, T), view(XT0 + 2 * T, 2, T)

    m.ea, m.en, m.ec, m.aa, m.nkk, m.kf, m.bv = (view(R2 + 2 * TP * k, 2, TP) for k in range(7))
    D0 = R2 + 14 * TP
    m.xc, m.gx, m.za = (view(D0 + 2 * T * k, 2, T) for k in range(3))
    m.rope_q = [view(R2 + 320 * k, 5, 8, 8) for k in range(4)]
    m.rope_i = [view(R2 + 1280 + 80 * k, 5, 4, 4) for k in range(4)]
    m.ki_c, m.ki_2 = view(R2 + 1600, 5, 32), view(R2 + 1760, 5, 32)

    d = [view(D0 + 512 * k, 4, P) for k in range(8)]
    r = [view(R4 + 512 * k, 4, P) for k in range(13)]
    m.AE, m.BE, m.KE, m.VE, m.BEt, m.KEt, m.VEt, m.Mak = d
    m.D, m.DT, m.E, m.D2, m.D2T, m.D4, m.D4T, m.X, m.XT_, m.FT, m.Zs = r[:11]
    m.attn = view(R4 + 512 * 11, 2, 4, CH)
    m.W, m.U = view(R4 + 512 * 12, 2, P), view(R4 + 512 * 12 + 256, 2, P)
    m.TB = view(XT0, 2, DB, P)
    m.RC, m.Tst = view(XT0 + 4096 - 512, 4, CH), view(XT0 + 4096 - 256, 2, P)
    m.AEb = view(R4 + 512 * 3, 2, DB, P)
    m.UEb = view(R4 + 512 * 8, DB, P)
    m.VEb = view(R4 + 512 * 0, DB, P)
    m.yc, m.y2 = m.ea, m.en

    m.qT, m.kT, m.kiT, m.qiT = view(XT0, 2, T), view(XT0 + 2 * T, 2, T), view(XT0 + 4 * T, T), view(XT0 + 5 * T, T)
    B0 = XT0 + 6 * T
    m.QB, m.WB, m.QI = view(B0, 2, DB, 32), view(B0 + 512, DB, 4, DS), view(B0 + 640, DB, 4, DS)
    sl = [view(R4 + T * k, T) for k in range(6)]
    m.score, m.work, m.eq, m.gt, m.pre, m.bias = sl
    m.relu = [view(R4 + 6 * T + 512 * k, 512) for k in range(2)]
    m.lg = [view(R4 + 6 * T + 1024 + T * k, T) for k in range(2)]
    m.KR = view(R4 + 6 * T + 1024, 5, P)
    m.pT = [view(R4 + 8 * T + 1024 + 512 * k, 4, P) for k in range(2)]
    m.pTn = m.relu[1][:, 0:P]
    m.relu_n = m.relu[1][:, 0:P].rearrange("p (h k) -> p h k", h=4)
    m.wb_in = m.pT[0]
    m.sums = view(R4 + 8 * T + 1024 + 512, 4, 32)
    m.K, m.V, m.ik = view(R2, 2, 4, PAST), view(R2 + 4096, 4, NPAGE, WA), view(R2 + 8192, DB, PAST)

    m.w_gu = [view(R2 + 6144 * k, KC, 2 * DEXP) for k in range(2)]
    m.w_dn = [view(R2 + 6144 * k + 4096, 2, DM) for k in range(2)]
    m.xg, m.y = ([view(R4 + at + DM * k, DM) for k in range(2)] for at in (0, 3840))
    m.xgT, m.silu, m.h, m.hT = view(R4 + 2048, KC, P), view(R4 + 3072, DEXP), view(R4 + 3328, DEXP), view(R4 + 3584, 2, P)
    m.yg = view(R2, 5, 2, DM)
    m.before, m.all1 = view(YT0, P), view(YT0 + P, P)
    m.chosen, m.slot, m.hot_hi, m.hot_lo = (view(YT0 + 256 + 80 * k, 5, NEXP) for k in range(4))
    m.extra, m.extra_sum, m.shift_to, m.own = (view(YT0 + 576 + NEXP * k, NEXP) for k in range(4))
    m.beyond, m.count = view(YT0 + 640, 8, NEXP), view(YT0 + 768, 8)
    m.hi, m.lo, m.gate_hi, m.gate_lo = (view(YT0 + 776 + 5 * k, 5) for k in range(4))
    return m


def program(nc, din, dout):
    with ExitStack() as ctx:
        arena = ctx.enter_context(nc.sbuf_tensor("arena", [P, ARENA], F32))
        pages = ctx.enter_context(nc.sbuf_tensor("pages", [1, DB * NPAGE], I32))
        ints = ctx.enter_context(nc.sbuf_tensor("ints", [P, 18], I32))
        ps = ctx.enter_context(nc.psum_tensor("ps", [P, 8, 512], F32))
        s = {name: ctx.enter_context(nc.semaphore(name)) for name in (*PER_LAYER, *ONCE)}
        m = memory(arena)
        m.pages, m.slots, m.extra_expert = pages, ints[:, 0:10].rearrange("p (k i) -> p k i", k=2), ints[0:1, 10:18]
        m.rows_in = nc.dram_tensor("rows_in", (BLOCKS * P, DM), F32, kind="Internal").ap()
        m.rows_out = nc.dram_tensor("rows_out", (BLOCKS * P, DM), F32, kind="Internal").ap()
        block = ctx.enter_context(nc.Block())

        @block.sync
        def _(sp):
            sync_program(sp, s, m, din, dout)

        @block.gpsimd
        def _(pool):
            pool_program(pool, s, m, dout)

        @block.tensor
        def _(pe):
            tensor_program(pe, s, m, ps)

        @block.scalar
        def _(act):
            scalar_program(act, s, m, ps)

        @block.vector
        def _(dve):
            vector_program(dve, s, m, ps)


def layer_of(ap, l):
    names = "abcdef"[:len(ap.shape) - 1]
    return ap[bass.ds(l, 1)].rearrange(f"z {' '.join(names)} -> (z {names[0]}) {' '.join(names[1:])}")


def sync_program(sp, s, m, din, dout):
    pages = m.pages
    sp.dma_start(m.consts, din["consts"]).then_inc(s["const_in"], 16)
    sp.dma_start(pages[:, :], din["page_table"]).then_inc(s["const_in"], 16)
    sp.dma_start(m.xT, din["xT"]).then_inc(s["x_in"], 16)
    sp.dma_start(m.w_router, din["w_router"]).then_inc(s["const_in"], 16)
    sp.dma_start(m.router_bias, din["router_bias"].partition_broadcast(P)).then_inc(s["const_in"], 16)
    sp.dma_start(m.x[:, 0:NT, :], din["x_prompt"].rearrange("(i p) d -> p i d", p=P)).then_inc(s["x_in"], 16)
    sp.dma_start(m.x[0:NS, NT, :], din["x_sample"]).then_inc(s["x_in"], 16)
    sp.wait_ge(s["const_in"], 64)

    with sp.Fori(0, DEPTH) as l:
        sp.wait_ge(s["mix_mm"], nth(l, "mix_mm", 0))
        sp.dma_start(m.wa, layer_of(din["wa"], l)).then_inc(s["wa_in"], 16)
        sp.dma_start(m.params, layer_of(din["params"], l)).then_inc(s["params_in"], 16)
        sp.wait_ge(s["ln_done"], nth(l, "ln_done", -4))
        for n in range(NCH):
            if n >= 3:
                sp.wait_ge(s["fm_mm"], nth(l, "fm_mm", n - 2))
            sp.dma_start(m.wf[n % 3], layer_of(din["wf"], l * NCH + n)).then_inc((s["wf0_in"], s["wf1_in"], s["wf2_in"])[n % 3], 16)
        sp.wait_ge(s["states_zeroed"], nth(l, "states_zeroed", 1))
        for q in range(2):
            for h in range(2):
                rows = slice(64 * h, 64 * h + 64)
                sp.dma_start(m.TB[rows, q, :, rows], layer_of(din["state_rwkv"], l)[64 * (2 * q + h):64 * (2 * q + h) + 64])\
                    .then_inc(s["state_in"], 16)
        sp.wait_ge(s["zeros_out"], 16 * BLOCKS // 2)
        sp.wait_ge(s["ln_done"], nth(l, "ln_done", 0))
        sp.dma_start(m.ln, layer_of(din["ln"], l * 2).partition_broadcast(P)).then_inc(s["ln_in"], 16)
        sp.wait_ge(s["rw_done"], nth(l, "rw_done", 1))
        for q in range(2):
            for h in range(2):
                rows = slice(64 * h, 64 * h + 64)
                n = 64 * (2 * q + h)
                sp.dma_start(layer_of(dout["state_p"], l)[n:n + 64], m.Tst[rows, q, rows]).then_inc(s["state_out"], 16)
                sp.dma_start(layer_of(dout["state_s"], l)[n:n + 64], m.TB[rows, q, :, rows]).then_inc(s["state_out"], 16)
        with sp.Fori(0, DB) as b:
            for c in range(NPAGE):
                page = sp.value_load(pages[0:1, bass.ds(b * NPAGE + c, 1)], min_val=0, max_val=NPHYS - 1)
                sp.dma_start(m.ik[0:32, bass.ds(b, 1), PAGE * c:PAGE * c + PAGE],
                             din["cache_ik"][bass.ds(l * NPHYS + page, 1)].rearrange("z d k -> d z k"))\
                    .then_inc(s["ik_in"], 16)
        sp.dma_start(m.wout, layer_of(din["wout"], l)).then_inc(s["wout_in"], 16)
        for g in range(2):
            with sp.Fori(0, 4) as j:
                for c in range(NPAGE):
                    page = sp.value_load(pages[0:1, bass.ds(j * NPAGE + (16 * g + c), 1)], min_val=0, max_val=NPHYS - 1)
                    if g and c == 0:
                        sp.wait_ge(s["s_lg_mm"], nth(l, "s_lg_mm", 1))
                    sp.dma_start(m.K[:, :, bass.ds(j, 1), PAGE * c:PAGE * c + PAGE],
                                 din["cache_k"][bass.ds(l * NPHYS + page, 1)].rearrange("z p q k -> p q z k"))\
                        .then_inc(s["k_in"], 16)
            with sp.Fori(0, 4) as j:
                for c in range(NPAGE):
                    page = sp.value_load(pages[0:1, bass.ds(j * NPAGE + (16 * g + c), 1)], min_val=0, max_val=NPHYS - 1)
                    if g and c == 0:
                        sp.wait_ge(s["s_pv_mm"], nth(l, "s_pv_mm", 1))
                    sp.dma_start(m.V[:, bass.ds(j, 1), c, :],
                                 din["cache_v"][bass.ds(l * NPHYS + page, 1)].rearrange("z k f -> k z f"))\
                        .then_inc(s["v_in"], 16)
        def block_weights(k, expert, moe_in):
            sp.dma_start(m.w_gu[k], layer_of(din["w_gu"], l * NEXP + expert)).then_inc(moe_in, 16)
            sp.dma_start(m.w_dn[k], layer_of(din["w_dn"], l * NEXP + expert)).then_inc(moe_in, 16)

        def block_rows(k, block, xg_in):
            sp.dma_start(m.xg[k], m.rows_in.rearrange("(n p) d -> p n d", p=P)[:, bass.ds(block, 1), :]
                         .rearrange("p n d -> p (n d)")).then_inc(xg_in, 16)

        sp.wait_ge(s["attn_done"], nth(l, "attn_done", 1))
        for k, moe_in in enumerate((s["moe0_in"], s["moe1_in"])):
            block_weights(k, k, moe_in)
        sp.wait_ge(s["x_scattered"], nth(l, "x_scattered", 160))
        for k, xg_in in enumerate((s["xg0_in"], s["xg1_in"])):
            block_rows(k, k, xg_in)
        with sp.Fori(1, NEXP // 2) as e:
            for k, (moe_in, xg_in) in enumerate(((s["moe0_in"], s["xg0_in"]), (s["moe1_in"], s["xg1_in"]))):
                sp.wait_ge(s["down_mm"], nth(l, "down_mm", e * 2 + (k - 1)))
                block_rows(k, e * 2 + k, xg_in)
                block_weights(k, e * 2 + k, moe_in)
        with sp.Fori(0, (BLOCKS - NEXP) // 2) as e:
            for k, (moe_in, xg_in) in enumerate(((s["moe0_in"], s["xg0_in"]), (s["moe1_in"], s["xg1_in"]))):
                expert = sp.value_load(m.extra_expert[0:1, bass.ds(e * 2 + k, 1)], min_val=0, max_val=NEXP - 1)
                sp.wait_ge(s["down_mm"], nth(l, "down_mm", e * 2 + (NEXP + k - 1)))
                block_rows(k, e * 2 + (NEXP + k), xg_in)
                block_weights(k, expert, moe_in)
        sp.wait_ge(s["ln_done"], nth(l, "ln_done", 5))
        sp.dma_start(m.ln, layer_of(din["ln"], l * 2 + 1).partition_broadcast(P)).then_inc(s["ln_in"], 16)


def pool_program(pool, s, m, dout):
    def gain_and_bias(l, first):
        pool.wait_ge(s["ln_in"], nth(l, "ln_in", 16 + 16 * (first > 0)))
        for i in range(5):
            n = P if i < NT else NS
            pool.wait_ge(s["ln_mid"], nth(l, "ln_mid", first + i + 1))
            pool.tensor_tensor(m.x[0:n, i, :], m.x[0:n, i, :], m.ln[0:n, 0, :], ALU.mult)
            pool.drain()
            pool.tensor_tensor(m.x[0:n, i, :], m.x[0:n, i, :], m.ln[0:n, 1, :], ALU.add).then_inc(s["ln_done"], 1)

    for _ in range(5):
        pool.drain().then_inc(s["ln_done"], 1)
    pool.memset(m.ln, 0.0)
    pool.drain()
    pool.wait_ge(s["rows_mm"], 10)
    for n in range(BLOCKS // 2):
        pool.dma_start(m.rows_in.rearrange("(n p) d -> p n d", p=P)[:, 2 * n:2 * n + 2, :], m.ln).then_inc(s["zeros_out"], 16)
    with pool.Fori(0, DEPTH) as l:
        pool.wait_ge(s["rows_ready"], nth(l, "rows_ready", 1))
        for name, a, w in (("k", WA, WA), ("v", 2 * WA, WA), ("ik", C_KI, 32)):
            pool.dma_start(layer_of(dout[name + "_p"], l).rearrange("(i p) f -> p i f", p=P), m.A[:, 0:NT, a:a + w])\
                .then_inc(s["rows_stored"], 16)
            pool.dma_start(layer_of(dout[name + "_s"], l), m.A[0:NS, NT, a:a + w]).then_inc(s["rows_stored"], 16)
        pool.wait_ge(s["small_ready"], nth(l, "small_ready", 1))
        pool.dma_start(layer_of(dout["small"], l), m.smalls).then_inc(s["small_out"], 16)
        gain_and_bias(l, 0)
        pool.wait_ge(s["zeros_out"], 16 * BLOCKS // 2)
        pool.wait_ge(s["idx_ready"], nth(l, "idx_ready", 1))
        pool.tensor_tensor(m.turn, m.const("ones"), m.const("ones"), ALU.add)
        pool.drain()
        for i in range(5):
            n = P if i < NT else NS
            for k in range(2):
                pool.indirect_dma_start(m.rows_in, bass.IndirectOffsetOnAxis(ap=m.slots[0:n, k, i:i + 1], axis=0),
                                        m.x[0:n, i, :], None).then_inc(s["x_scattered"], 16)
        pool.wait_ge(s["y0_stored"], nth(l, "y0_stored", 8 * BLOCKS))
        pool.wait_ge(s["y1_stored"], nth(l, "y1_stored", 8 * BLOCKS))
        pool.tensor_tensor(m.turn, m.const("ones"), m.const("ones"), ALU.add)
        pool.drain()
        for i, yg_in in enumerate((s["yg0_in"], s["yg1_in"], s["yg2_in"], s["yg3_in"], s["yg4_in"])):
            n = P if i < NT else NS
            for k in range(2):
                pool.indirect_dma_start(m.yg[0:n, i, k, :], None, m.rows_out,
                                        bass.IndirectOffsetOnAxis(ap=m.slots[0:n, k, i:i + 1], axis=0)).then_inc(yg_in, 16)
        gain_and_bias(l, 5)
    pool.wait_ge(s["ln_done"], nth(DEPTH, "ln_done", 0))
    pool.dma_start(dout["y_p"].rearrange("(i p) d -> p i d", p=P), m.x[:, 0:NT, :]).then_inc(s["y_out"], 16)
    pool.dma_start(dout["y_s"], m.x[0:NS, NT, :]).then_inc(s["y_out"], 16)
    pool.wait_ge(s["y_out"], 32)
    pool.wait_ge(s["rows_stored"], nth(DEPTH, "rows_stored", 0))
    pool.wait_ge(s["small_out"], nth(DEPTH, "small_out", 0))
    pool.wait_ge(s["state_out"], nth(DEPTH, "state_out", 0))


def tensor_program(pe, s, m, ps):
    ident = m.const("ident")
    chunks = [(0, SEQ), (SEQ, TP - SEQ)]

    def row_tile(i):
        return slice(i * P, i * P + (P if i < NT else NS))

    def row_projection(l):
        pe.wait_ge(s["wa_in"], nth(l, "wa_in", 16))
        for i in range(5):
            n = P if i < NT else NS
            for h, (a, w) in enumerate(((0, 512), (512, ACOLS - 512))):
                k = 2 * i + h
                if k >= 2:
                    pe.wait_ge(s["rows_copied"], nth(l, "rows_copied", k - 1))
                for c in range(KC):
                    mm = pe.matmul(ps[0:n, k % 2, 0:w], m.xT[:, c, row_tile(i)], m.wa[:, c, a:a + w],
                                   start=c == 0, stop=c == KC - 1)
                mm.then_inc(s["rows_mm"], 1)

    def column_projection(l):
        for n in range(NCH):
            pe.wait_ge((s["wf0_in"], s["wf1_in"], s["wf2_in"])[n % 3], nth(l, f"wf{n % 3}_in", 16 * (n // 3 + 1)))
            if n >= 2:
                pe.wait_ge(s["fm_copied"], nth(l, "fm_copied", n - 1))
            for c in range(KC):
                pe.matmul(ps[:, 2 + n % 2, :], m.wf[n % 3][:, c, :], m.xT[:, c, 0:SEQ], start=c == 0, stop=c == KC - 1)
                mm = pe.matmul(ps[:, 4 + n % 2, 0:NS], m.wf[n % 3][:, c, :], m.xT[:, c, SEQ:T],
                               start=c == 0, stop=c == KC - 1)
            mm.then_inc(s["fm_mm"], 1)

    def column_jobs(l):
        job = 0

        def product(lhsT, rhs, width):
            nonlocal job
            if job >= 2:
                pe.wait_ge(s["job_out"], nth(l, "job_out", job - 1))
            b = 4 + 2 * (job % 2)
            if job < 2:
                pe.wait_ge(s["fm_copied"], nth(l, "fm_copied", NCH))
            pe.matmul(ps[:, b, :], lhsT, rhs[:, 0:SEQ], start=True, stop=True)
            pe.matmul(ps[:, b + 1, 0:width - SEQ], lhsT, rhs[:, SEQ:width], start=True, stop=True).then_inc(s["job_mm"], 1)
            job += 1

        lora = m.param("lora")
        pe.wait_ge(s["lora_act"], nth(l, "lora_act", 1))
        for rows in (slice(0, 32), slice(32, 64)):
            for p in range(2):
                product(lora[rows, 128 * p:128 * p + 128], m.Z[rows, 6, :], TP)
        for w in ("gxw", "gaw"):
            for p in range(2):
                pe.wait_ge(s["conv_done"], nth(l, "conv_done", p + 1))
                product(m.param(w)[:, 128 * p:128 * p + 128], m.xc[:, p, :], T)
        for p in range(2):
            product(lora[64:128, 128 * p:128 * p + 128], m.Z[64:128, 6, :], TP)
        pe.wait_ge(s["bonus_in"], nth(l, "bonus_in", 1))
        for p in range(2):
            product(m.const("ones_head"), m.bonus[:, p, :], TP)
        pe.wait_ge(s["kk_in"], nth(l, "kk_in", 1))
        for p in range(2):
            product(m.const("ones_head"), m.bv[:, p, :], TP)

    def rwkv_loop(l):
        with pe.Fori(0, 4) as g:
            pe.wait_ge(s["rw_in"], nth(l, "rw_in", g + 1))
            for k in range(4):
                pe.matmul(ps[:, 0, 128 * k:128 * k + 128], m.BE[:, k, :], m.AE[:, k, :], start=True, stop=True)
                pe.matmul(ps[:, 3, 64 * k:64 * k + 64], m.BE[:, k, :], m.RC[:, k, :], start=True, stop=True)
                pe.matmul(ps[:, 2, 128 * k:128 * k + 128], m.KE[:, k, :], m.AE[:, k, :], start=True, stop=True)
                pe.matmul(ps[:, 3, 256 + 64 * k:320 + 64 * k], m.KE[:, k, :], m.RC[:, k, :], start=True, stop=True)
                mm = pe.matmul(ps[:, 1, 128 * k:128 * k + 128], m.AE[:, k, :], m.BE[:, k, :], start=True, stop=True)
            mm.then_inc(s["rw_mm"], 1)
            for b, tile in ((4, m.BE), (5, m.KE), (6, m.VE)):
                for k in range(4):
                    mm = pe.transpose(ps[:, b, 128 * k:128 * k + 128], tile[:, k, :], ident)
            mm.then_inc(s["rw_mm"], 1)

            def four(bank, lhsT, rhs):
                for k in range(4):
                    mm = pe.matmul(ps[:, bank, 128 * k:128 * k + 128], lhsT[:, k, :], rhs[:, k, :], start=True, stop=True)
                mm.then_inc(s["rw_mm"], 1)

            pe.wait_ge(s["rw_v"], nth(l, "rw_v", g * RW_DVE + 5))
            for bank, lhsT, rhs in ((0, m.DT, m.D), (1, m.D, m.DT)):
                four(bank, lhsT, rhs)
            pe.wait_ge(s["rw_v"], nth(l, "rw_v", g * RW_DVE + 7))
            for bank, lhsT, rhs in ((2, m.D2T, m.D2), (3, m.D2, m.D2T)):
                four(bank, lhsT, rhs)
            pe.wait_ge(s["rw_v"], nth(l, "rw_v", g * RW_DVE + 9))
            four(0, m.D4T, m.D4)
            pe.wait_ge(s["rw_v"], nth(l, "rw_v", g * RW_DVE + 10))
            four(1, m.D4T, m.X)
            pe.wait_ge(s["rw_v"], nth(l, "rw_v", g * RW_DVE + 11))
            four(2, m.D2T, m.X)
            pe.wait_ge(s["rw_v"], nth(l, "rw_v", g * RW_DVE + 12))
            four(3, m.DT, m.X)
            pe.wait_ge(s["rw_v"], nth(l, "rw_v", g * RW_DVE + 13))
            for k in range(4):
                mm = pe.transpose(ps[:, 0, 128 * k:128 * k + 128], m.X[:, k, :], ident)
            mm.then_inc(s["rw_mm"], 1)
            pe.wait_ge(s["rw_a"], nth(l, "rw_a", g * RW_ACT + 2))
            four(1, m.E, m.XT_)
            pe.wait_ge(s["rw_a"], nth(l, "rw_a", g * RW_ACT + 3))
            four(2, m.FT, m.X)
            pe.wait_ge(s["rw_v"], nth(l, "rw_v", g * RW_DVE + 14))
            four(3, m.FT, m.Zs)
            pe.wait_ge(s["rw_v"], nth(l, "rw_v", g * RW_DVE + 15))
            four(0, m.FT, m.Zs)
            pe.wait_ge(s["rw_v"], nth(l, "rw_v", g * RW_DVE + 16))
            for c in range(2):
                for p in range(2):
                    k = 2 * c + p
                    o = ps[:, 4, 128 * p:128 * p + 128]
                    pe.matmul(o, m.Mak[:, k, :], m.VEt[:, k, :], start=True, stop=False)
                    mm = pe.matmul(o, m.AE[:, k, :], m.Tst[:, p, :], start=False, stop=True)
                mm.then_inc(s["rw_mm"], 1)
                pe.wait_ge(s["rwc_v"], nth(l, "rwc_v", g * 6 + 3 * c + 1))
                for p in range(2):
                    mm = pe.matmul(ps[:, 5, 128 * p:128 * p + 128], m.Zs[:, 2 * c + p, :], m.W[:, p, :], start=True, stop=True)
                mm.then_inc(s["rw_mm"], 1)
                pe.wait_ge(s["rwc_v"], nth(l, "rwc_v", g * 6 + 3 * c + 2))
                for p in range(2):
                    k = 2 * c + p
                    o = ps[:, 6, 128 * p:128 * p + 128]
                    pe.matmul(o, m.BEt[:, k, :], m.U[:, p, :], start=True, stop=False)
                    pe.matmul(o, m.KEt[:, k, :], m.VEt[:, k, :], start=False, stop=False)
                    pe.matmul(o, ident, m.Tst[:, p, :], start=False, stop=True)
                if c:
                    pe.wait_ge(s["rw_a"], nth(l, "rw_a", g * RW_ACT + 4))
                for p in range(2):
                    k = 2 * c + p
                    o = ps[:, 7, 64 * p:64 * p + 64]
                    pe.matmul(o, m.VEt[:, k, :], m.attn[:, 1, k, :], start=True, stop=False)
                    pe.matmul(o, m.U[:, p, :], m.attn[:, 0, k, :], start=False, stop=False)
                    mm = pe.matmul(o, m.Tst[:, p, :], m.RC[:, k, :], start=False, stop=True)
                mm.then_inc(s["rw_mm"], 1)
                pe.wait_ge(s["rwc_v"], nth(l, "rwc_v", g * 6 + 3 * c + 3))

    def rwkv_sample(l):
        pe.wait_ge(s["rws_in"], nth(l, "rws_in", 1))
        pe.wait_ge(s["state_in"], nth(l, "state_in", 64))
        for k in range(2):
            pe.matmul(ps[:, 0, 128 * k:128 * k + 128], m.BE[:, k, :], m.AE[:, k, :], start=True, stop=True)
            pe.matmul(ps[:, 3, 64 * k:64 * k + 64], m.BE[:, k, :], m.RC[:, k, :], start=True, stop=True)
            pe.matmul(ps[:, 2, 128 * k:128 * k + 128], m.KE[:, k, :], m.AE[:, k, :], start=True, stop=True)
            pe.matmul(ps[:, 3, 256 + 64 * k:320 + 64 * k], m.KE[:, k, :], m.RC[:, k, :], start=True, stop=True)
            mm = pe.matmul(ps[:, 1, 128 * k:128 * k + 128], m.AE[:, k, :], m.BE[:, k, :], start=True, stop=True)
        mm.then_inc(s["rws_mm"], 1)
        for b, tile in ((4, m.BE), (5, m.KE), (6, m.VE)):
            for k in range(2):
                mm = pe.transpose(ps[:, b, 128 * k:128 * k + 128], tile[:, k, :], ident)
        mm.then_inc(s["rws_mm"], 1)
        pe.wait_ge(s["rws_v"], nth(l, "rws_v", 1))
        for k in range(2):
            mm = pe.matmul(ps[:, 0, 128 * k:128 * k + 128], m.DT[:, k, :], m.D[:, k, :], start=True, stop=True)
        mm.then_inc(s["rws_mm"], 1)
        pe.wait_ge(s["rws_v"], nth(l, "rws_v", 2))
        for k in range(2):
            mm = pe.matmul(ps[:, 1, 128 * k:128 * k + 128], m.DT[:, k, :], m.X[:, k, :], start=True, stop=True)
        mm.then_inc(s["rws_mm"], 1)
        pe.wait_ge(s["rws_a"], nth(l, "rws_a", 1))
        pe.wait_ge(s["rws_v"], nth(l, "rws_v", 3))
        for p in range(2):
            o = ps[:, 4, 128 * p:128 * p + 128]
            pe.matmul(o, m.Mak[:, p, :], m.VEt[:, p, :], start=True, stop=False)
            for b in range(DB):
                mm = pe.matmul(o, m.AEb[:, p, b, :], m.TB[:, p, b, :], start=False, stop=b == DB - 1)
        mm.then_inc(s["rws_mm"], 1)
        pe.wait_ge(s["rws_v"], nth(l, "rws_v", 4))
        for p in range(2):
            mm = pe.matmul(ps[:, 5, 128 * p:128 * p + 128], m.X[:, p, :], m.W[:, p, :], start=True, stop=True)
        mm.then_inc(s["rws_mm"], 1)
        pe.wait_ge(s["rws_v"], nth(l, "rws_v", 5))
        for p in range(2):
            o = ps[:, 7, 64 * p:64 * p + 64]
            pe.matmul(o, m.VEt[:, p, :], m.attn[:, 1, p, :], start=True, stop=False)
            pe.matmul(o, m.U[:, p, :], m.attn[:, 0, p, :], start=False, stop=False)
            for b in range(DB):
                q = slice(DS * b, DS * b + DS)
                mm = pe.matmul(o[:, q], m.TB[:, p, b, :], m.RC[:, p, q], start=False, stop=b == DB - 1)
        mm.then_inc(s["rws_mm"], 1)
        for p in range(2):
            pe.wait_ge(s["rws_v"], nth(l, "rws_v", 6 + 2 * p))
            for h in range(2):
                o = ps[:, 2 * p + h, :]
                q = slice(4 * h, 4 * h + 4)
                pe.matmul(o, m.BEt[:, p, :], m.UEb[:, q, :], start=True, stop=False)
                pe.matmul(o, m.KEt[:, p, :], m.VEb[:, q, :], start=False, stop=False)
                mm = pe.matmul(o, ident, m.TB[:, p, q, :], start=False, stop=True)
            mm.then_inc(s["rws_mm"], 1)

    def y_norm(l):
        for step, src in enumerate((m.yb, m.y2)):
            if step:
                pe.wait_ge(s["yn_in"], nth(l, "yn_in", 1))
            else:
                pe.wait_ge(s["rws_a"], nth(l, "rws_a", 2))
                pe.wait_ge(s["rws_v"], nth(l, "rws_v", 9))
            for p in range(2):
                pe.matmul(ps[:, 2 * p, :], m.const("ones_head"), src[:, p, 0:SEQ], start=True, stop=True)
                mm = pe.matmul(ps[:, 2 * p + 1, 0:64], m.const("ones_head"), src[:, p, SEQ:TP], start=True, stop=True)
            mm.then_inc(s["yn_mm"], 1)

    def head_transposes(l):
        pe.wait_ge(s["kr_ready"], nth(l, "kr_ready", 1))
        srcs = [m.A[:, :, 128 * k:128 * k + 128] for k in range(4)] + [m.A[:, :, C_QI:C_QI + 128], m.KR]
        for b, src in enumerate(srcs):
            for i in range(NT):
                pe.transpose(ps[:, b, 128 * i:128 * i + 128], src[:, i, :], ident)
            mm = pe.transpose(ps[:, 6, NS * b:NS * b + NS], src[0:NS, NT, :], ident[0:NS, 0:NS])
        mm.then_inc(s["tr_mm"], 1)

    def prompt_attention(l):
        pe.wait_ge(s["tr_copied"], nth(l, "tr_copied", 1))

        def indexer(i):
            if i >= 2:
                pe.wait_ge(s["relu_done"], nth(l, "relu_done", 4 * (i - 1)))
            for h in range(4):
                q = slice(32 * h, 32 * h + 32)
                mm = pe.matmul(ps[:, h, 0:P * (i + 1)], m.qiT[q, P * i:P * i + P], m.kiT[q, 0:P * (i + 1)],
                               start=True, stop=True)
            mm.then_inc(s["idx_mm"], 1)

        def logits(k):
            i, h = divmod(k, 4)
            q = slice(64 * (h % 2), 64 * (h % 2) + 64)
            if k >= 2:
                pe.wait_ge(s["lg_ready"], nth(l, "lg_ready", k - 1))
            pe.matmul(ps[:, 4 + k % 2, 0:P * (i + 1)], m.qT[q, h // 2, P * i:P * i + P], m.kT[q, h // 2, 0:P * (i + 1)],
                      start=True, stop=True).then_inc(s["lg_mm"], 1)

        logits(0)
        indexer(1)
        for k in range(16):
            i, h = divmod(k, 4)
            if k < 15:
                logits(k + 1)
            if h == 1 and i in (1, 2):
                indexer(i + 1)
            pe.wait_ge(s["p_ready"], nth(l, "p_ready", k + 1))
            if k >= 1:
                pe.wait_ge(s["pt_copied"], nth(l, "pt_copied", k))
            for c in range(i + 1):
                mm = pe.transpose(ps[:, 6, P * c:P * c + P], m.lg[k % 2][:, P * c:P * c + P], ident)
            mm.then_inc(s["pt_mm"], 1)
            pe.wait_ge(s["pt_copied"], nth(l, "pt_copied", k + 1))
            if h == 0 and i:
                pe.wait_ge(s["ya_copied"], nth(l, "ya_copied", i))
            q = slice(64 * (h % 2), 64 * (h % 2) + 64)
            for c in range(i + 1):
                mm = pe.matmul(ps[q, 7, P * (h // 2):P * (h // 2) + P], m.A[:, c, 512 + 64 * h:576 + 64 * h],
                               m.pT[k % 2][:, c, :], start=c == 0, stop=c == i)
            mm.then_inc(s["pv_mm"], 1)

    def sample_attention(l):
        pe.wait_ge(s["s_prep"], nth(l, "s_prep", 1))
        for h in range(4):
            mm = pe.matmul(ps[:, 0, NS * h:NS * h + NS], m.wb_in[0:NS, h, :], ident[0:NS, 0:NS], start=True, stop=True)
        mm.then_inc(s["s_wb_mm"], 1)
        pe.wait_ge(s["ik_in"], nth(l, "ik_in", 16 * DB * NPAGE))
        pe.wait_ge(s["ya_copied"], nth(l, "ya_copied", 4))
        for b in range(DB):
            for c in range(NPAGE):
                pe.matmul(ps[:, 1, 128 * c + 16 * b:128 * c + 16 * b + 16], m.ik[0:32, b, P * c:P * c + P],
                          m.QI[0:32, b, :, :], start=True, stop=True)
        for h in range(4):
            q = slice(32 * h, 32 * h + 32)
            mm = pe.matmul(ps[0:NS, 2 + h, 0:NS], m.qiT[q, SEQ:T], m.kiT[q, SEQ:T], start=True, stop=True)
        mm.then_inc(s["s_idx_mm"], 1)
        pe.wait_ge(s["s_sums"], nth(l, "s_sums", 1))
        for c in range(NPAGE):
            mm = pe.transpose(ps[0:NS, 0, P * c:P * c + P], m.sums[:, c, :], ident)
        mm.then_inc(s["s_tr_mm"], 1)
        pe.wait_ge(s["s_bias"], nth(l, "s_bias", 1))
        spread = m.const("spread")
        for g in range(2):
            pe.wait_ge(s["k_in"], nth(l, "k_in", 256 * (g + 1)))
            if g:
                pe.wait_ge(s["s_lg"], nth(l, "s_lg", 1))
            for j in range(4):
                for p in range(2):
                    pe.matmul(ps[32 * j:32 * j + 32, 2, :], m.QB[:, p, 4 * g + j, :], m.K[:, p, j, :],
                              start=p == 0, stop=False, skip_group_check=True)
            pe.matmul(ps[:, 2, :], spread[0:NS, P * g:P * g + P], m.bias[0:NS, 0:PAST], start=False, stop=True,
                      skip_group_check=True)
            for p in range(2):
                pe.matmul(ps[:, 3, 0:NS], m.QB[:, p, 4 * g:4 * g + 4, :].rearrange("p b m -> p (b m)"), m.kT[:, p, SEQ:T],
                          start=p == 0, stop=False)
            pe.matmul(ps[:, 3, 0:NS], spread[0:NS, P * g:P * g + P], m.bias[0:NS, PAST:T], start=False, stop=True)                .then_inc(s["s_lg_mm"], 1)
            pe.wait_ge(s["s_p"], nth(l, "s_p", g + 1))
            for c in range(NPAGE):
                pe.transpose(ps[:, 6, P * c:P * c + P], m.lg[0][:, P * c:P * c + P], ident)
            pe.transpose(ps[0:NS, 5, 0:P], m.lg[0][:, PAST:T], ident).then_inc(s["s_pt_mm"], 1)
            pe.wait_ge(s["s_pt"], nth(l, "s_pt", g + 1))
            pe.wait_ge(s["v_in"], nth(l, "v_in", 256 * (g + 1)))
            for j in range(4):
                for p in range(2):
                    o = ps[:, 7, 128 * p + 16 * (4 * g + j):128 * p + 16 * (4 * g + j) + 16]
                    for c in range(NPAGE):
                        pe.matmul(o, m.V[:, j, c, P * p:P * p + P], m.pT[0][:, c, 32 * j:32 * j + 16],
                                  start=c == 0, stop=False)
                    mm = pe.matmul(o, m.A[0:NS, NT, 512 + P * p:512 + P * p + P], m.pTn[0:NS, 32 * j:32 * j + 16],
                                   start=False, stop=True)
            mm.then_inc(s["s_pv_mm"], 1)

    def transposes_of_x(l, first):
        for i in range(5):
            n = P if i < NT else NS
            pe.wait_ge(s["ln_done"], nth(l, "ln_done", first + i + 1))
            if i:
                pe.wait_ge(s["xt_copied"], nth(l, "xt_copied", first + i))
            for c in range(KC):
                o, x = ps[:, 4 + c // 4, n * (c % 4):n * (c % 4) + n], m.x[0:n, i, P * c:P * c + P]
                if i < NT:
                    mm = pe.transpose(o, x, ident)
                else:
                    mm = pe.matmul(o, x, ident[0:n, 0:n], start=True, stop=True)
            mm.then_inc(s["xt_mm"], 1)

    def output_projection(l):
        pe.wait_ge(s["wout_in"], nth(l, "wout_in", 16))
        pe.wait_ge(s["attn_done"], nth(l, "attn_done", 1))
        for i in range(5):
            n = P if i < NT else NS
            if i >= 2:
                pe.wait_ge(s["ln_var"], nth(l, "ln_var", i - 1))
            for h in range(2):
                for c in range(8):
                    mm = pe.matmul(ps[0:n, 2 * (i % 2) + h, :], m.yT[:, c, row_tile(i)], m.wout[:, c, 512 * h:512 * h + 512],
                                   start=c == 0, stop=c == 7)
            mm.then_inc(s["mix_mm"], 1)
        transposes_of_x(l, 0)

    def experts(l):
        pe.wait_ge(s["xt_copied"], nth(l, "xt_copied", 5))
        for i in range(5):
            n = P if i < NT else NS
            for c in range(KC):
                mm = pe.matmul(ps[0:n, 7, NEXP * i:NEXP * i + NEXP], m.xT[:, c, row_tile(i)], m.w_router[:, c, :],
                               start=c == 0, stop=c == KC - 1)
        mm.then_inc(s["router_mm"], 1)
        pe.wait_ge(s["chosen"], nth(l, "chosen", 1))
        for i in range(6):
            o = ps[:, 6, NEXP * i:NEXP * i + NEXP]
            for j in range(min(i, NT)):
                pe.matmul(o, m.all1, m.chosen[:, j, :], start=j == 0, stop=False)
            if i < NT:
                pe.matmul(o, m.before, m.chosen[:, i, :], start=i == 0, stop=True)
            else:
                mm = pe.matmul(o, (m.before if i == NT else m.all1)[0:NS], m.chosen[0:NS, NT, :], start=False, stop=True)
        mm.then_inc(s["slots_mm"], 1)

        def rows_to_columns(e, k):
            pe.wait_ge((s["xg0_in"], s["xg1_in"])[k], nth(l, f"xg{k}_in", e * 16 + 16))
            pe.wait_ge(s["xgt_copied"], nth(l, "xgt_copied", e * 2 + k))
            for c in range(KC):
                mm = pe.transpose(ps[:, c // 4, P * (c % 4):P * (c % 4) + P], m.xg[k][:, P * c:P * c + P], ident)
            mm.then_inc(s["xgt_mm"], 1)

        def gate_and_up(e, k):
            pe.wait_ge((s["moe0_in"], s["moe1_in"])[k], nth(l, f"moe{k}_in", e * 32 + 32))
            pe.wait_ge(s["h_ready"], nth(l, "h_ready", e * 2 + k))
            pe.wait_ge(s["xgt_copied"], nth(l, "xgt_copied", e * 2 + (k + 1)))
            for c in range(KC):
                mm = pe.matmul(ps[:, 3, :], m.xgT[:, c, :], m.w_gu[k][:, c, :], start=c == 0, stop=c == KC - 1)
            mm.then_inc(s["gu_mm"], 1)

        def hidden_to_columns(e, k):
            pe.wait_ge(s["ht_copied"], nth(l, "ht_copied", e * 2 + k))
            pe.wait_ge(s["h_ready"], nth(l, "h_ready", e * 2 + (k + 1)))
            for f in range(2):
                mm = pe.transpose(ps[:, 2, P * f:P * f + P], m.h[:, P * f:P * f + P], ident)
            mm.then_inc(s["ht_mm"], 1)

        def down(e, k):
            pe.wait_ge(s["y_copied_a"], nth(l, "y_copied_a", e * 2 + k))
            pe.wait_ge(s["y_copied_v"], nth(l, "y_copied_v", e * 2 + k))
            pe.wait_ge(s["ht_copied"], nth(l, "ht_copied", e * 2 + (k + 1)))
            for h in range(2):
                for f in range(2):
                    mm = pe.matmul(ps[:, 5 + h, :], m.hT[:, f, :], m.w_dn[k][:, f, 512 * h:512 * h + 512],
                                   start=f == 0, stop=f == 1)
            mm.then_inc(s["down_mm"], 1)

        rows_to_columns(0, 0)
        gate_and_up(0, 0)
        with pe.Fori(0, BLOCKS // 2 - 1) as e:
            for k in range(2):
                rows_to_columns(e + k, 1 - k)
                hidden_to_columns(e, k)
                down(e, k)
                gate_and_up(e + k, 1 - k)
        e = BLOCKS // 2 - 1
        rows_to_columns(e, 1)
        hidden_to_columns(e, 0)
        down(e, 0)
        gate_and_up(e, 1)
        hidden_to_columns(e, 1)
        down(e, 1)
        transposes_of_x(l, 5)

    pe.drain().then_inc(s["mix_mm"], 1)
    pe.drain().then_inc(s["rw_mm"], 1)
    pe.wait_ge(s["const_in"], 64)
    pe.wait_ge(s["x_in"], 48)
    with pe.Fori(0, DEPTH) as l:
        pe.wait_ge(s["xt_copied"], nth(l, "xt_copied", 0))
        pe.wait_ge(s["params_in"], nth(l, "params_in", 16))
        row_projection(l)
        column_projection(l)
        column_jobs(l)
        rwkv_loop(l)
        rwkv_sample(l)
        y_norm(l)
        head_transposes(l)
        prompt_attention(l)
        sample_attention(l)
        output_projection(l)
        experts(l)


def scalar_program(act, s, m, ps):
    def copy(out, in_):
        return act.activation(out, in_, ACT.Copy)

    def seqs(ap):
        return ap.rearrange("p (b t) -> p b t", t=DS)

    def projections(l):
        for k in range(10):
            i, h = divmod(k, 2)
            n = P if i < NT else NS
            a, w = ((0, 512), (512, ACOLS - 512))[h]
            act.wait_ge(s["rows_mm"], nth(l, "rows_mm", k + 1))
            copy(m.A[0:n, i, a:a + w], ps[0:n, k % 2, 0:w]).then_inc(s["rows_copied"], 1)
        act.wait_ge(s["ki_var"], nth(l, "ki_var", 1))
        act.activation(m.kist[1], m.kist[1], ACT.Sqrt, bias=m.const("eps")[:, 0:1], scale=1.0 / 32).then_inc(s["ki_std"], 1)
        shift = m.small("shift").rearrange("p (n c) -> p n c", c=9)
        for n in range(NCH):
            act.wait_ge(s["fm_mm"], nth(l, "fm_mm", n + 1))
            if n >= 4:
                act.wait_ge(s["fm_used"], nth(l, "fm_used", n - 3))
            sample = seqs(ps[:, 4 + n % 2, 0:NS])
            if n < 7:
                copy(shift[:, n, 0:1], ps[:, 2 + n % 2, SEQ - 1:SEQ])
                copy(shift[:, n, 1:9], sample[:, :, DS - 1])
            copy(m.fm_p[n % 4][:, 3:3 + SEQ], ps[:, 2 + n % 2, :])
            copy(m.fm_s[n % 4][:, :, 3:7], sample).then_inc(s["fm_copied"], 1)

    def softplus_steps(l):
        act.wait_ge(s["lam_abs"], nth(l, "lam_abs", 1))
        act.activation(m.lam[1], m.lam[0], ACT.Exp, scale=-1.0).then_inc(s["lam_exp"], 1)
        act.wait_ge(s["lam_sum"], nth(l, "lam_sum", 1))
        act.activation(m.lam[3], m.lam[2], ACT.Ln).then_inc(s["lam_log"], 1)

    def job(l, j, out, func, width, bias=None):
        act.wait_ge(s["job_mm"], nth(l, "job_mm", j + 1))
        b = 4 + 2 * (j % 2)
        for o, i in ((out[:, 0:SEQ], ps[:, b, :]), (out[:, SEQ:width], ps[:, b + 1, 0:width - SEQ])):
            ins = copy(o, i) if func == ACT.Copy else act.activation(o, i, func) if bias is None else \
                act.activation(o, i, func, bias=bias)
        ins.then_inc(s["job_out"], 1)

    def column_stage(l):
        act.wait_ge(s["fm_used"], nth(l, "fm_used", 7))
        act.activation(m.Z[0:32, 6, :], m.Z[0:32, 6, :], ACT.Tanh)
        act.activation(m.Z[64:128, 6, :], m.Z[64:128, 6, :], ACT.Sigmoid).then_inc(s["lora_act"], 1)
        for p in range(2):
            job(l, p, m.ea[:, p, :], ACT.Sigmoid, TP, m.param("w0")[:, p:p + 1])
        for p in range(2):
            job(l, 2 + p, m.aa[:, p, :], ACT.Sigmoid, TP, m.param("a0")[:, p:p + 1])
        for p in range(2):
            job(l, 4 + p, m.gx[:, p, :], ACT.Sigmoid, T, m.param("gxb")[:, p:p + 1])
        for p in range(2):
            job(l, 6 + p, m.za[:, p, :], ACT.Sigmoid, T, m.param("gab")[:, p:p + 1])
        for p in range(2):
            job(l, 8 + p, m.gate[:, p, :], ACT.Copy, TP)
        act.wait_ge(s["dz_ready"], nth(l, "dz_ready", 1))
        act.activation(m.za_tanh, m.za, ACT.Tanh)
        act.activation(m.a_lru, m.za, ACT.Exp, scale=-1.0).then_inc(s["d_tanh"], 1)
        act.wait_ge(s["gelu_in"], nth(l, "gelu_in", 1))
        act.activation(m.gelu, m.gelu, ACT.Tanh, scale=GELU_C).then_inc(s["gelu_tanh"], 1)
        act.wait_ge(s["cum_ready"], nth(l, "cum_ready", 1))
        act.activation(m.ea, m.ea, ACT.Exp, scale=-DECAY)
        act.activation(m.ec, m.en, ACT.Exp, scale=-DECAY)
        act.activation(m.en, m.en, ACT.Exp, scale=DECAY).then_inc(s["exps_ready"], 1)
        act.wait_ge(s["job_mm"], nth(l, "job_mm", 12))
        for p in range(2):
            job(l, 10 + p, m.bonus[:, p, :], ACT.Copy, TP)
        act.wait_ge(s["om_ready"], nth(l, "om_ready", 1))
        act.activation(m.za, m.za, ACT.Sqrt).then_inc(s["om_sqrt"], 1)
        act.wait_ge(s["job_mm"], nth(l, "job_mm", 14))
        for p in range(2):
            job(l, 12 + p, m.bv[:, p, :], ACT.Sqrt, TP)

    def rwkv(l):
        with act.Fori(0, 4) as g:
            def mm(n):
                act.wait_ge(s["rw_mm"], nth(l, "rw_mm", g * RW_PE + n))

            mm(2)
            for b, t in ((4, m.BEt), (5, m.KEt), (6, m.VEt)):
                ins = copy(t.rearrange("p k n -> p (k n)"), ps[:, b, :])
            ins.then_inc(s["rw_a"], 1)
            mm(11)
            copy(m.XT_.rearrange("p k n -> p (k n)"), ps[:, 0, :]).then_inc(s["rw_a"], 1)
            mm(12)
            copy(m.FT.rearrange("p k n -> p (k n)"), ps[:, 1, :]).then_inc(s["rw_a"], 1)
            for c in range(2):
                mm(18 + 3 * c)
                copy(m.yb[:, :, bass.ds(g * (2 * CH) + c * CH, CH)], ps[:, 7, 0:128].rearrange("p (q t) -> p q t", q=2))\
                    .then_inc(s["rw_a"], 1)
        act.wait_ge(s["rws_mm"], nth(l, "rws_mm", 2))
        for b, t in ((4, m.BEt), (5, m.KEt), (6, m.VEt)):
            ins = copy(t[:, 0:2, :].rearrange("p k n -> p (k n)"), ps[:, b, 0:256])
        ins.then_inc(s["rws_a"], 1)
        act.wait_ge(s["rws_mm"], nth(l, "rws_mm", 7))
        copy(m.yb[:, :, SEQ:TP], ps[:, 7, 0:128].rearrange("p (q t) -> p q t", q=2)).then_inc(s["rws_a"], 1)
        act.wait_ge(s["yn_mm"], nth(l, "yn_mm", 2))
        for p in range(2):
            act.activation(m.ec[:, p, 0:SEQ], ps[:, 2 * p, :], ACT.Sqrt, bias=m.const("eps")[:, 1:2], scale=1.0 / 64)
            ins = act.activation(m.ec[:, p, SEQ:TP], ps[:, 2 * p + 1, 0:64], ACT.Sqrt, bias=m.const("eps")[:, 1:2],
                                 scale=1.0 / 64)
        ins.then_inc(s["yn_std"], 1)

    def attention(l):
        act.wait_ge(s["state_out"], nth(l, "state_out", 128))
        act.wait_ge(s["tr_mm"], nth(l, "tr_mm", 1))
        dst = [m.qT[:, 0, :], m.qT[:, 1, :], m.kT[:, 0, :], m.kT[:, 1, :], m.qiT, m.kiT]
        for b, o in enumerate(dst):
            act.activation(o[:, 0:SEQ], ps[:, b, :], ACT.Copy, scale=0.125 if b < 2 else 1.0)
            ins = act.activation(o[:, SEQ:T], ps[:, 6, NS * b:NS * b + NS], ACT.Copy, scale=0.125 if b < 2 else 1.0)
        ins.then_inc(s["tr_copied"], 1)

        def relus(i):
            act.wait_ge(s["idx_mm"], nth(l, "idx_mm", i))
            for h in range(4):
                k = 4 * (i - 1) + h
                if k >= 2:
                    act.wait_ge(s["rl_used"], nth(l, "rl_used", k - 1))
                act.activation(m.relu[h % 2][:, 0:P * (i + 1)], ps[:, h, 0:P * (i + 1)], ACT.Relu, scale=32 ** -0.5)\
                    .then_inc(s["relu_done"], 1)

        for k in range(16):
            i, h = divmod(k, 4)
            if h == 0 and i:
                relus(i)
            act.wait_ge(s["lg_ready"], nth(l, "lg_ready", k + 1))
            act.activation(m.lg[k % 2][:, 0:P * (i + 1)], m.lg[k % 2][:, 0:P * (i + 1)], ACT.Exp,
                           bias=m.nmax[:, k % 2:k % 2 + 1], accum_out=m.ssum[:, k % 2:k % 2 + 1]).then_inc(s["p_exp"], 1)
            act.wait_ge(s["pt_mm"], nth(l, "pt_mm", k + 1))
            if k >= 2:
                act.wait_ge(s["pv_mm"], nth(l, "pv_mm", k - 1))
            copy(m.pT[k % 2][:, 0:i + 1, :].rearrange("p c n -> p (c n)"), ps[:, 6, 0:P * (i + 1)]).then_inc(s["pt_copied"], 1)
            if h == 3:
                act.wait_ge(s["pv_mm"], nth(l, "pv_mm", k + 1))
                copy(m.yT[:, 0:2, P * i:P * i + P], ps[:, 7, 0:256].rearrange("p (q n) -> p q n", q=2))\
                    .then_inc(s["ya_copied"], 1)

        act.wait_ge(s["s_wb_mm"], nth(l, "s_wb_mm", 1))
        copy(m.WB, ps[:, 0, 0:4 * NS].rearrange("p (h b t) -> p b h t", h=4, t=DS)).then_inc(s["s_wb"], 1)
        act.wait_ge(s["s_idx_mm"], nth(l, "s_idx_mm", 1))
        act.activation(m.relu[0], ps[:, 1, :], ACT.Relu, scale=32 ** -0.5)
        for h in range(4):
            ins = act.activation(m.relu_n[0:NS, h, :], ps[0:NS, 2 + h, 0:NS], ACT.Relu, scale=32 ** -0.5)
        ins.then_inc(s["s_relu"], 1)
        act.wait_ge(s["s_tr_mm"], nth(l, "s_tr_mm", 1))
        copy(m.score[0:NS, 0:PAST], ps[0:NS, 0, :]).then_inc(s["s_score"], 1)
        for g in range(2):
            act.wait_ge(s["s_lg_mm"], nth(l, "s_lg_mm", g + 1))
            if g:
                act.wait_ge(s["s_pt_mm"], nth(l, "s_pt_mm", 1))
            copy(m.lg[0][:, 0:PAST], ps[:, 2, :])
            copy(m.lg[0][:, PAST:T], ps[:, 3, 0:NS]).then_inc(s["s_lg"], 1)
            act.wait_ge(s["s_max"], nth(l, "s_max", g + 1))
            act.activation(m.lg[0], m.lg[0], ACT.Exp, bias=m.nmax[:, 0:1], accum_out=m.ssum[:, 0:1]).then_inc(s["s_exp"], 1)
            act.wait_ge(s["s_pt_mm"], nth(l, "s_pt_mm", g + 1))
            if g:
                act.wait_ge(s["s_pv_mm"], nth(l, "s_pv_mm", 1))
            copy(m.pT[0].rearrange("p c n -> p (c n)"), ps[:, 6, :])
            copy(m.pTn[0:NS, :], ps[0:NS, 5, 0:P]).then_inc(s["s_pt"], 1)
        act.wait_ge(s["s_pv_mm"], nth(l, "s_pv_mm", 2))
        for p in range(2):
            for h in range(2):
                q = slice(64 * h, 64 * h + 64)
                ins = copy(seqs(m.yT[q, p, SEQ:T]), ps[q, 7, P * p:P * p + P].rearrange("p (b h t) -> p b h t", b=DB, h=4)[:, :, 2 * p + h, :])
        ins.then_inc(s["attn_done"], 1)

    def norm(l, first):
        if first == 0:
            act.wait_ge(s["rows_stored"], nth(l, "rows_stored", 96))
            act.wait_ge(s["small_out"], nth(l, "small_out", 16))
        for i in range(5):
            n = P if i < NT else NS
            act.wait_ge(s["ln_var"], nth(l, "ln_var", first + i + 1))
            act.activation(m.std[i % 2][0:n], m.mv[i % 2][0:n, 1:2], ACT.Sqrt, bias=m.const("eps")[0:n, 0:1])\
                .then_inc(s["ln_std"], 1)
        for i in range(5):
            n = P if i < NT else NS
            act.wait_ge(s["xt_mm"], nth(l, "xt_mm", first + i + 1))
            for h in range(2):
                ins = copy(m.xT[:, 4 * h:4 * h + 4, P * i:P * i + n], ps[:, 4 + h, 0:4 * n].rearrange("p (c t) -> p c t", c=4))
            ins.then_inc(s["xt_copied"], 1)

    def experts(l):
        act.wait_ge(s["router_mm"], nth(l, "router_mm", 1))
        act.activation(m.gsig[:, 0:NT, :], ps[:, 7, 0:NT * NEXP].rearrange("p (i e) -> p i e", e=NEXP), ACT.Sigmoid)
        act.activation(m.gsig[0:NS, NT, :], ps[0:NS, 7, NT * NEXP:5 * NEXP], ACT.Sigmoid).then_inc(s["router_sig"], 1)

        def columns_of_rows(e, k):
            act.wait_ge(s["xgt_mm"], nth(l, "xgt_mm", e * 2 + (k + 1)))
            copy(m.xgT.rearrange("p (h c) n -> p h (c n)", h=2), ps[:, 0:2, :]).then_inc(s["xgt_copied"], 1)

        def silu(e, k):
            act.wait_ge(s["h_ready"], nth(l, "h_ready", e * 2 + k))
            act.wait_ge(s["gu_mm"], nth(l, "gu_mm", e * 2 + (k + 1)))
            act.activation(m.silu, ps[:, 3, 0:DEXP], ACT.Silu).then_inc(s["silu_done"], 1)

        def rows_back(e, k):
            act.wait_ge((s["y0_stored"], s["y1_stored"])[k], nth(l, f"y{k}_stored", e * 16))
            act.wait_ge(s["down_mm"], nth(l, "down_mm", e * 2 + (k + 1)))
            copy(m.y[k][:, 0:512], ps[:, 5, :]).then_inc(s["y_copied_a"], 1)

        def store(e, k):
            act.wait_ge(s["y_copied_a"], nth(l, "y_copied_a", e * 2 + (k + 1)))
            act.wait_ge(s["y_copied_v"], nth(l, "y_copied_v", e * 2 + (k + 1)))
            act.dma_start(m.rows_out.rearrange("(n p) d -> p n d", p=P)[:, bass.ds(e * 2 + k, 1), :]
                          .rearrange("p n d -> p (n d)"), m.y[k]).then_inc((s["y0_stored"], s["y1_stored"])[k], 16)

        columns_of_rows(0, 0)
        silu(0, 0)
        with act.Fori(0, BLOCKS // 2 - 1) as e:
            for k in range(2):
                columns_of_rows(e + k, 1 - k)
                rows_back(e, k)
                silu(e + k, 1 - k)
                store(e, k)
        e = BLOCKS // 2 - 1
        columns_of_rows(e, 1)
        rows_back(e, 0)
        silu(e, 1)
        store(e, 0)
        rows_back(e, 1)
        store(e, 1)

    for name in ("xt_copied", "xgt_copied", "y_copied_a", "y0_stored", "y1_stored"):
        act.drain().then_inc(s[name], 1)
    act.wait_ge(s["const_in"], 64)
    act.wait_ge(s["zeroed"], 1)
    with act.Fori(0, DEPTH) as l:
        softplus_steps(l)
        projections(l)
        column_stage(l)
        rwkv(l)
        attention(l)
        norm(l, 0)
        experts(l)
        norm(l, 5)


def vector_program(dve, s, m, ps):
    tt, ts, stt = dve.tensor_tensor, dve.tensor_scalar, dve.scalar_tensor_tensor
    mul, add, sub = ALU.mult, ALU.add, ALU.subtract
    ident = m.const("ident")

    def seqs(ap):
        return ap.rearrange("p (b t) -> p b t", t=DS)

    def lay(ap):
        return ap.rearrange("p (a b) -> p a b", b=P) if len(ap.shape) == 2 else ap

    def softplus(l):
        L = m.lam
        stt(L[0], m.param("lam"), -1.0, m.param("lam"), mul, ALU.max).then_inc(s["lam_abs"], 1)
        ts(L[7], m.param("lam"), -1.0, 0.0, mul, ALU.max)
        ts(m.omka, m.param("ka"), -1.0, 1.0, mul, add)
        dve.wait_ge(s["lam_exp"], nth(l, "lam_exp", 1))
        ts(L[2], L[1], 1.0, None, add).then_inc(s["lam_sum"], 1)
        dve.wait_ge(s["lam_log"], nth(l, "lam_log", 1))
        ts(L[4], L[2], 1.0, None, ALU.is_equal)
        dve.drain()
        tt(L[3], L[3], L[4], add)
        stt(L[5], L[2], -1.0, L[4], add, add)
        dve.drain()
        dve.reciprocal(L[5], L[5])
        tt(L[6], L[1], L[3], mul)
        dve.drain()
        tt(L[6], L[6], L[5], mul)
        dve.drain()
        tt(L[6], L[6], L[7], add)
        dve.drain()
        ts(L[6], L[6], 8.0, None, mul)

    def rotate(x1, x2, c, sn, t):
        tt(t[0], x1, c, mul)
        tt(t[1], x2, sn, mul)
        tt(t[2], x2, c, mul)
        tt(t[3], x1, sn, mul)
        dve.drain()
        tt(x1, t[0], t[1], sub)
        return tt(x2, t[2], t[3], add)

    def row_stage(l):
        dve.wait_ge(s["rows_copied"], nth(l, "rows_copied", 10))
        ki = m.A[:, :, C_KI:C_KI + 32]
        dve.tensor_reduce(m.kist[0], ki, AX.X, add)
        dve.drain()
        ts(m.kist[0], m.kist[0], 1.0 / 32, None, mul)
        dve.drain()
        tt(m.ki_c, ki, m.kist[0].unsqueeze(2).broadcast_to([P, 5, 32]), sub)
        dve.drain()
        tt(m.ki_2, m.ki_c, m.ki_c, mul)
        dve.drain()
        dve.tensor_reduce(m.kist[1], m.ki_2, AX.X, add).then_inc(s["ki_var"], 1)

        def table(name, half, heads):
            return m.const(name).rearrange("p (i f) -> p i f", f=half).unsqueeze(2).broadcast_to([P, 5, heads, half])

        qk = m.A[:, :, 0:512].rearrange("p i (h d) -> p i h d", d=64)
        rotate(qk[:, :, :, 0:8], qk[:, :, :, 8:16], table("cos_q", 8, 8), table("sin_q", 8, 8), m.rope_q)
        qi = m.A[:, :, C_QI:C_KI].rearrange("p i (h d) -> p i h d", d=32)
        rotate(qi[:, :, :, 0:4], qi[:, :, :, 4:8], table("cos_i", 4, 4), table("sin_i", 4, 4), m.rope_i)
        wi = m.A[:, :, C_WI:ACOLS]
        ts(wi, wi, 0.5, None, mul)
        dve.wait_ge(s["ki_std"], nth(l, "ki_std", 1))
        dve.reciprocal(m.kist[1], m.kist[1])
        dve.drain()
        tt(m.ki_c, m.ki_c, m.kist[1].unsqueeze(2).broadcast_to([P, 5, 32]), mul)
        dve.drain()
        tt(m.ki_c, m.ki_c, m.param("idxg").unsqueeze(1).broadcast_to([P, 5, 32]), mul)
        dve.drain()
        tt(ki, m.ki_c, m.param("idxb").unsqueeze(1).broadcast_to([P, 5, 32]), add)
        dve.drain()
        t = [r[:, :, 0, :] for r in m.rope_i]
        c = m.const("cos_i").rearrange("p (i f) -> p i f", f=4)
        sn = m.const("sin_i").rearrange("p (i f) -> p i f", f=4)
        rotate(ki[:, :, 0:4], ki[:, :, 4:8], c, sn, t).then_inc(s["rows_ready"], 1)

    def taps(out, src, w, first, bias=None):
        n = len(w)
        width = SEQ if len(src.shape) == 2 else DS

        def at(k):
            return src[:, first + k:first + k + width] if len(src.shape) == 2 else src[:, :, first + k:first + k + width]

        ts(out, at(0), w[0], bias, mul, add) if bias is not None else ts(out, at(0), w[0], None, mul)
        for k in range(1, n):
            dve.drain()
            ins = stt(out, at(k), w[k], out, mul, add)
        return ins

    def columns(l):
        dve.wait_ge(s["rows_mm"], nth(l, "rows_mm", 10))
        dve.memset(m.Z[:, :, T:TP], 0.0)
        for f in m.fm_p:
            dve.memset(f[:, 0:3], 0.0)
        mu = m.param("mu")
        shift = m.param("shift").rearrange("p (n b) -> p n b", b=DB)
        for n in range(7):
            fp, fs = m.fm_p[n % 4], m.fm_s[n % 4]
            dve.tensor_copy(fs[:, :, 2], shift[:, n, :])
            dve.drain()
            dve.wait_ge(s["fm_copied"], nth(l, "fm_copied", n + 1))
            tt(m.diff[:, 0:SEQ], fp[:, 2:2 + SEQ], fp[:, 3:3 + SEQ], sub)
            tt(seqs(m.diff[:, SEQ:T]), fs[:, :, 2:6], fs[:, :, 3:7], sub)
            dve.drain()
            stt(m.Z[:, n, 0:SEQ], m.diff[:, 0:SEQ], mu[:, n:n + 1], fp[:, 3:3 + SEQ], mul, add)
            stt(seqs(m.Z[:, n, SEQ:T]), seqs(m.diff[:, SEQ:T]), mu[:, n:n + 1], fs[:, :, 3:7], mul, add)\
                .then_inc(s["fm_used"], 1)
        convc = m.param("convc").rearrange("p (j b t) -> p j b t", j=2, b=DB)
        tail = m.small("convc").rearrange("p (j c) -> p j c", j=2)
        cw = m.param("cw")
        for j in range(2):
            n = 7 + 3 * j
            cg, xin, bg = n % 4, (n + 1) % 4, (n + 2) % 4
            dve.tensor_copy(m.fm_s[cg][:, :, 1:3], convc[:, j, :, :])
            dve.wait_ge(s["fm_copied"], nth(l, "fm_copied", n + 3))
            tt(m.fm_p[cg][:, 3:3 + SEQ], m.fm_p[cg][:, 3:3 + SEQ], m.fm_p[xin][:, 3:3 + SEQ], mul)
            tt(m.fm_s[cg][:, :, 3:7], m.fm_s[cg][:, :, 3:7], m.fm_s[xin][:, :, 3:7], mul)
            dve.drain()
            w = [cw[:, 3 * j + k:3 * j + k + 1] for k in range(3)]
            taps(m.conv[:, 0:SEQ], m.fm_p[cg], w, 1)
            taps(seqs(m.conv[:, SEQ:T]), m.fm_s[cg], w, 1)
            dve.tensor_copy(tail[:, j, 0:2], m.fm_p[cg][:, 1 + SEQ:3 + SEQ])
            dve.tensor_copy(tail[:, j, 2:18].rearrange("p (b t) -> p b t", t=2), m.fm_s[cg][:, :, 5:7])
            dve.drain()
            tt(m.yT[:, 4 + j, 0:SEQ], m.conv[:, 0:SEQ], m.fm_p[bg][:, 3:3 + SEQ], mul)
            tt(seqs(m.yT[:, 4 + j, SEQ:T]), seqs(m.conv[:, SEQ:T]), m.fm_s[bg][:, :, 3:7], mul).then_inc(s["fm_used"], 3)
        convd = m.param("convd").rearrange("p (j b t) -> p j b t", j=2, b=DB)
        tail = m.small("convd").rearrange("p (j c) -> p j c", j=2)
        dw, db = m.param("dw"), m.param("db")
        for j in range(2):
            n = 13 + 2 * j
            xb, gb = n % 4, (n + 1) % 4
            dve.tensor_copy(m.fm_s[xb][:, :, 0:3], convd[:, j, :, :])
            dve.drain()
            dve.wait_ge(s["fm_copied"], nth(l, "fm_copied", n + 2))
            w = [dw[:, 4 * j + k:4 * j + k + 1] for k in range(4)]
            taps(m.xc[:, j, 0:SEQ], m.fm_p[xb], w, 0, db[:, j:j + 1])
            taps(seqs(m.xc[:, j, SEQ:T]), m.fm_s[xb], w, 0, db[:, j:j + 1]).then_inc(s["conv_done"], 1)
            dve.tensor_copy(tail[:, j, 0:3], m.fm_p[xb][:, SEQ:3 + SEQ])
            dve.tensor_copy(tail[:, j, 3:27].rearrange("p (b t) -> p b t", t=3), m.fm_s[xb][:, :, 4:7])
            dve.tensor_copy(m.gb[:, j, 0:SEQ], m.fm_p[gb][:, 3:3 + SEQ])
            dve.tensor_copy(seqs(m.gb[:, j, SEQ:T]), m.fm_s[gb][:, :, 3:7]).then_inc(s["fm_used"], 2)

    def column_math(l):
        r, k, v = (m.Z[:, 2 * n:2 * n + 2, :] for n in range(3))
        for p in range(2):
            ts(m.nkk[:, p, :], k[:, p, :], m.param("kkw")[:, p:p + 1], None, mul)
        dve.drain()
        tt(m.bv, m.nkk, m.nkk, mul).then_inc(s["kk_in"], 1)
        dve.wait_ge(s["job_out"], nth(l, "job_out", 2))
        for p in range(2):
            dve.tensor_tensor_scan(m.en[:, p, :], m.const("reset"), m.ea[:, p, :], 0.0, mul, add)
        dve.drain()
        tt(m.ea, m.en, m.ea, sub).then_inc(s["cum_ready"], 1)
        dve.wait_ge(s["job_out"], nth(l, "job_out", 4))
        for p in range(2):
            ts(m.kf[:, p, :], m.aa[:, p, :], m.param("ka")[:, p:p + 1], m.omka[:, p:p + 1], mul, add)
        dve.drain()
        tt(m.kf, m.kf, k, mul)
        dve.drain()
        for p in range(2):
            stt(m.bonus[:, p, :], r[:, p, :], m.param("rk")[:, p:p + 1], m.kf[:, p, :], mul, mul)
        dve.drain().then_inc(s["bonus_in"], 1)
        dve.wait_ge(s["job_out"], nth(l, "job_out", 8))
        for p in range(2):
            ts(m.za[:, p, :], m.za[:, p, :], m.lam[6][:, p:p + 1], None, mul)
        dve.drain().then_inc(s["dz_ready"], 1)
        dve.wait_ge(s["fm_mm"], nth(l, "fm_mm", NCH))
        tt(m.gelu, m.gb, m.gb, mul)
        dve.drain()
        ts(m.gelu, m.gelu, 0.044715, 1.0, mul, add)
        dve.drain()
        tt(m.gelu, m.gelu, m.gb, mul).then_inc(s["gelu_in"], 1)
        dve.wait_ge(s["d_tanh"], nth(l, "d_tanh", 1))
        ts(m.za, m.za_tanh, 1.0, None, add)
        dve.drain()
        dve.reciprocal(m.za, m.za)
        dve.drain()
        stt(m.za, m.za, 2.0, m.za_tanh, mul, mul).then_inc(s["om_ready"], 1)
        tt(m.gx, m.gx, m.xc, mul)
        dve.wait_ge(s["gelu_tanh"], nth(l, "gelu_tanh", 1))
        stt(m.gelu, m.gelu, 1.0, m.gb, add, mul)
        dve.drain()
        dve.wait_ge(s["om_sqrt"], nth(l, "om_sqrt", 1))
        tt(m.gx, m.gx, m.za, mul)
        dve.drain()
        us, as_ = m.gx[:, :, SEQ:T].rearrange("p q (b t) -> p q b t", t=DS), m.a_lru[:, :, SEQ:T].rearrange("p q (b t) -> p q b t", t=DS)
        h0 = m.param("lru").rearrange("p (q b) -> p q b", b=DB)
        tt(m.hs[:, :, 0:DB], as_[:, :, :, 0], h0, mul)
        dve.drain()
        tt(us[:, :, :, 0], us[:, :, :, 0], m.hs[:, :, 0:DB], add)
        dve.memset(as_[:, :, :, 0], 0.0)
        dve.drain()
        for p in range(2):
            dve.tensor_tensor_scan(m.hs[:, p, :], m.a_lru[:, p, :], m.gx[:, p, :], 0.0, mul, add)
        dve.drain()
        tail = m.small("lru").rearrange("p (q c) -> p q c", q=2)
        dve.tensor_copy(tail[:, :, 0:1], m.hs[:, :, SEQ - 1:SEQ])
        dve.tensor_copy(tail[:, :, 1:9], m.hs[:, :, SEQ:T].rearrange("p q (b t) -> p q b t", t=DS)[:, :, :, DS - 1])\
            .then_inc(s["small_ready"], 1)
        for p in range(2):
            stt(m.yT[:, 6 + p, :], m.gelu[:, p, :], 0.5, m.hs[:, p, :], mul, mul)
        dve.drain()
        dve.memset(m.TB, 0.0).then_inc(s["states_zeroed"], 1)
        for t in (m.AE, m.BE, m.KE, m.VE, m.Tst):
            dve.memset(t, 0.0)
        dve.wait_ge(s["job_out"], nth(l, "job_out", 12))
        tt(m.bonus, m.bonus, v, mul)
        dve.wait_ge(s["job_out"], nth(l, "job_out", 14))
        ts(m.bv, m.bv, 1e-12, None, ALU.max)
        dve.drain()
        dve.reciprocal(m.bv, m.bv)
        dve.drain()
        stt(m.nkk, m.nkk, -1.0, m.bv, mul, mul)
        dve.drain()
        dve.drain()
        dve.wait_ge(s["exps_ready"], nth(l, "exps_ready", 1))
        stt(m.bv, m.nkk, -1.0, m.aa, mul, mul)
        dve.drain()

    def chunk_inputs(at, n):
        def chunks(t, rows):
            return t[rows, :, at].rearrange("p q (c t) -> p c q t", t=CH)

        def four(t):
            return t.rearrange("p (c q) n -> p c q n", q=2)[:, 0:n]

        r, v = m.Z[:, 0:2, :], m.Z[:, 4:6, :]
        for h in range(2):
            rows = slice(64 * h, 64 * h + 64)
            for c in range(n):
                def cut(t):
                    return chunks(t, rows)[:, c]

                def put(t):
                    return four(t)[rows, c, :, rows]
                tt(put(m.AE), cut(m.nkk), cut(m.ea), mul)
                tt(put(m.BE), cut(m.bv), cut(m.en), mul)
                tt(put(m.KE), cut(m.kf), cut(m.en), mul)
                dve.tensor_copy(put(m.VE), cut(v))
        everyone = slice(0, P)
        for c in range(n):
            tt(four(m.RC)[:, c], chunks(r, everyone)[:, c], chunks(m.ec, everyone)[:, c], mul)

    def flat(t, n=4):
        return t[:, 0:n, :].rearrange("p k n -> p (k n)")

    def mask(out, bank, name, n, sem=None):
        w = CONST[name][1]
        k = 8 if w == CH else n
        ins = tt(out, ps[:, bank, 0:k * w].rearrange("p (k n) -> p k n", n=w),
                 m.const(name).unsqueeze(1).broadcast_to([P, k, w]), mul)
        return ins

    def rwkv_loop(l):
        eye = ident.unsqueeze(1).broadcast_to([P, 4, P])
        with dve.Fori(0, 4) as g:
            def mm(n):
                dve.wait_ge(s["rw_mm"], nth(l, "rw_mm", g * RW_PE + n))

            dve.drain()
            mm(0)
            chunk_inputs(bass.ds(g * (2 * CH), 2 * CH), 2)
            for c in range(2):
                dve.tensor_copy(m.pc[:, c, :], m.ec[:, :, bass.ds(g * (2 * CH) + (c * CH + CH - 1), 1)]
                                .rearrange("p q z -> p (q z)"))
            dve.drain().then_inc(s["rw_in"], 1)
            mm(1)
            mask(m.D, 0, "strict_near", 4).then_inc(s["rw_v"], 1)
            mask(m.DT, 1, "strict_near_t", 4).then_inc(s["rw_v"], 1)
            mask(m.E, 0, "strict_far", 4).then_inc(s["rw_v"], 1)
            mask(m.Mak, 2, "strict", 4).then_inc(s["rw_v"], 1)
            mask(m.attn.rearrange("p a k t -> p (a k) t"), 3, "incl", 4).then_inc(s["rw_v"], 1)
            mm(3)
            dve.tensor_copy(flat(m.D2), ps[:, 0, :]).then_inc(s["rw_v"], 1)
            mm(4)
            dve.tensor_copy(flat(m.D2T), ps[:, 1, :]).then_inc(s["rw_v"], 1)
            mm(5)
            dve.tensor_copy(flat(m.D4), ps[:, 2, :]).then_inc(s["rw_v"], 1)
            mm(6)
            dve.tensor_copy(flat(m.D4T), ps[:, 3, :]).then_inc(s["rw_v"], 1)

            def grow(n, bank, to, plus):
                dve.drain()
                mm(n)
                tt(to, ps[:, bank, :].rearrange("p (k n) -> p k n", n=P), plus, add).then_inc(s["rw_v"], 1)

            grow(7, 0, m.X, eye)
            grow(8, 1, m.X, m.X)
            grow(9, 2, m.X, m.X)
            grow(10, 3, m.X, m.X)
            grow(13, 2, m.Zs, m.X)
            grow(14, 3, m.Zs, m.X)
            grow(15, 0, m.Zs, m.X)
            for c in range(2):
                mm(16 + 3 * c)
                dve.tensor_copy(flat(m.W, 2), ps[:, 4, 0:256]).then_inc(s["rwc_v"], 1)
                mm(17 + 3 * c)
                dve.tensor_copy(flat(m.U, 2), ps[:, 5, 0:256]).then_inc(s["rwc_v"], 1)
                mm(18 + 3 * c)
                tt(m.Tst, ps[:, 6, 0:256].rearrange("p (q n) -> p q n", n=P),
                   m.pc[:, c, :].unsqueeze(2).broadcast_to([P, 2, P]), mul).then_inc(s["rwc_v"], 1)

    def rwkv_sample(l):
        chunk_inputs(slice(SEQ, TP), 1)
        dve.drain()
        dve.memset(m.AEb, 0.0)
        dve.drain()
        for p in range(2):
            for h in range(2):
                src = m.AE[:, p, 64 * h:64 * h + NS]
                for b in range(DB):
                    c = 64 * h + DS * b
                    ins = dve.tensor_copy(m.AEb[:, p, b, c:c + DS], src[:, DS * b:DS * b + DS])
        ins.then_inc(s["rws_in"], 1)
        dve.wait_ge(s["rws_mm"], nth(l, "rws_mm", 1))
        mask(m.D[:, 0:2], 0, "s_strict", 2)
        mask(m.DT[:, 0:2], 1, "s_strict_t", 2)
        mask(m.Mak[:, 0:2], 2, "s_strict", 2)
        for a in range(2):
            tt(m.attn[:, a, 0:2, :], ps[:, 3, 256 * a:256 * a + 128].rearrange("p (k n) -> p k n", n=CH),
               m.const("s_incl").unsqueeze(1).broadcast_to([P, 2, CH]), mul)
        dve.drain().then_inc(s["rws_v"], 1)
        dve.wait_ge(s["rws_mm"], nth(l, "rws_mm", 3))
        tt(m.X[:, 0:2], ps[:, 0, 0:256].rearrange("p (k n) -> p k n", n=P), ident.unsqueeze(1).broadcast_to([P, 2, P]), add)\
            .then_inc(s["rws_v"], 1)
        dve.drain()
        dve.wait_ge(s["rws_mm"], nth(l, "rws_mm", 4))
        tt(m.X[:, 0:2], ps[:, 1, 0:256].rearrange("p (k n) -> p k n", n=P), m.X[:, 0:2], add).then_inc(s["rws_v"], 1)
        dve.wait_ge(s["rws_mm"], nth(l, "rws_mm", 5))
        dve.tensor_copy(flat(m.W, 2), ps[:, 4, 0:256]).then_inc(s["rws_v"], 1)
        dve.wait_ge(s["rws_mm"], nth(l, "rws_mm", 6))
        dve.tensor_copy(flat(m.U, 2), ps[:, 5, 0:256]).then_inc(s["rws_v"], 1)
        ec = m.ec[:, :, SEQ:T].rearrange("p q (b t) -> p q b t", t=DS)
        own = m.const("s_rows").unsqueeze(2).broadcast_to([P, DB, P])
        for p in range(2):
            dve.drain()
            dve.wait_ge(s["rws_a"], nth(l, "rws_a", 1))
            if p:
                dve.wait_ge(s["rws_mm"], nth(l, "rws_mm", 8))
            tt(m.UEb, m.U[:, p, :].unsqueeze(1).broadcast_to([P, DB, P]), own, mul)
            tt(m.VEb, m.VEt[:, p, :].unsqueeze(1).broadcast_to([P, DB, P]), own, mul)
            dve.drain().then_inc(s["rws_v"], 1)
            dve.wait_ge(s["rws_mm"], nth(l, "rws_mm", 8 + p))
            for h in range(2):
                ins = tt(m.TB[:, p, 4 * h:4 * h + 4, :], ps[:, 2 * p + h, :].rearrange("p (b n) -> p b n", n=P),
                         ec[:, p, 4 * h:4 * h + 4, DS - 1].unsqueeze(2).broadcast_to([P, 4, P]), mul)
            ins.then_inc(s["rws_v"], 1)

    def rwkv_out(l):
        dve.wait_ge(s["rws_a"], nth(l, "rws_a", 2))
        dve.wait_ge(s["yn_mm"], nth(l, "yn_mm", 1))
        for p in range(2):
            stt(m.yc[:, p, 0:SEQ], ps[:, 2 * p, :], -1.0 / 64, m.yb[:, p, 0:SEQ], mul, add)
            stt(m.yc[:, p, SEQ:TP], ps[:, 2 * p + 1, 0:64], -1.0 / 64, m.yb[:, p, SEQ:TP], mul, add)
        dve.drain()
        tt(m.y2, m.yc, m.yc, mul).then_inc(s["yn_in"], 1)
        dve.wait_ge(s["yn_std"], nth(l, "yn_std", 1))
        dve.reciprocal(m.ec, m.ec)
        dve.drain()
        tt(m.yc, m.yc, m.ec, mul)
        dve.drain()
        for p in range(2):
            ts(m.yc[:, p, :], m.yc[:, p, :], m.param("lnxg")[:, p:p + 1], m.param("lnxb")[:, p:p + 1], mul, add)
        dve.drain()
        tt(m.yc, m.yc, m.bonus, add)
        dve.drain()
        tt(m.yT[:, 2:4, :], m.yc[:, :, 0:T], m.gate[:, :, 0:T], mul).then_inc(s["rw_done"], 1)

    def select(rows, width, topk):
        sc, wk = m.score[rows, 0:width], m.work[rows, 0:width]
        eq, gt, pre, bias = (t[rows, 0:width] for t in (m.eq, m.gt, m.pre, m.bias))
        top = m.top8[rows]
        dve.tensor_copy(wk, sc)
        dve.drain()
        with dve.Fori(0, (topk - 1) // 8):
            dve.max(top, wk)
            dve.drain()
            dve.match_replace(wk, top, wk, -3e38)
            dve.drain()
        dve.max(top, wk)
        dve.drain()
        last = (topk - 1) % 8
        thr = top[:, last:last + 1]
        ts(gt, sc, thr, None, ALU.is_gt)
        ts(eq, sc, thr, None, ALU.is_equal)
        dve.drain()
        dve.tensor_reduce(m.cnt[rows, 0:1], gt, AX.X, add)
        dve.tensor_tensor_scan(pre, m.const("ones")[rows].broadcast_to([rows.stop, width]), eq, 0.0, mul, add)
        dve.drain()
        ts(m.cnt[rows, 1:2], m.cnt[rows, 0:1], -1.0, float(topk), mul, add)
        dve.drain()
        stt(pre, pre, m.cnt[rows, 1:2], eq, ALU.is_le, mul)
        dve.drain()
        tt(pre, pre, gt, add)
        dve.drain()
        ts(bias, pre, 1.0, -NEG, sub, mul)

    def attention(l):
        dve.tensor_copy(m.KR[:, 0:NT].rearrange("p i (h d) -> p i h d", d=32),
                        m.A[:, 0:NT, C_KI:C_KI + 32].unsqueeze(2).broadcast_to([P, NT, 4, 32]))
        dve.tensor_copy(m.KR[0:NS, NT].rearrange("p (h d) -> p h d", d=32),
                        m.A[0:NS, NT, C_KI:C_KI + 32].unsqueeze(1).broadcast_to([NS, 4, 32]))
        dve.drain().then_inc(s["kr_ready"], 1)
        dve.tensor_copy(m.bias[:, 0:P], m.const("causal"))

        def scores(i):
            w = P * (i + 1)
            for h in range(4):
                dve.drain()
                dve.wait_ge(s["relu_done"], nth(l, "relu_done", 4 * (i - 1) + h + 1))
                wi = m.A[:, i, C_WI + h:C_WI + h + 1]
                if h:
                    ins = stt(m.score[:, 0:w], m.relu[h % 2][:, 0:w], wi, m.score[:, 0:w], mul, add)
                else:
                    ins = ts(m.score[:, 0:w], m.relu[0][:, 0:w], wi, None, mul)
                ins.then_inc(s["rl_used"], 1)
            dve.drain()
            tt(m.score[:, w - P:w], m.score[:, w - P:w], m.const("causal"), add)
            dve.drain()
            select(slice(0, P), w, TOPK_P)
            dve.drain()
            tt(m.bias[:, w - P:w], m.bias[:, w - P:w], m.const("causal"), add)

        def softmax_in(k):
            i, h = divmod(k, 4)
            w = P * (i + 1)
            dve.drain()
            dve.wait_ge(s["lg_mm"], nth(l, "lg_mm", k + 1))
            if k >= 2:
                dve.wait_ge(s["pt_mm"], nth(l, "pt_mm", k - 1))
            tt(m.lg[k % 2][:, 0:w], ps[:, 4 + k % 2, 0:w], m.bias[:, 0:w], add)
            dve.drain()
            dve.tensor_reduce(m.nmax[:, k % 2:k % 2 + 1], m.lg[k % 2][:, 0:w], AX.X, ALU.max, negate=True)\
                .then_inc(s["lg_ready"], 1)

        def softmax_out(k):
            w = P * (k // 4 + 1)
            dve.wait_ge(s["p_exp"], nth(l, "p_exp", k + 1))
            dve.reciprocal(m.rsum[:, k % 2:k % 2 + 1], m.ssum[:, k % 2:k % 2 + 1])
            dve.drain()
            ts(m.lg[k % 2][:, 0:w], m.lg[k % 2][:, 0:w], m.rsum[:, k % 2:k % 2 + 1], None, mul).then_inc(s["p_ready"], 1)

        for i in range(NT):
            if i:
                scores(i)
            for h in range(4):
                softmax_in(4 * i + h)
                if h:
                    softmax_out(4 * i + h - 1)
            softmax_out(4 * i + 3)

        dve.memset(m.QB, 0.0)
        dve.wait_ge(s["pv_mm"], nth(l, "pv_mm", 16))
        dve.tensor_copy(m.wb_in[0:NS], m.A[0:NS, NT, C_WI:ACOLS].unsqueeze(2).broadcast_to([NS, 4, P]))
        dve.drain()
        for p in range(2):
            for h in range(2):
                q = slice(64 * h, 64 * h + 64)
                dve.tensor_copy(m.QB[q, p, :, DS * (2 * p + h):DS * (2 * p + h) + DS], seqs(m.qT[q, p, SEQ:T]))
        for h in range(4):
            dve.tensor_copy(m.QI[0:32, :, h, :], seqs(m.qiT[32 * h:32 * h + 32, SEQ:T]))
        dve.drain().then_inc(s["s_prep"], 1)
        dve.wait_ge(s["s_relu"], nth(l, "s_relu", 1))
        dve.wait_ge(s["s_wb"], nth(l, "s_wb", 1))
        R = m.relu[0].rearrange("p (c n) -> p c n", c=4)
        tt(R, R, m.WB.rearrange("p b h t -> p (b h t)").unsqueeze(1).broadcast_to([P, 4, P]), mul)
        dve.drain()
        R = m.relu[0].rearrange("p (c h t) -> p c h t", h=4, t=DS)
        S4 = m.sums.rearrange("p c (b t) -> p (c b) t", t=DS)
        tt(S4, R[:, :, 0, :], R[:, :, 1, :], add)
        for h in (2, 3):
            dve.drain()
            ins = tt(S4, S4, R[:, :, h, :], add)
        ins.then_inc(s["s_sums"], 1)
        new = m.score[0:NS, PAST:T]
        ts(new, m.relu_n[0:NS, 0, :], m.A[0:NS, NT, C_WI:C_WI + 1], None, mul)
        for h in range(1, 4):
            dve.drain()
            stt(new, m.relu_n[0:NS, h, :], m.A[0:NS, NT, C_WI + h:C_WI + h + 1], new, mul, add)
        dve.drain()
        tt(new, new, m.const("new_bias")[0:NS], add)
        dve.drain()
        dve.wait_ge(s["s_score"], nth(l, "s_score", 1))
        select(slice(0, NS), T, TOPK_S)
        dve.drain()
        tt(m.bias[0:NS, PAST:T], m.bias[0:NS, PAST:T], m.const("new_bias")[0:NS], add).then_inc(s["s_bias"], 1)
        for g in range(2):
            dve.wait_ge(s["s_lg"], nth(l, "s_lg", g + 1))
            dve.tensor_reduce(m.nmax[:, 0:1], m.lg[0], AX.X, ALU.max, negate=True).then_inc(s["s_max"], 1)
            dve.wait_ge(s["s_exp"], nth(l, "s_exp", g + 1))
            dve.reciprocal(m.rsum[:, 0:1], m.ssum[:, 0:1])
            dve.drain()
            ts(m.lg[0], m.lg[0], m.rsum[:, 0:1], None, mul).then_inc(s["s_p"], 1)

    def norm(l, first, residual):
        def stats(i):
            n = P if i < NT else NS
            if residual:
                dve.wait_ge(s["mix_mm"], nth(l, "mix_mm", i + 1))
                xr = m.x[0:n, i, :].rearrange("p (h d) -> p h d", h=2)
                stt(xr, xr, ALPHA, ps[0:n, 2 * (i % 2):2 * (i % 2) + 2, :], mul, add)
                dve.drain()
            else:
                dve.wait_ge((s["yg0_in"], s["yg1_in"], s["yg2_in"], s["yg3_in"], s["yg4_in"])[i], nth(l, f"yg{i}_in", 32))
                for k, gate in enumerate((m.gate_hi, m.gate_lo)):
                    stt(m.x[0:n, i, :], m.yg[0:n, i, k, :], gate[0:n, i:i + 1], m.x[0:n, i, :], mul, add)
                    dve.drain()
            for h in range(2):
                dve.bn_stats(m.bn[i % 2][0:n, h, :], m.x[0:n, i, 512 * h:512 * h + 512])
            dve.drain()
            dve.bn_aggr(m.mv[i % 2][0:n], m.bn[i % 2][0:n]).then_inc(s["ln_var"], 1)

        def scale(i):
            n = P if i < NT else NS
            dve.wait_ge(s["ln_std"], nth(l, "ln_std", first + i + 1))
            dve.reciprocal(m.std[i % 2][0:n], m.std[i % 2][0:n])
            dve.drain()
            ts(m.x[0:n, i, :], m.x[0:n, i, :], m.mv[i % 2][0:n, 0:1], m.std[i % 2][0:n], sub, mul).then_inc(s["ln_mid"], 1)

        stats(0)
        for i in range(1, 5):
            stats(i)
            scale(i - 1)
            dve.drain()
        scale(4)

    def router(l):
        G, S_, (a, b, c) = m.gsel, m.gsig, m.g16
        g0, g1, g2, g3 = m.g4
        tt(G, S_, m.router_bias.unsqueeze(1).broadcast_to([P, 5, NEXP]), add)
        dve.drain()
        G4 = G.rearrange("p i (g e) -> p i g e", e=4)
        lo, hi = [G4[:, :, :, k] for k in (0, 2)], [G4[:, :, :, k] for k in (1, 3)]
        tt(g0, lo[0], hi[0], ALU.max)
        tt(g1, lo[0], hi[0], ALU.min)
        tt(g2, lo[1], hi[1], ALU.max)
        tt(g3, lo[1], hi[1], ALU.min)
        dve.drain()
        tt(g1, g1, g3, ALU.max)
        dve.drain()
        tt(g3, g0, g2, ALU.min)
        dve.drain()
        tt(g0, g0, g2, ALU.max)
        dve.drain()
        tt(g1, g1, g3, ALU.max)
        dve.drain()
        tt(g0, g0, g1, add)
        dve.drain()

        def first_best(value, order, scratch, best):
            w = value.shape[2]
            dve.tensor_reduce(best, value, AX.X, ALU.max)
            dve.drain()
            tt(scratch, value, best.unsqueeze(2).broadcast_to([P, 5, w]), ALU.is_equal)
            dve.drain()
            tt(scratch, scratch, m.const(order).unsqueeze(1).broadcast_to([P, 5, w]), mul)
            dve.drain()
            dve.tensor_reduce(best, scratch, AX.X, ALU.max)
            dve.drain()
            tt(scratch, m.const(order).unsqueeze(1).broadcast_to([P, 5, w]), best.unsqueeze(2).broadcast_to([P, 5, w]),
               ALU.is_equal)
            dve.drain()

        first_best(g0, "group_order", g1, m.g1[0])
        ts(g1, g1, 1.0, -NEG, sub, mul)
        dve.drain()
        tt(G4, G4, g1.unsqueeze(3).broadcast_to([P, 5, 4, 4]), add)
        dve.drain()
        first_best(G, "expert_order", a, m.g1[0])
        stt(G, a, NEG, G, mul, add)
        dve.drain()
        first_best(G, "expert_order", b, m.g1[0])
        tt(a, a, b, add)
        ts(m.before, m.const("causal"), 0.0, None, ALU.is_lt)
        dve.memset(m.all1, 1.0)
        dve.drain()
        dve.tensor_copy(m.chosen, a)
        dve.drain().then_inc(s["chosen"], 1)
        tt(a, a, S_, mul)
        dve.drain()
        dve.tensor_reduce(m.g1[1], a, AX.X, add)
        dve.drain()
        dve.reciprocal(m.g1[2], m.g1[1])
        dve.drain()
        tt(m.gates, a, m.g1[2].unsqueeze(2).broadcast_to([P, 5, NEXP]), mul)

    def dispatch(l):
        order = m.const("expert_order")
        dve.wait_ge(s["slots_mm"], nth(l, "slots_mm", 1))
        pos = ps[:, 6, 0:5 * NEXP].rearrange("p (i e) -> p i e", e=NEXP)
        total = ps[:, 6, 5 * NEXP:6 * NEXP]
        ts(m.extra, total, float(P), None, ALU.is_gt)
        for k in range(2, -(-T // P)):
            dve.drain()
            stt(m.extra, total, float(P * k), m.extra, ALU.is_gt, add)
        dve.drain()
        dve.tensor_tensor_scan(m.extra_sum, m.const("ones").broadcast_to([P, NEXP]), m.extra, 0.0, mul, add)
        ts(m.own, order, -float(P), float(P * NEXP), mul, add)
        dve.drain()
        tt(m.shift_to, m.extra_sum, m.extra, sub)
        dve.drain()
        ts(m.shift_to, m.shift_to, float(NEXP - 1), float(P), add, mul)
        dve.drain()
        tt(m.shift_to, m.shift_to, m.own, sub)
        ts(m.slot, pos, float(P), None, ALU.is_ge)
        dve.drain()
        tt(m.slot, m.slot, m.shift_to.unsqueeze(1).broadcast_to([P, 5, NEXP]), mul)
        dve.drain()
        tt(m.slot, m.slot, pos, add)
        dve.drain()
        tt(m.slot, m.slot, m.own.unsqueeze(1).broadcast_to([P, 5, NEXP]), add)
        dve.drain()
        stt(m.slot, m.slot, 1.0, m.chosen, add, mul)
        dve.drain()
        dve.tensor_reduce(m.hi, m.slot, AX.X, ALU.max)
        dve.tensor_reduce(m.lo, m.slot, AX.X, add)
        dve.drain()
        tt(m.lo, m.lo, m.hi, sub)
        tt(m.hot_hi, m.slot, m.hi.unsqueeze(2).broadcast_to([P, 5, NEXP]), ALU.is_equal)
        dve.drain()
        tt(m.hot_lo, m.slot, m.lo.unsqueeze(2).broadcast_to([P, 5, NEXP]), ALU.is_equal)
        tt(m.hot_hi, m.hot_hi, m.gates, mul)
        ts(m.slots[:, 0, :], m.hi, -1.0, None, add)
        ts(m.slots[:, 1, :], m.lo, -1.0, None, add)
        dve.drain()
        tt(m.hot_lo, m.hot_lo, m.gates, mul)
        dve.tensor_reduce(m.gate_hi, m.hot_hi, AX.X, add)
        tt(m.beyond[0:1], m.extra_sum[0:1].unsqueeze(1).broadcast_to([1, 8, NEXP]),
           order[0:1, 0:8].unsqueeze(2).broadcast_to([1, 8, NEXP]), add)
        dve.drain()
        dve.tensor_reduce(m.gate_lo, m.hot_lo, AX.X, add)
        ts(m.beyond[0:1], m.beyond[0:1], float(NEXP), None, ALU.is_le)
        dve.drain()
        dve.tensor_reduce(m.count[0:1], m.beyond[0:1], AX.X, add)
        dve.drain()
        ts(m.extra_expert, m.count[0:1], float(NEXP - 1), None, ALU.min)
        dve.drain().then_inc(s["idx_ready"], 1)

    def experts(l):
        dve.wait_ge(s["router_sig"], nth(l, "router_sig", 1))
        router(l)
        dispatch(l)
        dve.wait_ge(s["x_scattered"], nth(l, "x_scattered", 160))
        dve.wait_ge(s["xt_mm"], nth(l, "xt_mm", 5))
        for i in range(5):
            n = P if i < NT else NS
            ts(m.x[0:n, i, :], m.x[0:n, i, :], ALPHA, None, mul)

        def hidden(e, k):
            dve.wait_ge(s["silu_done"], nth(l, "silu_done", e * 2 + (k + 1)))
            tt(m.h, m.silu, ps[:, 3, DEXP:2 * DEXP], mul).then_inc(s["h_ready"], 1)

        def hidden_columns(e, k):
            dve.wait_ge(s["ht_mm"], nth(l, "ht_mm", e * 2 + (k + 1)))
            dve.tensor_copy(m.hT.rearrange("p f n -> p (f n)"), ps[:, 2, 0:DEXP]).then_inc(s["ht_copied"], 1)

        def rows_back(e, k):
            dve.wait_ge((s["y0_stored"], s["y1_stored"])[k], nth(l, f"y{k}_stored", e * 16))
            dve.wait_ge(s["down_mm"], nth(l, "down_mm", e * 2 + (k + 1)))
            dve.tensor_copy(m.y[k][:, 512:DM], ps[:, 6, :]).then_inc(s["y_copied_v"], 1)

        hidden(0, 0)
        with dve.Fori(0, BLOCKS // 2 - 1) as e:
            for k in range(2):
                hidden_columns(e, k)
                rows_back(e, k)
                hidden(e + k, 1 - k)
        e = BLOCKS // 2 - 1
        hidden_columns(e, 0)
        rows_back(e, 0)
        hidden(e, 1)
        hidden_columns(e, 1)
        rows_back(e, 1)

    dve.memset(m.A[:, NT, :], 0.0)
    dve.memset(m.gsig[:, NT, :], 1.0)
    dve.drain().then_inc(s["zeroed"], 1)
    for name in ("h_ready", "ht_copied", "y_copied_v"):
        dve.drain().then_inc(s[name], 1)
    dve.wait_ge(s["const_in"], 64)
    dve.wait_ge(s["x_in"], 48)
    with dve.Fori(0, DEPTH) as l:
        dve.wait_ge(s["params_in"], nth(l, "params_in", 16))
        softplus(l)
        row_stage(l)
        columns(l)
        column_math(l)
        rwkv_loop(l)
        rwkv_sample(l)
        rwkv_out(l)
        attention(l)
        norm(l, 0, True)
        experts(l)
        norm(l, 5, False)


def kernel(x_prompt, x_sample, cache_k, cache_v, cache_ik, page_table, state_rwkv, state_rwkv_shift,
           state_conv_c, state_conv_d, state_lru, w_in, w_out, idx_ln_g, idx_ln_b, rwkv_mu, rwkv_w0,
           rwkv_w2, rwkv_a0, rwkv_a2, rwkv_g2, rwkv_kk, rwkv_ka, rwkv_rk, rwkv_lnx_g, rwkv_lnx_b,
           convc_w, convd_w, convd_b, lru_gx_w, lru_gx_b, lru_ga_w, lru_ga_b, lru_lam,
           ln1_g, ln1_b, ln2_g, ln2_b, w_router, router_bias, moe_w_gate, moe_w_up, moe_w_down):
    import concourse.bacc as bacc
    from concourse.bass_utils import run_bass_kernel_spmd

    def arr(a):
        return np.asarray(a)

    L = DEPTH
    xs = arr(x_sample).reshape(NS, DM)
    xp = arr(x_prompt).reshape(SEQ, DM)
    w_in, w_out = arr(w_in), arr(w_out)

    def by_rows(w):
        *lead, k, n = w.shape
        return np.moveaxis(w.reshape(*lead, k // P, P, n), -3, -2)

    b0, c0, d0 = ACOLS, ACOLS + 896, ACOLS + 896 + 768
    starts = [b0 + P * n for n in range(7)]
    for j in range(2):
        starts += [c0 + WA + P * j, c0 + 2 * WA + P * j, c0 + P * j]
    for j in range(2):
        starts += [d0 + P * j, d0 + WA + P * j]
    wf = np.stack([w_in[:, :, a:a + P] for a in starts], 1)
    gu = np.stack([by_rows(arr(moe_w_gate)), by_rows(arr(moe_w_up))], -2)

    params = np.zeros((L, P, PARAM_W), np.float32)

    def put(name, a, rows=slice(0, P)):
        at, w = PARAM[name]
        params[:, rows, at:at + w] = a.reshape(L, -1, w)

    def cols(a, n=2):
        return np.moveaxis(arr(a).reshape(L, n, P), 1, 2)

    put("mu", cols(rwkv_mu, 7))
    for name, a in (("w0", rwkv_w0), ("a0", rwkv_a0), ("kkw", rwkv_kk), ("ka", rwkv_ka), ("rk", arr(rwkv_rk).reshape(L, WA)),
                    ("lnxg", rwkv_lnx_g), ("lnxb", rwkv_lnx_b), ("db", convd_b), ("gxb", lru_gx_b), ("gab", lru_ga_b),
                    ("lam", lru_lam)):
        put(name, cols(a))
    put("cw", arr(convc_w).reshape(L, 3, 2, P).transpose(0, 3, 2, 1))
    put("dw", arr(convd_w).reshape(L, 4, 2, P).transpose(0, 3, 2, 1))
    put("shift", arr(state_rwkv_shift).reshape(L, DB, 7, P).transpose(0, 3, 2, 1))
    put("convc", arr(state_conv_c).reshape(L, DB, 2, 2, P).transpose(0, 4, 3, 1, 2))
    put("convd", arr(state_conv_d).reshape(L, DB, 3, 2, P).transpose(0, 4, 3, 1, 2))
    put("lru", arr(state_lru).reshape(L, DB, 2, P).transpose(0, 3, 2, 1))
    put("lora", np.concatenate([arr(rwkv_w2), arr(rwkv_a2), arr(rwkv_g2)], 1))
    for name, w in (("gxw", lru_gx_w), ("gaw", lru_ga_w)):
        g = np.zeros((L, P, 2, P), np.float32)
        for h in range(4):
            q = slice(64 * (h % 2), 64 * (h % 2) + 64)
            g[:, q, h // 2, q] = arr(w)[:, h]
        put(name, g)
    put("idxg", np.repeat(arr(idx_ln_g)[:, None], P, 1))
    put("idxb", np.repeat(arr(idx_ln_b)[:, None], P, 1))

    table = arr(page_table)
    arrays = {
        "consts": constants(),
        "page_table": table.reshape(1, DB * NPAGE).astype(np.int32),
        "xT": np.concatenate([xp, xs]).T.reshape(KC, P, T).transpose(1, 0, 2),
        "x_prompt": xp, "x_sample": xs,
        "w_router": by_rows(arr(w_router)), "router_bias": arr(router_bias),
        "wa": by_rows(w_in[:, :, 0:ACOLS]),
        "wf": by_rows(wf).reshape(L * NCH, P, KC, P),
        "wout": by_rows(w_out),
        "params": params,
        "ln": np.stack([np.stack([arr(ln1_g), arr(ln1_b)], 1), np.stack([arr(ln2_g), arr(ln2_b)], 1)], 1).reshape(2 * L, 2, DM),
        "state_rwkv": arr(state_rwkv).transpose(0, 2, 4, 1, 3).reshape(L, WA, DB, 64),
        "cache_k": arr(cache_k).reshape(L * NPHYS, PAGE, 2, P).transpose(0, 3, 2, 1),
        "cache_v": arr(cache_v).reshape(L * NPHYS, PAGE, WA),
        "cache_ik": arr(cache_ik).reshape(L * NPHYS, PAGE, 32).transpose(0, 2, 1),
        "w_gu": gu.reshape(L * NEXP, P, KC, 2, DEXP),
        "w_dn": by_rows(arr(moe_w_down)).reshape(L * NEXP, P, 2, DM),
    }
    outs = {
        "y_p": (SEQ, DM), "y_s": (NS, DM), "k_p": (L, SEQ, WA), "v_p": (L, SEQ, WA), "ik_p": (L, SEQ, 32),
        "k_s": (L, NS, WA), "v_s": (L, NS, WA), "ik_s": (L, NS, 32), "small": (L, P, SMALL_W),
        "state_p": (L, WA, 64), "state_s": (L, WA, DB, 64),
    }
    nc = bacc.Bacc("TRN2", target_bir_lowering=False, num_devices=1)
    arrays = {k: np.ascontiguousarray(a) for k, a in arrays.items()}
    din = {k: nc.dram_tensor("in_" + k, a.shape, mybir.dt.from_np(a.dtype), kind="ExternalInput").ap()
           for k, a in arrays.items()}
    dout = {k: nc.dram_tensor("out_" + k, shape, F32, kind="ExternalOutput").ap() for k, shape in outs.items()}
    program(nc, din, dout)
    r = run_bass_kernel_spmd(nc, [{"in_" + k: a for k, a in arrays.items()}], core_ids=[0]).results[0]
    o = {k: np.asarray(r["out_" + k]) for k in outs}

    def piece(name, n):
        at, w = SMALL[name]
        return o["small"][:, :, at:at + w].reshape(L, P, n, w // n)

    shift = piece("shift", 7)
    shift = shift.transpose(0, 3, 2, 1).reshape(L, 9, 1, 896)
    cc = piece("convc", 2).transpose(0, 3, 2, 1).reshape(L, 18, WA)
    cd = piece("convd", 2).transpose(0, 3, 2, 1).reshape(L, 27, WA)
    lru = piece("lru", 2).transpose(0, 3, 2, 1).reshape(L, 9, WA)
    sp = o["state_p"].reshape(L, 1, 4, 64, 64).transpose(0, 1, 2, 4, 3)
    ss = o["state_s"].reshape(L, 4, 64, DB, 64).transpose(0, 3, 1, 4, 2)
    return (
        o["y_p"].reshape(1, SEQ, DM), o["y_s"].reshape(DB, DS, DM),
        o["k_p"].reshape(L, 1, SEQ, 4, 64), o["v_p"].reshape(L, 1, SEQ, 4, 64), o["ik_p"].reshape(L, 1, SEQ, 32),
        sp, shift[:, 0:1], cc[:, 0:2].reshape(L, 1, 2, WA), cd[:, 0:3].reshape(L, 1, 3, WA), lru[:, 0:1],
        o["k_s"].reshape(L, DB, DS, 4, 64), o["v_s"].reshape(L, DB, DS, 4, 64), o["ik_s"].reshape(L, DB, DS, 32),
        ss, shift[:, 1:], cc[:, 2:].reshape(L, DB, 2, WA), cd[:, 3:].reshape(L, DB, 3, WA), lru[:, 1:],
    )
```

```python
from contextlib import ExitStack

import numpy as np

import concourse.bass as bass
from concourse import mybir

F32 = mybir.dt.float32
I32 = mybir.dt.int32
ALU = mybir.AluOpType
ACT = mybir.ActivationFunctionType
AX = mybir.AxisListType

DM = 1024
SEQ = 512
DEPTH = 2
DB, DS = 8, 4
PAST, PAGE = 512, 128
NPAGE = PAST // PAGE
NPHYS = 5 * DB * NPAGE // 4
NS = DB * DS
T = SEQ + NS
TP = SEQ + 64
P = 128
KC = DM // P
NT = SEQ // P
WA = 256
ACOLS = 932
C_QI, C_KI, C_WI = 768, 896, 928
NCH = 17
TOPK_P, TOPK_S = 128, 129
CH = 64
NEXP, DEXP = 16, 256
BLOCKS = NEXP + 2 * T // P
ALPHA = (2 * DEPTH) ** 0.25
DECAY = float(np.exp(-0.5))
NEG = -1e30
GELU_C = float(np.sqrt(2.0 / np.pi))


def offsets(spec):
    at, out = 0, {}
    for name, width in spec:
        out[name] = (at, width)
        at += width
    return out, at


CONST, CONST_W = offsets([
    ("ident", 128), ("causal", 128), ("ones_head", 128),
    ("strict_near", 128), ("strict_near_t", 128), ("strict_far", 128), ("strict", 128), ("incl", 64),
    ("s_strict", 128), ("s_strict_t", 128), ("s_incl", 64), ("s_rows", 8), ("spread", 256),
    ("new_bias", 32), ("cos_q", 40), ("sin_q", 40), ("cos_i", 20), ("sin_i", 20), ("reset", TP),
    ("ones", 1), ("group_order", 4), ("expert_order", 16), ("eps", 2),
])

PARAM, PARAM_W = offsets([
    ("mu", 7), ("w0", 2), ("a0", 2), ("kkw", 2), ("ka", 2), ("rk", 2), ("lnxg", 2), ("lnxb", 2),
    ("cw", 6), ("dw", 8), ("db", 2), ("gxb", 2), ("gab", 2), ("lam", 2),
    ("shift", 56), ("convc", 32), ("convd", 48), ("lru", 16),
    ("lora", 256), ("gxw", 256), ("gaw", 256), ("idxg", 32), ("idxb", 32),
])

SMALL, SMALL_W = offsets([("shift", 63), ("convc", 36), ("convd", 54), ("lru", 18)])


def constants():
    c = np.zeros((P, CONST_W), np.float32)

    def put(name, a):
        at, w = CONST[name]
        a = np.asarray(a, np.float32)
        c[:a.shape[0], at:at + w] = a.reshape(a.shape[0], w)

    i = np.arange(P)
    put("ident", np.eye(P))
    put("causal", np.where(i[None] <= i[:, None], 0.0, NEG))
    put("ones_head", (i[:, None] // 64 == i[None] // 64))
    s, t, same = i[:, None] % 64, i[None] % 64, i[:, None] // 64 == i[None] // 64
    near = (s < t) & same & (s // 16 == t // 16)
    far = (s < t) & same & (s // 16 != t // 16)
    put("strict_near", near)
    put("strict_near_t", near.T)
    put("strict_far", far)
    put("strict", (s < t) & same)
    tc = np.arange(64)[None]
    put("incl", i[:, None] % 64 <= tc)
    ss = (s < t) & same & (s // DS == t // DS) & (s < NS) & (t < NS)
    put("s_strict", ss)
    put("s_strict_t", ss.T)
    put("s_incl", (i[:, None] % 64 <= tc) & (i[:, None] % 64 // DS == tc // DS) & (i[:, None] % 64 < NS) & (tc < NS))
    put("s_rows", (i[:, None] % 64) // DS == np.arange(8)[None])
    spread = np.zeros((NS, 2, P), np.float32)
    for g in range(2):
        for j in range(4):
            for h in range(4):
                for q in range(DS):
                    spread[(4 * g + j) * DS + q, g, 32 * j + h * DS + q] = 1.0
    put("spread", spread)
    a = np.arange(NS)
    put("new_bias", np.where((a[None] // DS == a[:, None] // DS) & (a[None] % DS <= a[:, None] % DS), 0.0, NEG))
    pos = np.zeros((5 * P,), np.float32)
    pos[:SEQ] = np.arange(SEQ)
    pos[SEQ:T] = PAST + a % DS
    for name, half in (("q", 8), ("i", 4)):
        freq = (np.float32(500000.0) ** (-np.arange(half, dtype=np.float32) / np.float32(half))).astype(np.float32)
        ang = pos[:, None] * freq[None]
        put("cos_" + name, np.cos(ang).reshape(5, P, half).transpose(1, 0, 2))
        put("sin_" + name, np.sin(ang).reshape(5, P, half).transpose(1, 0, 2))
    reset = np.ones(TP, np.float32)
    reset[0:SEQ:CH] = 0
    reset[SEQ:T:DS] = 0
    reset[T:] = 0
    put("reset", np.broadcast_to(reset, (P, TP)))
    put("ones", np.ones((P, 1)))
    put("group_order", np.broadcast_to(4.0 - np.arange(4), (P, 4)))
    put("expert_order", np.broadcast_to(16.0 - np.arange(16), (P, 16)))
    put("eps", np.broadcast_to(np.array([1e-5, 64e-5], np.float32), (P, 2)))
    return c


RW_PE, RW_DVE, RW_ACT = 34, 23, 11
PER_LAYER = dict(
    params_in=16, wa_in=16, wf0_in=96, wf1_in=96, wf2_in=80, ln_in=32,
    ik_in=16 * DB * NPAGE, k0_in=8 * DB * NPAGE, k1_in=8 * DB * NPAGE, v0_in=8 * DB * NPAGE, v1_in=8 * DB * NPAGE,
    state_in=64, wout_in=16, moe0_in=16 * BLOCKS, moe1_in=16 * BLOCKS,
    rows_mm=10, rows_copied=10, fm_mm=NCH, fm_copied=NCH, fm_used=NCH, rows_ready=1, rows_stored=96, lora_act=1, ki_var=1, ki_std=1,
    lam_abs=1, lam_exp=1, lam_sum=1, lam_log=1, job_mm=14, job_out=14, conv_done=2, kk_in=1, cum_ready=1, bonus_in=1,
    dz_ready=1, d_tanh=1, gelu_in=1, gelu_tanh=1, om_ready=1, om_sqrt=1, exps_ready=1, states_zeroed=1,
    rwc_v=24, rw_in=4, rw_mm=4 * RW_PE, rw_v=4 * RW_DVE, rw_a=4 * RW_ACT,
    rws_in=1, rws_mm=9, rws_v=9, rws_a=2, yn_in=1, yn_mm=2, yn_std=1, rw_done=1, state_out=128,
    kr_ready=1, tr_mm=6, tr_copied=6, tr_sample=2, idx_mm=3, relu_done=12, rl_used=12,
    lg_mm=4, lg_taken=4, lg_ready=4, p_exp=4, p_ready=4, pt_mm=16, pt_copied=16, pv_mm=4, ya_copied=4,
    s_prep=1, s_idx_mm=1, s_relu=1, s_sums=1, s_tr_mm=1, s_score=1, selected=1, qb_ready=1,
    s_lg_mm=2, s_lg=2, s_max=2, s_exp=2, s_p=2, s_pt_mm=2, s_pt=2, s_pv_mm=2, attn_done=1,
    x_kept=32, x_back=32, small_ready=1, small_out=16,
    mix_mm=5, ln_var=10, ln_std=10, ln_mid=10, ln_done=10, xt_mm=10, xt_copied=10,
    router_mm=1, router_sig=1, chosen=1, slots_mm=1, idx_ready=1, x_scattered=160,
    xg0_in=8 * BLOCKS, xg1_in=8 * BLOCKS, xgt_mm=BLOCKS, xgt_copied=BLOCKS, gu_mm=BLOCKS, silu_done=BLOCKS, h_ready=BLOCKS,
    ht_mm=BLOCKS, ht_copied=BLOCKS, down_mm=BLOCKS, y_copied_a=BLOCKS, y_copied_v=BLOCKS,
    y0_stored=8 * BLOCKS, y1_stored=8 * BLOCKS, yg0_in=32, yg1_in=32, yg2_in=32, yg3_in=32, yg4_in=32,
)
ONCE = ("const_in", "x_in", "zeroed", "zeros_out")


START = dict(mix_mm=1, rw_mm=1, xt_copied=1, h_ready=1, ln_done=5, xgt_copied=1, ht_copied=1,
             y_copied_a=1, y_copied_v=1, y0_stored=1, y1_stored=1, x_kept=1)


def nth(l, name, n):
    return l * PER_LAYER[name] + (n + START.get(name, 0))


ZEROED = 16 * (BLOCKS // 2 + (BLOCKS - NEXP) // 2)
ARENA = 52100


class Map:
    pass


def memory(arena):
    m = Map()
    end = 0

    def region(n):
        nonlocal end
        end += n
        return end - n

    def view(at, *shape):
        n = int(np.prod(shape))
        assert at + n <= ARENA, (at, shape)
        v = arena[:, at:at + n]
        if len(shape) == 1:
            return v
        names = "abcd"[:len(shape)]
        return v.rearrange(f"p ({' '.join(names)}) -> p {' '.join(names)}", **dict(zip(names[1:], shape[1:])))

    C0, WR0, X0, A0 = region(CONST_W), region(KC * NEXP + NEXP), region(5 * DM), region(5 * ACOLS)
    PV0, YT0, LN0, OS0, XT0 = region(PARAM_W), region(8 * T), region(2 * DM), region(SMALL_W), region(8 * T)
    SM0, R1, R2, R4 = region(680), region(8 * DM), region(12288), region(13 * 512)
    assert end <= ARENA, end

    m.consts = view(C0, CONST_W)
    m.const = lambda name: view(C0 + CONST[name][0], CONST[name][1])
    m.param = lambda name: view(PV0 + PARAM[name][0], PARAM[name][1])
    m.small = lambda name: view(OS0 + SMALL[name][0], SMALL[name][1])
    m.params, m.smalls = view(PV0, PARAM_W), view(OS0, SMALL_W)
    m.w_router, m.router_bias = view(WR0, KC, NEXP), view(WR0 + KC * NEXP, NEXP)
    m.x = view(X0, 5, DM)
    m.A = view(A0, 5, ACOLS)
    m.yT = view(YT0, 8, T)
    m.xT = view(XT0, 8, T)
    m.ln = view(LN0, 2, DM)

    st = view(SM0, 680)
    m.nmax, m.ssum, m.rsum = ([st[:, 8 * k + 4 * j:8 * k + 4 * j + 4] for j in range(2)] for k in range(3))
    m.lam = [st[:, 24 + 2 * k:26 + 2 * k] for k in range(8)]
    m.bn, m.mv, m.std = [view(SM0 + 44, 2, 6), view(SM0 + 666, 2, 6)], [st[:, 56:58], st[:, 58:60]], [st[:, 664:665], st[:, 665:666]]
    m.pc = view(SM0 + 60, 2, 2)
    m.kist = [view(SM0 + 64 + 5 * k, 5) for k in range(4)]
    m.gsig, m.gsel, m.gates = (view(SM0 + 84 + 80 * k, 5, NEXP) for k in range(3))
    m.g16 = [view(SM0 + 324 + 80 * k, 5, NEXP) for k in range(3)]
    m.g4 = [view(SM0 + 564 + 20 * k, 5, 4) for k in range(4)]
    m.g1 = [view(SM0 + 644 + 5 * k, 5) for k in range(3)]
    m.omka, m.turn = st[:, 660:662], st[:, 678:679]

    m.wa, m.wout = view(R1, KC, ACOLS), view(R1, KC, DM)
    m.Z = view(R1, 7, TP)
    m.gate, m.bonus, m.yb = (view(R1 + 7 * TP + 2 * TP * k, 2, TP) for k in range(3))
    assert 13 * TP <= 8 * DM
    m.gb = view(R1 + 11 * TP, 2, T)

    FMW = 3 + SEQ + DB * 7
    m.wf = [view(R4 + 1024 * k, KC, P) for k in range(3)]
    fm = [view(R4 + 3072 + FMW * k, FMW) for k in range(4)]
    m.fm_p = [f[:, 0:3 + SEQ] for f in fm]
    m.fm_s = [f[:, 3 + SEQ:FMW].rearrange("p (b t) -> p b t", t=7) for f in fm]
    m.diff = view(R4 + 3072 + 4 * FMW, T)
    m.conv = view(R4 + 3072 + 4 * FMW + T, T)
    m.za_tanh, m.a_lru = view(R4 + 3072, 2, T), view(R4 + 3072 + 2 * T, 2, T)
    m.hs, m.gelu = view(XT0, 2, T), view(XT0 + 2 * T, 2, T)

    m.ea, m.en, m.ec, m.aa, m.nkk, m.kf, m.bv = (view(R2 + 2 * TP * k, 2, TP) for k in range(7))
    D0 = R2 + 14 * TP
    m.xc, m.gx, m.za = (view(D0 + 2 * T * k, 2, T) for k in range(3))
    m.rope_q = [view(R2 + 320 * k, 5, 8, 8) for k in range(4)]
    m.rope_i = [view(R2 + 1280 + 80 * k, 5, 4, 4) for k in range(4)]
    m.ki_c, m.ki_2 = view(R2 + 1600, 5, 32), view(R2 + 1760, 5, 32)

    d = [view(D0 + 512 * k, 4, P) for k in range(8)]
    r = [view(R4 + 512 * k, 4, P) for k in range(13)]
    m.AE, m.BE, m.KE, m.VE, m.BEt, m.KEt, m.VEt, m.Mak = d
    m.D, m.DT, m.E, m.D2, m.D2T, m.D4, m.D4T, m.X, m.XT_, m.FT, m.Zs = r[:11]
    m.attn = view(R4 + 512 * 11, 2, 4, CH)
    m.W, m.U = view(R4 + 512 * 12, 2, P), view(R4 + 512 * 12 + 256, 2, P)
    m.TB = view(XT0, 2, DB, P)
    m.RC, m.Tst = view(XT0 + 4096 - 512, 4, CH), view(XT0 + 4096 - 256, 2, P)
    m.AEb = view(R4 + 512 * 3, 2, DB, P)
    m.UEb = view(R4 + 512 * 8, DB, P)
    m.VEb = view(R4 + 512 * 0, DB, P)
    m.yc, m.y2 = m.ea, m.en

    m.qT, m.kT, m.kiT, m.qiT = view(X0, 2, T), view(X0 + 2 * T, 2, T), view(X0 + 4 * T, T), view(X0 + 5 * T, T)
    m.QB = view(X0 + 4 * T, 2, DB, 32)
    m.chain_at, m.chain_w = (0, 512, 896, 1152), (512, 384, 256, T)
    CW = 1152 + T
    m.bias, m.score, m.work, m.eq, m.pre = (
        [view(at + a, w) for a, w in zip(m.chain_at, m.chain_w)] for at in (X0 + 6 * T, R2, R2 + CW, R2 + 2 * CW, R2 + 3 * CW))
    m.top8, m.cnt = [view(R2 + 12224 + 8 * k, 8) for k in range(4)], [view(R2 + 12256 + 2 * k, 2) for k in range(4)]
    m.KR, m.wb_in = view(R2 + 3 * CW, 5, P), view(R2 + 3 * CW + 640, 4, P)
    m.sums = view(R2 + 2 * CW, 4, 32)
    m.relu = [view(R2 + 4 * CW + 512 * k, 512) for k in range(2)]
    m.relu_n, m.WB = view(R2 + 4 * CW + 1024, 4, 32), view(R2 + 4 * CW + 1152, DB, 4, DS)
    m.QI, m.ik = view(R2 + 11168, 2, 4, DS), view(R2 + 11200, 2, PAST)
    m.lg, m.pT = ([view(R1 + at + 2048 * k, 4, PAST) for k in range(2)] for at in (0, 4096))
    m.s_lg, m.s_pT = ([view(R4 + at + w * k, w) for k in range(2)] for at, w in ((0, T), (2 * T, PAST)))
    m.s_pTn = [view(R4 + 2 * T + 2 * PAST + P * k, P) for k in range(2)]
    m.K = [view(at, 2, 4, PAST) for at in (R2, XT0)]
    m.V = [view(at, 4, NPAGE, WA) for at in (R2 + 4096, R4 + 2560)]

    m.w_gu = [view(R2 + 6144 * k, KC, 2 * DEXP) for k in range(2)]
    m.w_dn = [view(R2 + 6144 * k + 4096, 2, DM) for k in range(2)]
    m.xg, m.y = ([view(R4 + at + DM * k, DM) for k in range(2)] for at in (0, 3840))
    m.xgT, m.silu, m.h, m.hT = view(R4 + 2048, KC, P), view(R4 + 3072, DEXP), view(R4 + 3328, DEXP), view(R4 + 3584, 2, P)
    m.yg = view(R2, 5, 2, DM)
    m.before, m.all1 = view(YT0, P), view(YT0 + P, P)
    m.chosen, m.slot, m.hot_hi, m.hot_lo = (view(YT0 + 256 + 80 * k, 5, NEXP) for k in range(4))
    m.extra, m.extra_sum, m.shift_to, m.own = (view(YT0 + 576 + NEXP * k, NEXP) for k in range(4))
    m.beyond, m.count = view(YT0 + 640, 8, NEXP), view(YT0 + 768, 8)
    m.hi, m.lo, m.gate_hi, m.gate_lo = (view(YT0 + 776 + 5 * k, 5) for k in range(4))
    return m


def program(nc, din, dout):
    with ExitStack() as ctx:
        arena = ctx.enter_context(nc.sbuf_tensor("arena", [P, ARENA], F32))
        pages = ctx.enter_context(nc.sbuf_tensor("pages", [1, DB * NPAGE], I32))
        ints = ctx.enter_context(nc.sbuf_tensor("ints", [P, 19], I32))
        ps = ctx.enter_context(nc.psum_tensor("ps", [P, 8, 512], F32))
        s = {name: ctx.enter_context(nc.semaphore(name)) for name in (*PER_LAYER, *ONCE)}
        m = memory(arena)
        m.pages, m.slots, m.extra_expert = pages, ints[:, 0:10].rearrange("p (k i) -> p k i", k=2), ints[0:1, 10:18]
        m.extra_blocks = ints[0:1, 18:19]
        m.rows_in = nc.dram_tensor("rows_in", (BLOCKS * P, DM), F32, kind="Internal").ap()
        m.rows_out = nc.dram_tensor("rows_out", (BLOCKS * P, DM), F32, kind="Internal").ap()
        block = ctx.enter_context(nc.Block())

        @block.sync
        def _(sp):
            sync_program(sp, s, m, din, dout)

        @block.gpsimd
        def _(pool):
            pool_program(pool, s, m, din, dout)

        @block.tensor
        def _(pe):
            tensor_program(pe, s, m, ps)

        @block.scalar
        def _(act):
            scalar_program(act, s, m, ps, dout)

        @block.vector
        def _(dve):
            vector_program(dve, s, m, ps)


def layer_of(ap, l):
    names = "abcdef"[:len(ap.shape) - 1]
    return ap[bass.ds(l, 1)].rearrange(f"z {' '.join(names)} -> (z {names[0]}) {' '.join(names[1:])}")


def sync_program(sp, s, m, din, dout):
    pages = m.pages
    sp.dma_start(m.consts, din["consts"]).then_inc(s["const_in"], 16)
    sp.dma_start(pages[:, :], din["page_table"]).then_inc(s["const_in"], 16)
    sp.dma_start(m.xT, din["xT"]).then_inc(s["x_in"], 16)
    sp.dma_start(m.w_router, din["w_router"]).then_inc(s["const_in"], 16)
    sp.dma_start(m.router_bias, din["router_bias"].partition_broadcast(P)).then_inc(s["const_in"], 16)
    sp.dma_start(dout["x"][0], din["x"]).then_inc(s["x_in"], 16)
    sp.wait_ge(s["const_in"], 64)

    with sp.Fori(0, DEPTH) as l:
        sp.wait_ge(s["mix_mm"], nth(l, "mix_mm", 0))
        sp.dma_start(m.wa, layer_of(din["wa"], l)).then_inc(s["wa_in"], 16)
        sp.dma_start(m.params, layer_of(din["params"], l)).then_inc(s["params_in"], 16)
        sp.wait_ge(s["ln_done"], nth(l, "ln_done", -4))
        for n in range(NCH):
            if n >= 3:
                sp.wait_ge(s["fm_mm"], nth(l, "fm_mm", n - 2))
            sp.dma_start(m.wf[n % 3], layer_of(din["wf"], l * NCH + n)).then_inc((s["wf0_in"], s["wf1_in"], s["wf2_in"])[n % 3], 16)
            if n == 2:
                for g in range(2):
                    for j in range(4):
                        for c in range(NPAGE):
                            b = (4 * g + j) * NPAGE + c
                            page = sp.value_load(pages[0:1, b:b + 1], min_val=0, max_val=NPHYS - 1)
                            sp.dma_start(m.ik[32 * j:32 * j + 32, g, PAGE * c:PAGE * c + PAGE],
                                         din["cache_ik"][bass.ds(l * NPHYS + page, 1)].rearrange("z d k -> d (z k)"))\
                                .then_inc(s["ik_in"], 16)
        sp.wait_ge(s["states_zeroed"], nth(l, "states_zeroed", 1))
        for q in range(2):
            for h in range(2):
                rows = slice(64 * h, 64 * h + 64)
                sp.dma_start(m.TB[rows, q, :, rows], layer_of(din["state_rwkv"], l)[64 * (2 * q + h):64 * (2 * q + h) + 64])\
                    .then_inc(s["state_in"], 16)
        sp.wait_ge(s["zeros_out"], ZEROED)
        sp.wait_ge(s["ln_done"], nth(l, "ln_done", 0))
        sp.dma_start(m.ln, layer_of(din["ln"], l * 2).partition_broadcast(P)).then_inc(s["ln_in"], 16)
        sp.wait_ge(s["rw_done"], nth(l, "rw_done", 1))
        for q in range(2):
            for h in range(2):
                rows = slice(64 * h, 64 * h + 64)
                n = 64 * (2 * q + h)
                sp.dma_start(layer_of(dout["state_p"], l)[n:n + 64], m.Tst[rows, q, rows]).then_inc(s["state_out"], 16)
                sp.dma_start(layer_of(dout["state_s"], l)[n:n + 64], m.TB[rows, q, :, rows]).then_inc(s["state_out"], 16)
        for g in range(2):
            with sp.Fori(0, 4) as j:
                for c in range(NPAGE):
                    page = sp.value_load(pages[0:1, bass.ds(j * NPAGE + (16 * g + c), 1)], min_val=0, max_val=NPHYS - 1)
                    if g and c == 0:
                        sp.wait_ge(s["state_out"], nth(l, "state_out", 128))
                    sp.dma_start(m.K[g][:, :, bass.ds(j, 1), PAGE * c:PAGE * c + PAGE],
                                 din["cache_k"][bass.ds(l * NPHYS + page, 1)].rearrange("z p q k -> p q z k"))\
                        .then_inc((s["k0_in"], s["k1_in"])[g], 16)
        sp.wait_ge(s["pv_mm"], nth(l, "pv_mm", 4))
        sp.dma_start(m.wout, layer_of(din["wout"], l)).then_inc(s["wout_in"], 16)

        def block_weights(k, expert, moe_in):
            sp.dma_start(m.w_gu[k], layer_of(din["w_gu"], l * NEXP + expert)).then_inc(moe_in, 16)
            sp.dma_start(m.w_dn[k], layer_of(din["w_dn"], l * NEXP + expert)).then_inc(moe_in, 16)

        def block_rows(k, block, xg_in):
            sp.dma_start(m.xg[k], m.rows_in.rearrange("(n p) d -> p n d", p=P)[:, bass.ds(block, 1), :]
                         .rearrange("p n d -> p (n d)")).then_inc(xg_in, 16)

        sp.wait_ge(s["attn_done"], nth(l, "attn_done", 1))
        sp.dma_start(m.x[:, 0:NT, :], layer_of(dout["x"], l)[0:SEQ].rearrange("(i p) d -> p i d", p=P)).then_inc(s["x_back"], 16)
        sp.dma_start(m.x[0:NS, NT, :], layer_of(dout["x"], l)[SEQ:T]).then_inc(s["x_back"], 16)
        for k, moe_in in enumerate((s["moe0_in"], s["moe1_in"])):
            block_weights(k, k, moe_in)
        sp.wait_ge(s["x_scattered"], nth(l, "x_scattered", 160))
        for k, xg_in in enumerate((s["xg0_in"], s["xg1_in"])):
            block_rows(k, k, xg_in)
        with sp.Fori(1, NEXP // 2) as e:
            for k, (moe_in, xg_in) in enumerate(((s["moe0_in"], s["xg0_in"]), (s["moe1_in"], s["xg1_in"]))):
                sp.wait_ge(s["down_mm"], nth(l, "down_mm", e * 2 + (k - 1)))
                block_rows(k, e * 2 + k, xg_in)
                block_weights(k, e * 2 + k, moe_in)
        extra = sp.value_load(m.extra_blocks, min_val=0, max_val=BLOCKS - NEXP)
        with sp.Fori(0, (BLOCKS - NEXP) // 2) as e:
            with sp.If(extra > e * 2):
                for k, (moe_in, xg_in) in enumerate(((s["moe0_in"], s["xg0_in"]), (s["moe1_in"], s["xg1_in"]))):
                    expert = sp.value_load(m.extra_expert[0:1, bass.ds(e * 2 + k, 1)], min_val=0, max_val=NEXP - 1)
                    sp.wait_ge(s["down_mm"], nth(l, "down_mm", e * 2 + (NEXP + k - 1)))
                    block_rows(k, e * 2 + (NEXP + k), xg_in)
                    block_weights(k, expert, moe_in)
            with sp.If(extra <= e * 2):
                sp.wait_ge(s["down_mm"], nth(l, "down_mm", e * 2 + NEXP)).then_inc(s["xg0_in"], 16)
                sp.drain().then_inc(s["xg1_in"], 16)
                sp.drain().then_inc(s["moe0_in"], 32)
                sp.drain().then_inc(s["moe1_in"], 32)
        sp.wait_ge(s["ln_done"], nth(l, "ln_done", 5))
        sp.dma_start(m.ln, layer_of(din["ln"], l * 2 + 1).partition_broadcast(P)).then_inc(s["ln_in"], 16)


def pool_program(pool, s, m, din, dout):
    def add_bias(l, first):
        pool.wait_ge(s["ln_in"], nth(l, "ln_in", 16 + 16 * (first > 0)))
        for i in range(5):
            n = P if i < NT else NS
            pool.wait_ge(s["ln_mid"], nth(l, "ln_mid", first + i + 1))
            pool.tensor_tensor(m.x[0:n, i, :], m.x[0:n, i, :], m.ln[0:n, 1, :], ALU.add).then_inc(s["ln_done"], 1)

    for _ in range(5):
        pool.drain().then_inc(s["ln_done"], 1)
    pool.memset(m.ln, 0.0)
    pool.drain()
    pool.wait_ge(s["rows_mm"], 10)
    for n in range(BLOCKS // 2):
        pool.dma_start(m.rows_in.rearrange("(n p) d -> p n d", p=P)[:, 2 * n:2 * n + 2, :], m.ln).then_inc(s["zeros_out"], 16)
    for n in range(NEXP // 2, BLOCKS // 2):
        pool.dma_start(m.rows_out.rearrange("(n p) d -> p n d", p=P)[:, 2 * n:2 * n + 2, :], m.ln).then_inc(s["zeros_out"], 16)
    with pool.Fori(0, DEPTH) as l:
        pool.wait_ge(s["rows_ready"], nth(l, "rows_ready", 1))
        for name, a, w in (("k", WA, WA), ("v", 2 * WA, WA), ("ik", C_KI, 32)):
            pool.dma_start(layer_of(dout[name + "_p"], l).rearrange("(i p) f -> p i f", p=P), m.A[:, 0:NT, a:a + w])\
                .then_inc(s["rows_stored"], 16)
            pool.dma_start(layer_of(dout[name + "_s"], l), m.A[0:NS, NT, a:a + w]).then_inc(s["rows_stored"], 16)
        pool.wait_ge(s["small_ready"], nth(l, "small_ready", 1))
        pool.dma_start(layer_of(dout["small"], l), m.smalls).then_inc(s["small_out"], 16)
        pool.wait_ge(s["rw_done"], nth(l, "rw_done", 1))
        pool.tensor_tensor(m.turn, m.const("ones"), m.const("ones"), ALU.add)
        pool.drain()
        for g in range(2):
            with pool.Fori(0, 4) as j:
                for c in range(NPAGE):
                    page = pool.value_load(m.pages[0:1, bass.ds(j * NPAGE + (16 * g + c), 1)], min_val=0, max_val=NPHYS - 1)
                    pool.dma_start(m.V[g][:, bass.ds(j, 1), c, :],
                                   din["cache_v"][bass.ds(l * NPHYS + page, 1)].rearrange("z k f -> k z f"))\
                        .then_inc((s["v0_in"], s["v1_in"])[g], 16)
        add_bias(l, 0)
        pool.wait_ge(s["zeros_out"], ZEROED)
        pool.wait_ge(s["idx_ready"], nth(l, "idx_ready", 1))
        pool.tensor_tensor(m.turn, m.const("ones"), m.const("ones"), ALU.add)
        pool.drain()
        for i in range(5):
            n = P if i < NT else NS
            for k in range(2):
                pool.indirect_dma_start(m.rows_in, bass.IndirectOffsetOnAxis(ap=m.slots[0:n, k, i:i + 1], axis=0),
                                        m.x[0:n, i, :], None).then_inc(s["x_scattered"], 16)
        pool.wait_ge(s["y0_stored"], nth(l, "y0_stored", 8 * BLOCKS))
        pool.wait_ge(s["y1_stored"], nth(l, "y1_stored", 8 * BLOCKS))
        pool.tensor_tensor(m.turn, m.const("ones"), m.const("ones"), ALU.add)
        pool.drain()
        for i, yg_in in enumerate((s["yg0_in"], s["yg1_in"], s["yg2_in"], s["yg3_in"], s["yg4_in"])):
            n = P if i < NT else NS
            for k in range(2):
                pool.indirect_dma_start(m.yg[0:n, i, k, :], None, m.rows_out,
                                        bass.IndirectOffsetOnAxis(ap=m.slots[0:n, k, i:i + 1], axis=0)).then_inc(yg_in, 16)
        add_bias(l, 5)
    pool.wait_ge(s["x_kept"], nth(DEPTH, "x_kept", 0))
    pool.wait_ge(s["rows_stored"], nth(DEPTH, "rows_stored", 0))
    pool.wait_ge(s["small_out"], nth(DEPTH, "small_out", 0))
    pool.wait_ge(s["state_out"], nth(DEPTH, "state_out", 0))


def tensor_program(pe, s, m, ps):
    ident = m.const("ident")

    def row_tile(i):
        return slice(i * P, i * P + (P if i < NT else NS))

    def row_projection(l):
        pe.wait_ge(s["wa_in"], nth(l, "wa_in", 16))
        for i in range(5):
            n = P if i < NT else NS
            for h, (a, w) in enumerate(((0, 512), (512, ACOLS - 512))):
                k = 2 * i + h
                if k >= 2:
                    pe.wait_ge(s["rows_copied"], nth(l, "rows_copied", k - 1))
                for c in range(KC):
                    mm = pe.matmul(ps[0:n, k % 2, 0:w], m.xT[:, c, row_tile(i)], m.wa[:, c, a:a + w],
                                   start=c == 0, stop=c == KC - 1)
                mm.then_inc(s["rows_mm"], 1)

    def column_projection(l):
        between = {1: lambda: head_transposes(l, 0), 2: lambda: head_transposes(l, 3), 3: lambda: sample_indexer(l),
                   4: lambda: indexer(l, 3), 5: lambda: indexer(l, 2), 6: lambda: indexer(l, 1), 7: lambda: sample_scores(l)}
        for n in range(NCH):
            pe.wait_ge((s["wf0_in"], s["wf1_in"], s["wf2_in"])[n % 3], nth(l, f"wf{n % 3}_in", 16 * (n // 3 + 1)))
            if n >= 2:
                pe.wait_ge(s["fm_copied"], nth(l, "fm_copied", n - 1))
            for c in range(KC):
                pe.matmul(ps[:, 2 + n % 2, :], m.wf[n % 3][:, c, :], m.xT[:, c, 0:SEQ], start=c == 0, stop=c == KC - 1)
                mm = pe.matmul(ps[:, 4 + n % 2, 0:NS], m.wf[n % 3][:, c, :], m.xT[:, c, SEQ:T],
                               start=c == 0, stop=c == KC - 1)
            mm.then_inc(s["fm_mm"], 1)
            if n in between:
                between[n]()

    def head_transposes(l, first):
        pe.wait_ge(s["kr_ready"], nth(l, "kr_ready", 1))
        srcs = [m.A[:, :, 128 * k:128 * k + 128] for k in range(4)] + [m.A[:, :, C_QI:C_QI + 128], m.KR]
        for b in range(first, first + 3):
            if b >= 3:
                pe.wait_ge(s["tr_copied"], nth(l, "tr_copied", b - 2))
                pe.wait_ge(s["tr_sample"], nth(l, "tr_sample", 1))
            for i in range(NT):
                pe.transpose(ps[:, (6, 7, 0)[b % 3], 128 * i:128 * i + 128], srcs[b][:, i, :], ident)
            mm = pe.transpose(ps[:, 1, NS * b:NS * b + NS], srcs[b][0:NS, NT, :], ident[0:NS, 0:NS])
            mm.then_inc(s["tr_mm"], 1)

    def indexer(l, i):
        if i < 3:
            pe.wait_ge(s["relu_done"], nth(l, "relu_done", 4 * (3 - i)))
        else:
            pe.wait_ge(s["s_relu"], nth(l, "s_relu", 1))
        for h in range(4):
            q = slice(32 * h, 32 * h + 32)
            mm = pe.matmul(ps[:, (6, 7, 0, 1)[h], 0:P * (i + 1)], m.qiT[q, P * i:P * i + P], m.kiT[q, 0:P * (i + 1)],
                           start=True, stop=True)
        mm.then_inc(s["idx_mm"], 1)

    def sample_indexer(l):
        pe.wait_ge(s["s_prep"], nth(l, "s_prep", 1))
        pe.wait_ge(s["ik_in"], nth(l, "ik_in", 16 * DB * NPAGE))
        for h in range(4):
            pe.matmul(ps[:, 7, 256 + NS * h:256 + NS * h + NS], m.wb_in[0:NS, h, :], ident[0:NS, 0:NS], start=True, stop=True)
        for c in range(NPAGE):
            for g in range(2):
                for j in range(4):
                    q, a = slice(32 * j, 32 * j + 32), 16 * (2 * c + g)
                    pe.matmul(ps[:, (7, 0, 1, 6)[j], a:a + 16], m.ik[q, g, P * c:P * c + P], m.QI[q, g, :, :],
                              start=True, stop=True)
        for h in range(4):
            q = slice(32 * h, 32 * h + 32)
            mm = pe.matmul(ps[0:NS, (7, 0, 1, 6)[h], P:P + NS], m.qiT[q, SEQ:T], m.kiT[q, SEQ:T], start=True, stop=True)
        mm.then_inc(s["s_idx_mm"], 1)

    def sample_scores(l):
        pe.wait_ge(s["relu_done"], nth(l, "relu_done", 12))
        pe.wait_ge(s["s_sums"], nth(l, "s_sums", 1))
        for c in range(NPAGE):
            mm = pe.transpose(ps[0:NS, 0, P * c:P * c + P], m.sums[:, c, :], ident)
        mm.then_inc(s["s_tr_mm"], 1)

    def column_jobs(l):
        job = 0

        def product(lhsT, rhs, width):
            nonlocal job
            if job >= 2:
                pe.wait_ge(s["job_out"], nth(l, "job_out", job - 1))
            b = 4 + 2 * (job % 2)
            if job < 2:
                pe.wait_ge(s["fm_copied"], nth(l, "fm_copied", NCH))
            pe.matmul(ps[:, b, :], lhsT, rhs[:, 0:SEQ], start=True, stop=True)
            pe.matmul(ps[:, b + 1, 0:width - SEQ], lhsT, rhs[:, SEQ:width], start=True, stop=True).then_inc(s["job_mm"], 1)
            job += 1

        lora = m.param("lora")
        pe.wait_ge(s["lora_act"], nth(l, "lora_act", 1))
        for w in ("gxw", "gaw"):
            for p in range(2):
                pe.wait_ge(s["conv_done"], nth(l, "conv_done", p + 1))
                product(m.param(w)[:, 128 * p:128 * p + 128], m.xc[:, p, :], T)
        for p in range(2):
            product(lora[64:128, 128 * p:128 * p + 128], m.Z[64:128, 6, :], TP)
        for rows in (slice(0, 32), slice(32, 64)):
            for p in range(2):
                product(lora[rows, 128 * p:128 * p + 128], m.Z[rows, 6, :], TP)
        pe.wait_ge(s["bonus_in"], nth(l, "bonus_in", 1))
        for p in range(2):
            product(m.const("ones_head"), m.bonus[:, p, :], TP)
        pe.wait_ge(s["kk_in"], nth(l, "kk_in", 1))
        for p in range(2):
            product(m.const("ones_head"), m.bv[:, p, :], TP)

    def rwkv_loop(l):
        with pe.Fori(0, 4) as g:
            pe.wait_ge(s["rw_in"], nth(l, "rw_in", g + 1))
            for k in range(4):
                pe.matmul(ps[:, 0, 128 * k:128 * k + 128], m.BE[:, k, :], m.AE[:, k, :], start=True, stop=True)
                pe.matmul(ps[:, 3, 64 * k:64 * k + 64], m.BE[:, k, :], m.RC[:, k, :], start=True, stop=True)
                pe.matmul(ps[:, 2, 128 * k:128 * k + 128], m.KE[:, k, :], m.AE[:, k, :], start=True, stop=True)
                pe.matmul(ps[:, 3, 256 + 64 * k:320 + 64 * k], m.KE[:, k, :], m.RC[:, k, :], start=True, stop=True)
                mm = pe.matmul(ps[:, 1, 128 * k:128 * k + 128], m.AE[:, k, :], m.BE[:, k, :], start=True, stop=True)
            mm.then_inc(s["rw_mm"], 1)
            for b, tile in ((4, m.BE), (5, m.KE), (6, m.VE)):
                for k in range(4):
                    mm = pe.transpose(ps[:, b, 128 * k:128 * k + 128], tile[:, k, :], ident)
            mm.then_inc(s["rw_mm"], 1)

            def two(c, bank, lhsT, rhs):
                for p in range(2):
                    k = 2 * c + p
                    mm = pe.matmul(ps[:, 4 * c + bank, 128 * p:128 * p + 128], lhsT[:, k, :], rhs[:, k, :], start=True, stop=True)
                mm.then_inc(s["rw_mm"], 1)

            pe.wait_ge(s["rw_v"], nth(l, "rw_v", g * RW_DVE + 5))
            for c in range(2):
                if c:
                    pe.wait_ge(s["rw_a"], nth(l, "rw_a", g * RW_ACT + 1))
                two(c, 0, m.DT, m.D)
                two(c, 1, m.D, m.DT)
            for c in range(2):
                pe.wait_ge(s["rw_v"], nth(l, "rw_v", g * RW_DVE + 6 + c))
                pe.wait_ge(s["rw_a"], nth(l, "rw_a", g * RW_ACT + 2 + c))
                two(c, 2, m.D2T, m.D2)
                two(c, 3, m.D2, m.D2T)
            for c in range(2):
                pe.wait_ge(s["rw_v"], nth(l, "rw_v", g * RW_DVE + 8 + c))
                pe.wait_ge(s["rw_a"], nth(l, "rw_a", g * RW_ACT + 4 + c))
                two(c, 0, m.D4T, m.D4)
            for step, lhsT in enumerate((m.D4T, m.D2T, m.DT)):
                for c in range(2):
                    pe.wait_ge(s["rw_v"], nth(l, "rw_v", g * RW_DVE + 10 + 2 * step + c))
                    two(c, 1 + step, lhsT, m.X)
            for c in range(2):
                pe.wait_ge(s["rw_v"], nth(l, "rw_v", g * RW_DVE + 16 + c))
                for p in range(2):
                    mm = pe.transpose(ps[:, 4 * c, 128 * p:128 * p + 128], m.X[:, 2 * c + p, :], ident)
                mm.then_inc(s["rw_mm"], 1)
            for c in range(2):
                pe.wait_ge(s["rw_a"], nth(l, "rw_a", g * RW_ACT + 6 + c))
                two(c, 1, m.E, m.XT_)
            for c in range(2):
                pe.wait_ge(s["rw_a"], nth(l, "rw_a", g * RW_ACT + 8 + c))
                two(c, 2, m.FT, m.X)
            for step in range(2):
                for c in range(2):
                    pe.wait_ge(s["rw_v"], nth(l, "rw_v", g * RW_DVE + 18 + 2 * step + c))
                    two(c, (3, 0)[step], m.FT, m.Zs)
            pe.wait_ge(s["rw_v"], nth(l, "rw_v", g * RW_DVE + 23))
            for c in range(2):
                for p in range(2):
                    k = 2 * c + p
                    o = ps[:, 4, 128 * p:128 * p + 128]
                    pe.matmul(o, m.Mak[:, k, :], m.VEt[:, k, :], start=True, stop=False)
                    mm = pe.matmul(o, m.AE[:, k, :], m.Tst[:, p, :], start=False, stop=True)
                mm.then_inc(s["rw_mm"], 1)
                pe.wait_ge(s["rwc_v"], nth(l, "rwc_v", g * 6 + 3 * c + 1))
                for p in range(2):
                    mm = pe.matmul(ps[:, 5, 128 * p:128 * p + 128], m.Zs[:, 2 * c + p, :], m.W[:, p, :], start=True, stop=True)
                mm.then_inc(s["rw_mm"], 1)
                pe.wait_ge(s["rwc_v"], nth(l, "rwc_v", g * 6 + 3 * c + 2))
                for p in range(2):
                    k = 2 * c + p
                    o = ps[:, 6, 128 * p:128 * p + 128]
                    pe.matmul(o, m.BEt[:, k, :], m.U[:, p, :], start=True, stop=False)
                    pe.matmul(o, m.KEt[:, k, :], m.VEt[:, k, :], start=False, stop=False)
                    pe.matmul(o, ident, m.Tst[:, p, :], start=False, stop=True)
                if c:
                    pe.wait_ge(s["rw_a"], nth(l, "rw_a", g * RW_ACT + 10))
                for p in range(2):
                    k = 2 * c + p
                    o = ps[:, 7, 64 * p:64 * p + 64]
                    pe.matmul(o, m.VEt[:, k, :], m.attn[:, 1, k, :], start=True, stop=False)
                    pe.matmul(o, m.U[:, p, :], m.attn[:, 0, k, :], start=False, stop=False)
                    mm = pe.matmul(o, m.Tst[:, p, :], m.RC[:, k, :], start=False, stop=True)
                mm.then_inc(s["rw_mm"], 1)
                pe.wait_ge(s["rwc_v"], nth(l, "rwc_v", g * 6 + 3 * c + 3))

    def rwkv_sample(l):
        pe.wait_ge(s["rws_in"], nth(l, "rws_in", 1))
        pe.wait_ge(s["state_in"], nth(l, "state_in", 64))
        for k in range(2):
            pe.matmul(ps[:, 0, 128 * k:128 * k + 128], m.BE[:, k, :], m.AE[:, k, :], start=True, stop=True)
            pe.matmul(ps[:, 3, 64 * k:64 * k + 64], m.BE[:, k, :], m.RC[:, k, :], start=True, stop=True)
            pe.matmul(ps[:, 2, 128 * k:128 * k + 128], m.KE[:, k, :], m.AE[:, k, :], start=True, stop=True)
            pe.matmul(ps[:, 3, 256 + 64 * k:320 + 64 * k], m.KE[:, k, :], m.RC[:, k, :], start=True, stop=True)
            mm = pe.matmul(ps[:, 1, 128 * k:128 * k + 128], m.AE[:, k, :], m.BE[:, k, :], start=True, stop=True)
        mm.then_inc(s["rws_mm"], 1)
        for b, tile in ((4, m.BE), (5, m.KE), (6, m.VE)):
            for k in range(2):
                mm = pe.transpose(ps[:, b, 128 * k:128 * k + 128], tile[:, k, :], ident)
        mm.then_inc(s["rws_mm"], 1)
        pe.wait_ge(s["rws_v"], nth(l, "rws_v", 1))
        for k in range(2):
            mm = pe.matmul(ps[:, 0, 128 * k:128 * k + 128], m.DT[:, k, :], m.D[:, k, :], start=True, stop=True)
        mm.then_inc(s["rws_mm"], 1)
        pe.wait_ge(s["rws_v"], nth(l, "rws_v", 2))
        for k in range(2):
            mm = pe.matmul(ps[:, 1, 128 * k:128 * k + 128], m.DT[:, k, :], m.X[:, k, :], start=True, stop=True)
        mm.then_inc(s["rws_mm"], 1)
        pe.wait_ge(s["rws_a"], nth(l, "rws_a", 1))
        pe.wait_ge(s["rws_v"], nth(l, "rws_v", 3))
        for p in range(2):
            o = ps[:, 4, 128 * p:128 * p + 128]
            pe.matmul(o, m.Mak[:, p, :], m.VEt[:, p, :], start=True, stop=False)
            for b in range(DB):
                mm = pe.matmul(o, m.AEb[:, p, b, :], m.TB[:, p, b, :], start=False, stop=b == DB - 1)
        mm.then_inc(s["rws_mm"], 1)
        pe.wait_ge(s["rws_v"], nth(l, "rws_v", 4))
        for p in range(2):
            mm = pe.matmul(ps[:, 5, 128 * p:128 * p + 128], m.X[:, p, :], m.W[:, p, :], start=True, stop=True)
        mm.then_inc(s["rws_mm"], 1)
        pe.wait_ge(s["rws_v"], nth(l, "rws_v", 5))
        for p in range(2):
            o = ps[:, 7, 64 * p:64 * p + 64]
            pe.matmul(o, m.VEt[:, p, :], m.attn[:, 1, p, :], start=True, stop=False)
            pe.matmul(o, m.U[:, p, :], m.attn[:, 0, p, :], start=False, stop=False)
            for b in range(DB):
                q = slice(DS * b, DS * b + DS)
                mm = pe.matmul(o[:, q], m.TB[:, p, b, :], m.RC[:, p, q], start=False, stop=b == DB - 1)
        mm.then_inc(s["rws_mm"], 1)
        for p in range(2):
            pe.wait_ge(s["rws_v"], nth(l, "rws_v", 6 + 2 * p))
            for h in range(2):
                o = ps[:, 2 * p + h, :]
                q = slice(4 * h, 4 * h + 4)
                pe.matmul(o, m.BEt[:, p, :], m.UEb[:, q, :], start=True, stop=False)
                pe.matmul(o, m.KEt[:, p, :], m.VEb[:, q, :], start=False, stop=False)
                mm = pe.matmul(o, ident, m.TB[:, p, q, :], start=False, stop=True)
            mm.then_inc(s["rws_mm"], 1)

    def y_norm(l):
        for step, src in enumerate((m.yb, m.y2)):
            if step:
                pe.wait_ge(s["yn_in"], nth(l, "yn_in", 1))
            else:
                pe.wait_ge(s["rws_a"], nth(l, "rws_a", 2))
                pe.wait_ge(s["rws_v"], nth(l, "rws_v", 9))
            for p in range(2):
                pe.matmul(ps[:, 2 * p, :], m.const("ones_head"), src[:, p, 0:SEQ], start=True, stop=True)
                mm = pe.matmul(ps[:, 2 * p + 1, 0:64], m.const("ones_head"), src[:, p, SEQ:TP], start=True, stop=True)
            mm.then_inc(s["yn_mm"], 1)

    def prompt_attention(l):
        def logits(i):
            if i:
                pe.wait_ge(s["lg_taken"], nth(l, "lg_taken", i))
            for h in range(4):
                q = slice(64 * (h % 2), 64 * (h % 2) + 64)
                mm = pe.matmul(ps[:, h, 0:P * (i + 1)], m.qT[q, h // 2, P * i:P * i + P], m.kT[q, h // 2, 0:P * (i + 1)],
                               start=True, stop=True)
            mm.then_inc(s["lg_mm"], 1)

        def values(i, h):
            pe.wait_ge(s["pt_copied"], nth(l, "pt_copied", 4 * i + h + 1))
            q = slice(64 * (h % 2), 64 * (h % 2) + 64)
            for c in range(i + 1):
                mm = pe.matmul(ps[q, 6 + i % 2, P * (h // 2):P * (h // 2) + P], m.A[:, c, 512 + 64 * h:576 + 64 * h],
                               m.pT[i % 2][:, h, P * c:P * c + P], start=c == 0, stop=c == i)
            return mm

        def output(i):
            pe.wait_ge(s["p_ready"], nth(l, "p_ready", i + 1))
            for h in range(4):
                k = 4 * i + h
                if k >= 2:
                    pe.wait_ge(s["pt_copied"], nth(l, "pt_copied", k - 1))
                for c in range(i + 1):
                    mm = pe.transpose(ps[:, 4 + h % 2, P * c:P * c + P], m.lg[i % 2][:, h, P * c:P * c + P], ident)
                mm.then_inc(s["pt_mm"], 1)
                if h == 0 and i >= 2:
                    pe.wait_ge(s["ya_copied"], nth(l, "ya_copied", i - 1))
                if h:
                    values(i, h - 1)
            values(i, 3).then_inc(s["pv_mm"], 1)

        pe.wait_ge(s["yn_std"], nth(l, "yn_std", 1))
        logits(0)
        for i in range(NT):
            if i + 1 < NT:
                logits(i + 1)
            output(i)

    def sample_attention(l):
        spread = m.const("spread")
        bias = m.bias[3]
        for g in range(2):
            pe.wait_ge((s["k0_in"], s["k1_in"])[g], nth(l, f"k{g}_in", 256))
            a = 2 - 2 * g
            pe.wait_ge(s["qb_ready"], nth(l, "qb_ready", 1))
            for j in range(4):
                for p in range(2):
                    pe.matmul(ps[32 * j:32 * j + 32, a, :], m.QB[:, p, 4 * g + j, :], m.K[g][:, p, j, :],
                              start=p == 0, stop=False, skip_group_check=True)
            pe.matmul(ps[:, a, :], spread[0:NS, P * g:P * g + P], bias[0:NS, 0:PAST], start=False, stop=True,
                      skip_group_check=True)
            for p in range(2):
                pe.matmul(ps[:, a + 1, 0:NS], m.QB[:, p, 4 * g:4 * g + 4, :].rearrange("p b m -> p (b m)"), m.kT[:, p, SEQ:T],
                          start=p == 0, stop=False)
            pe.matmul(ps[:, a + 1, 0:NS], spread[0:NS, P * g:P * g + P], bias[0:NS, PAST:T], start=False, stop=True)\
                .then_inc(s["s_lg_mm"], 1)
        for g in range(2):
            pe.wait_ge(s["pt_copied"], nth(l, "pt_copied", 16))
            pe.wait_ge(s["s_p"], nth(l, "s_p", g + 1))
            if g:
                pe.wait_ge(s["s_pt"], nth(l, "s_pt", 1))
            for c in range(NPAGE):
                pe.transpose(ps[:, 4, P * c:P * c + P], m.s_lg[g][:, P * c:P * c + P], ident)
            pe.transpose(ps[0:NS, 5, 0:P], m.s_lg[g][:, PAST:T], ident).then_inc(s["s_pt_mm"], 1)
            pe.wait_ge(s["s_pt"], nth(l, "s_pt", g + 1))
            pe.wait_ge(s["ya_copied"], nth(l, "ya_copied", 4))
            pe.wait_ge((s["v0_in"], s["v1_in"])[g], nth(l, f"v{g}_in", 256))
            for j in range(4):
                for p in range(2):
                    o = ps[:, 7, 128 * p + 16 * (4 * g + j):128 * p + 16 * (4 * g + j) + 16]
                    for c in range(NPAGE):
                        pe.matmul(o, m.V[g][:, j, c, P * p:P * p + P], m.s_pT[g][:, P * c + 32 * j:P * c + 32 * j + 16],
                                  start=c == 0, stop=False)
                    mm = pe.matmul(o, m.A[0:NS, NT, 512 + P * p:512 + P * p + P], m.s_pTn[g][0:NS, 32 * j:32 * j + 16],
                                   start=False, stop=True)
            mm.then_inc(s["s_pv_mm"], 1)

    def transposes_of_x(l, first, i):
        n = P if i < NT else NS
        if i:
            pe.wait_ge(s["xt_copied"], nth(l, "xt_copied", first + i))
        pe.wait_ge(s["ln_done"], nth(l, "ln_done", first + i + 1))
        for c in range(KC):
            o, x = ps[:, 4 + c // 4, n * (c % 4):n * (c % 4) + n], m.x[0:n, i, P * c:P * c + P]
            if i < NT:
                mm = pe.transpose(o, x, ident)
            else:
                mm = pe.matmul(o, x, ident[0:n, 0:n], start=True, stop=True)
        mm.then_inc(s["xt_mm"], 1)

    def router(l, i):
        pe.wait_ge(s["xt_copied"], nth(l, "xt_copied", i + 1))
        for c in range(KC):
            mm = pe.matmul(ps[0:(P if i < NT else NS), 7, NEXP * i:NEXP * i + NEXP], m.xT[:, c, row_tile(i)],
                           m.w_router[:, c, :], start=c == 0, stop=c == KC - 1)
        return mm

    def output_projection(l):
        pe.wait_ge(s["wout_in"], nth(l, "wout_in", 16))
        pe.wait_ge(s["attn_done"], nth(l, "attn_done", 1))
        for i in range(5):
            n = P if i < NT else NS
            if i >= 2:
                pe.wait_ge(s["ln_var"], nth(l, "ln_var", i - 1))
            for h in range(2):
                for c in range(8):
                    mm = pe.matmul(ps[0:n, 2 * (i % 2) + h, :], m.yT[:, c, row_tile(i)], m.wout[:, c, 512 * h:512 * h + 512],
                                   start=c == 0, stop=c == 7)
            mm.then_inc(s["mix_mm"], 1)
            if i >= 2:
                transposes_of_x(l, 0, i - 2)
        router(l, 0)
        router(l, 1)
        transposes_of_x(l, 0, NT - 1)
        router(l, 2)
        transposes_of_x(l, 0, NT)
        router(l, 3)
        router(l, NT).then_inc(s["router_mm"], 1)

    def experts(l):
        pe.wait_ge(s["chosen"], nth(l, "chosen", 1))
        for i in range(6):
            o = ps[:, 6, NEXP * i:NEXP * i + NEXP]
            for j in range(min(i, NT)):
                pe.matmul(o, m.all1, m.chosen[:, j, :], start=j == 0, stop=False)
            if i < NT:
                pe.matmul(o, m.before, m.chosen[:, i, :], start=i == 0, stop=True)
            else:
                mm = pe.matmul(o, (m.before if i == NT else m.all1)[0:NS], m.chosen[0:NS, NT, :], start=False, stop=True)
        mm.then_inc(s["slots_mm"], 1)

        def rows_to_columns(e, k):
            pe.wait_ge((s["xg0_in"], s["xg1_in"])[k], nth(l, f"xg{k}_in", e * 16 + 16))
            pe.wait_ge(s["xgt_copied"], nth(l, "xgt_copied", e * 2 + k))
            for c in range(KC):
                mm = pe.transpose(ps[:, c // 4, P * (c % 4):P * (c % 4) + P], m.xg[k][:, P * c:P * c + P], ident)
            mm.then_inc(s["xgt_mm"], 1)

        def gate_and_up(e, k):
            pe.wait_ge((s["moe0_in"], s["moe1_in"])[k], nth(l, f"moe{k}_in", e * 32 + 32))
            pe.wait_ge(s["h_ready"], nth(l, "h_ready", e * 2 + k))
            pe.wait_ge(s["xgt_copied"], nth(l, "xgt_copied", e * 2 + (k + 1)))
            for c in range(KC):
                mm = pe.matmul(ps[:, 3, :], m.xgT[:, c, :], m.w_gu[k][:, c, :], start=c == 0, stop=c == KC - 1)
            mm.then_inc(s["gu_mm"], 1)

        def hidden_to_columns(e, k):
            pe.wait_ge(s["ht_copied"], nth(l, "ht_copied", e * 2 + k))
            pe.wait_ge(s["h_ready"], nth(l, "h_ready", e * 2 + (k + 1)))
            for f in range(2):
                mm = pe.transpose(ps[:, 2, P * f:P * f + P], m.h[:, P * f:P * f + P], ident)
            mm.then_inc(s["ht_mm"], 1)

        def down(e, k):
            pe.wait_ge(s["y_copied_a"], nth(l, "y_copied_a", e * 2 + k))
            pe.wait_ge(s["y_copied_v"], nth(l, "y_copied_v", e * 2 + k))
            pe.wait_ge(s["ht_copied"], nth(l, "ht_copied", e * 2 + (k + 1)))
            for h in range(2):
                for f in range(2):
                    mm = pe.matmul(ps[:, 5 + h, :], m.hT[:, f, :], m.w_dn[k][:, f, 512 * h:512 * h + 512],
                                   start=f == 0, stop=f == 1)
            mm.then_inc(s["down_mm"], 1)

        rows_to_columns(0, 0)
        gate_and_up(0, 0)
        with pe.Fori(0, NEXP // 2 - 1) as e:
            for k in range(2):
                rows_to_columns(e + k, 1 - k)
                hidden_to_columns(e, k)
                down(e, k)
                gate_and_up(e + k, 1 - k)
        e = NEXP // 2 - 1
        rows_to_columns(e, 1)
        hidden_to_columns(e, 0)
        down(e, 0)
        gate_and_up(e, 1)
        hidden_to_columns(e, 1)
        down(e, 1)
        extra = pe.value_load(m.extra_blocks, min_val=0, max_val=BLOCKS - NEXP)
        with pe.Fori(NEXP // 2, BLOCKS // 2) as e:
            with pe.If(extra > e * 2 - NEXP):
                rows_to_columns(e, 0)
                gate_and_up(e, 0)
                rows_to_columns(e, 1)
                hidden_to_columns(e, 0)
                down(e, 0)
                gate_and_up(e, 1)
                hidden_to_columns(e, 1)
                down(e, 1)
            with pe.If(extra <= e * 2 - NEXP):
                pe.wait_ge(s["xg0_in"], nth(l, "xg0_in", e * 16 + 16))
                pe.wait_ge(s["xg1_in"], nth(l, "xg1_in", e * 16 + 16))
                pe.wait_ge(s["moe0_in"], nth(l, "moe0_in", e * 32 + 32))
                pe.wait_ge(s["moe1_in"], nth(l, "moe1_in", e * 32 + 32))
                pe.wait_ge(s["y_copied_a"], nth(l, "y_copied_a", e * 2))
                pe.wait_ge(s["y_copied_v"], nth(l, "y_copied_v", e * 2)).then_inc(s["xgt_mm"], 2)
                pe.drain().then_inc(s["gu_mm"], 2)
                pe.drain().then_inc(s["ht_mm"], 2)
                pe.drain().then_inc(s["down_mm"], 2)
        for i in range(5):
            transposes_of_x(l, 5, i)

    pe.drain().then_inc(s["mix_mm"], 1)
    pe.drain().then_inc(s["rw_mm"], 1)
    pe.wait_ge(s["const_in"], 64)
    pe.wait_ge(s["x_in"], 32)
    with pe.Fori(0, DEPTH) as l:
        pe.wait_ge(s["xt_copied"], nth(l, "xt_copied", 0))
        pe.wait_ge(s["params_in"], nth(l, "params_in", 16))
        row_projection(l)
        column_projection(l)
        column_jobs(l)
        rwkv_loop(l)
        rwkv_sample(l)
        y_norm(l)
        prompt_attention(l)
        sample_attention(l)
        output_projection(l)
        experts(l)


def scalar_program(act, s, m, ps, dout):
    def copy(out, in_):
        return act.activation(out, in_, ACT.Copy)

    def seqs(ap):
        return ap.rearrange("p (b t) -> p b t", t=DS)

    def projections(l):
        for k in range(10):
            i, h = divmod(k, 2)
            n = P if i < NT else NS
            a, w = ((0, 512), (512, ACOLS - 512))[h]
            act.wait_ge(s["rows_mm"], nth(l, "rows_mm", k + 1))
            copy(m.A[0:n, i, a:a + w], ps[0:n, k % 2, 0:w]).then_inc(s["rows_copied"], 1)
        act.wait_ge(s["ki_var"], nth(l, "ki_var", 1))
        act.activation(m.kist[1], m.kist[1], ACT.Sqrt, bias=m.const("eps")[:, 0:1], scale=1.0 / 32).then_inc(s["ki_std"], 1)
        shift = m.small("shift").rearrange("p (n c) -> p n c", c=9)
        between = {1: lambda: head_columns(l, 0), 2: lambda: head_columns(l, 3), 3: lambda: sample_indexer(l),
                   4: lambda: relus(l, 3), 5: lambda: relus(l, 2), 6: lambda: relus(l, 1), 7: lambda: sample_scores(l)}
        for n in range(NCH):
            act.wait_ge(s["fm_mm"], nth(l, "fm_mm", n + 1))
            if n >= 4:
                act.wait_ge(s["fm_used"], nth(l, "fm_used", n - 3))
            sample = seqs(ps[:, 4 + n % 2, 0:NS])
            if n < 7:
                copy(shift[:, n, 0:1], ps[:, 2 + n % 2, SEQ - 1:SEQ])
                copy(shift[:, n, 1:9], sample[:, :, DS - 1])
            copy(m.fm_p[n % 4][:, 3:3 + SEQ], ps[:, 2 + n % 2, :])
            copy(m.fm_s[n % 4][:, :, 3:7], sample).then_inc(s["fm_copied"], 1)
            if n in between:
                between[n]()

    def softplus_steps(l):
        act.wait_ge(s["lam_abs"], nth(l, "lam_abs", 1))
        act.activation(m.lam[1], m.lam[0], ACT.Exp, scale=-1.0).then_inc(s["lam_exp"], 1)
        act.wait_ge(s["lam_sum"], nth(l, "lam_sum", 1))
        act.activation(m.lam[3], m.lam[2], ACT.Ln).then_inc(s["lam_log"], 1)

    def job(l, j, out, func, width, bias=None):
        act.wait_ge(s["job_mm"], nth(l, "job_mm", j + 1))
        b = 4 + 2 * (j % 2)
        for o, i in ((out[:, 0:SEQ], ps[:, b, :]), (out[:, SEQ:width], ps[:, b + 1, 0:width - SEQ])):
            ins = copy(o, i) if func == ACT.Copy else act.activation(o, i, func) if bias is None else \
                act.activation(o, i, func, bias=bias)
        ins.then_inc(s["job_out"], 1)

    def column_stage(l):
        act.wait_ge(s["fm_used"], nth(l, "fm_used", 7))
        act.activation(m.Z[0:32, 6, :], m.Z[0:32, 6, :], ACT.Tanh)
        act.activation(m.Z[64:128, 6, :], m.Z[64:128, 6, :], ACT.Sigmoid).then_inc(s["lora_act"], 1)
        for p in range(2):
            job(l, p, m.gx[:, p, :], ACT.Sigmoid, T, m.param("gxb")[:, p:p + 1])
        for p in range(2):
            job(l, 2 + p, m.za[:, p, :], ACT.Sigmoid, T, m.param("gab")[:, p:p + 1])
        for p in range(2):
            job(l, 4 + p, m.gate[:, p, :], ACT.Copy, TP)
        act.wait_ge(s["selected"], nth(l, "selected", 1))
        for p in range(2):
            job(l, 6 + p, m.ea[:, p, :], ACT.Sigmoid, TP, m.param("w0")[:, p:p + 1])
        for p in range(2):
            job(l, 8 + p, m.aa[:, p, :], ACT.Sigmoid, TP, m.param("a0")[:, p:p + 1])
        act.wait_ge(s["dz_ready"], nth(l, "dz_ready", 1))
        act.activation(m.za_tanh, m.za, ACT.Tanh)
        act.activation(m.a_lru, m.za, ACT.Exp, scale=-1.0).then_inc(s["d_tanh"], 1)
        act.wait_ge(s["gelu_in"], nth(l, "gelu_in", 1))
        act.activation(m.gelu, m.gelu, ACT.Tanh, scale=GELU_C).then_inc(s["gelu_tanh"], 1)
        act.wait_ge(s["cum_ready"], nth(l, "cum_ready", 1))
        act.activation(m.ea, m.ea, ACT.Exp, scale=-DECAY)
        act.activation(m.ec, m.en, ACT.Exp, scale=-DECAY)
        act.activation(m.en, m.en, ACT.Exp, scale=DECAY).then_inc(s["exps_ready"], 1)
        act.wait_ge(s["job_mm"], nth(l, "job_mm", 12))
        for p in range(2):
            job(l, 10 + p, m.bonus[:, p, :], ACT.Copy, TP)
        act.wait_ge(s["om_ready"], nth(l, "om_ready", 1))
        act.activation(m.za, m.za, ACT.Sqrt).then_inc(s["om_sqrt"], 1)
        act.wait_ge(s["job_mm"], nth(l, "job_mm", 14))
        for p in range(2):
            job(l, 12 + p, m.bv[:, p, :], ACT.Sqrt, TP)

    def rwkv(l):
        with act.Fori(0, 4) as g:
            def mm(n):
                act.wait_ge(s["rw_mm"], nth(l, "rw_mm", g * RW_PE + n))

            mm(2)
            for b, t in ((4, m.BEt), (5, m.KEt), (6, m.VEt)):
                ins = copy(t.rearrange("p k n -> p (k n)"), ps[:, b, :])
            ins.then_inc(s["rw_a"], 1)
            def turned(n, bank, t):
                for c in range(2):
                    mm(n[c])
                    copy(t[:, 2 * c:2 * c + 2, :].rearrange("p k n -> p (k n)"), ps[:, 4 * c + bank, 0:2 * P]).then_inc(s["rw_a"], 1)

            turned((4, 6), 1, m.D2T)
            turned((8, 10), 3, m.D4T)
            turned((19, 20), 0, m.XT_)
            turned((21, 22), 1, m.FT)
            for c in range(2):
                mm(31 + 3 * c)
                copy(m.yb[:, :, bass.ds(g * (2 * CH) + c * CH, CH)], ps[:, 7, 0:128].rearrange("p (q t) -> p q t", q=2))\
                    .then_inc(s["rw_a"], 1)
        act.wait_ge(s["rws_mm"], nth(l, "rws_mm", 2))
        for b, t in ((4, m.BEt), (5, m.KEt), (6, m.VEt)):
            ins = copy(t[:, 0:2, :].rearrange("p k n -> p (k n)"), ps[:, b, 0:256])
        ins.then_inc(s["rws_a"], 1)
        act.wait_ge(s["rws_mm"], nth(l, "rws_mm", 7))
        copy(m.yb[:, :, SEQ:TP], ps[:, 7, 0:128].rearrange("p (q t) -> p q t", q=2)).then_inc(s["rws_a"], 1)
        act.wait_ge(s["yn_mm"], nth(l, "yn_mm", 2))
        for p in range(2):
            act.activation(m.ec[:, p, 0:SEQ], ps[:, 2 * p, :], ACT.Sqrt, bias=m.const("eps")[:, 1:2], scale=1.0 / 64)
            ins = act.activation(m.ec[:, p, SEQ:TP], ps[:, 2 * p + 1, 0:64], ACT.Sqrt, bias=m.const("eps")[:, 1:2],
                                 scale=1.0 / 64)
        ins.then_inc(s["yn_std"], 1)

    def head_columns(l, first):
        if first == 0:
            act.wait_ge(s["x_kept"], nth(l, "x_kept", 0))
        dst = [m.qT[:, 0, :], m.qT[:, 1, :], m.kT[:, 0, :], m.kT[:, 1, :], m.qiT, m.kiT]
        for b in range(first, first + 3):
            act.wait_ge(s["tr_mm"], nth(l, "tr_mm", b + 1))
            act.activation(dst[b][:, 0:SEQ], ps[:, (6, 7, 0)[b % 3], :], ACT.Copy, scale=0.125 if b < 2 else 1.0)\
                .then_inc(s["tr_copied"], 1)
        for b in range(first, first + 3):
            ins = act.activation(dst[b][:, SEQ:T], ps[:, 1, NS * b:NS * b + NS], ACT.Copy, scale=0.125 if b < 2 else 1.0)
        ins.then_inc(s["tr_sample"], 1)

    def relus(l, i):
        if i == 3:
            act.wait_ge(s["s_sums"], nth(l, "s_sums", 1))
        act.wait_ge(s["idx_mm"], nth(l, "idx_mm", 4 - i))
        for h in range(4):
            k = 4 * (3 - i) + h
            if k >= 2:
                act.wait_ge(s["rl_used"], nth(l, "rl_used", k - 1))
            act.activation(m.relu[h % 2][:, 0:P * (i + 1)], ps[:, (6, 7, 0, 1)[h], 0:P * (i + 1)], ACT.Relu, scale=32 ** -0.5)\
                .then_inc(s["relu_done"], 1)

    def sample_indexer(l):
        act.wait_ge(s["s_idx_mm"], nth(l, "s_idx_mm", 1))
        copy(m.WB, ps[:, 7, 256:256 + 4 * NS].rearrange("p (h b t) -> p b h t", h=4, t=DS))
        dots = m.relu[0].rearrange("p (c j n) -> p c j n", j=4, n=16)
        for j, bank in enumerate((7, 0, 1, 6)):
            act.activation(dots[:, :, j, :], ps[:, bank, 0:P].rearrange("p (c n) -> p c n", n=16), ACT.Relu, scale=32 ** -0.5)
            ins = act.activation(m.relu_n[0:NS, j, :], ps[0:NS, bank, P:P + NS], ACT.Relu, scale=32 ** -0.5)
        ins.then_inc(s["s_relu"], 1)

    def sample_scores(l):
        act.wait_ge(s["s_tr_mm"], nth(l, "s_tr_mm", 1))
        copy(m.score[3][0:NS, 0:PAST], ps[0:NS, 0, :]).then_inc(s["s_score"], 1)

    def attention(l):
        def exps(i):
            act.wait_ge(s["lg_ready"], nth(l, "lg_ready", i + 1))
            for h in range(4):
                x = m.lg[i % 2][:, h, 0:P * (i + 1)]
                ins = act.activation(x, x, ACT.Exp, bias=m.nmax[i % 2][:, h:h + 1], accum_out=m.ssum[i % 2][:, h:h + 1])
            ins.then_inc(s["p_exp"], 1)

        def turned(i):
            for h in range(4):
                act.wait_ge(s["pt_mm"], nth(l, "pt_mm", 4 * i + h + 1))
                copy(m.pT[i % 2][:, h, 0:P * (i + 1)], ps[:, 4 + h % 2, 0:P * (i + 1)]).then_inc(s["pt_copied"], 1)

        def output(i):
            act.wait_ge(s["pv_mm"], nth(l, "pv_mm", i + 1))
            copy(m.yT[:, 0:2, P * i:P * i + P], ps[:, 6 + i % 2, 0:256].rearrange("p (q n) -> p q n", q=2))\
                .then_inc(s["ya_copied"], 1)

        exps(0)
        for i in range(NT):
            if i + 1 < NT:
                exps(i + 1)
            turned(i)
            output(i)

        for g in range(2):
            act.wait_ge(s["s_lg_mm"], nth(l, "s_lg_mm", g + 1))
            copy(m.s_lg[g][:, 0:PAST], ps[:, 2 - 2 * g, :])
            copy(m.s_lg[g][:, PAST:T], ps[:, 3 - 2 * g, 0:NS]).then_inc(s["s_lg"], 1)
        for g in range(2):
            act.wait_ge(s["s_max"], nth(l, "s_max", g + 1))
            act.activation(m.s_lg[g], m.s_lg[g], ACT.Exp, bias=m.nmax[g][:, 0:1], accum_out=m.ssum[g][:, 0:1])\
                .then_inc(s["s_exp"], 1)
        for g in range(2):
            act.wait_ge(s["s_pt_mm"], nth(l, "s_pt_mm", g + 1))
            copy(m.s_pT[g], ps[:, 4, :])
            copy(m.s_pTn[g][0:NS, :], ps[0:NS, 5, 0:P]).then_inc(s["s_pt"], 1)
        act.wait_ge(s["s_pv_mm"], nth(l, "s_pv_mm", 2))
        for p in range(2):
            for h in range(2):
                q = slice(64 * h, 64 * h + 64)
                ins = copy(seqs(m.yT[q, p, SEQ:T]), ps[q, 7, P * p:P * p + P].rearrange("p (b h t) -> p b h t", b=DB, h=4)[:, :, 2 * p + h, :])
        ins.then_inc(s["attn_done"], 1)

    def norm(l, first):
        if first == 0:
            act.wait_ge(s["rows_stored"], nth(l, "rows_stored", 96))
            act.wait_ge(s["small_out"], nth(l, "small_out", 16))
        def deviation(i):
            n = P if i < NT else NS
            act.wait_ge(s["ln_var"], nth(l, "ln_var", first + i + 1))
            act.activation(m.std[i % 2][0:n], m.mv[i % 2][0:n, 1:2], ACT.Sqrt, bias=m.const("eps")[0:n, 0:1])\
                .then_inc(s["ln_std"], 1)

        def columns_of_x(i):
            n = P if i < NT else NS
            act.wait_ge(s["xt_mm"], nth(l, "xt_mm", first + i + 1))
            for h in range(2):
                ins = copy(m.xT[:, 4 * h:4 * h + 4, P * i:P * i + n], ps[:, 4 + h, 0:4 * n].rearrange("p (c t) -> p c t", c=4))
            ins.then_inc(s["xt_copied"], 1)

        for i in range(5):
            deviation(i)
            if i >= 2:
                columns_of_x(i - 2)
        columns_of_x(3)
        columns_of_x(4)
        if first:
            act.wait_ge(s["ln_done"], nth(l, "ln_done", 10))
            act.dma_start(layer_of(dout["x"], l + 1)[0:SEQ].rearrange("(i p) d -> p i d", p=P), m.x[:, 0:NT, :])\
                .then_inc(s["x_kept"], 16)
            act.dma_start(layer_of(dout["x"], l + 1)[SEQ:T], m.x[0:NS, NT, :]).then_inc(s["x_kept"], 16)

    def experts(l):
        act.wait_ge(s["router_mm"], nth(l, "router_mm", 1))
        act.activation(m.gsig[:, 0:NT, :], ps[:, 7, 0:NT * NEXP].rearrange("p (i e) -> p i e", e=NEXP), ACT.Sigmoid)
        act.activation(m.gsig[0:NS, NT, :], ps[0:NS, 7, NT * NEXP:5 * NEXP], ACT.Sigmoid).then_inc(s["router_sig"], 1)

        def columns_of_rows(e, k):
            act.wait_ge(s["xgt_mm"], nth(l, "xgt_mm", e * 2 + (k + 1)))
            copy(m.xgT.rearrange("p (h c) n -> p h (c n)", h=2), ps[:, 0:2, :]).then_inc(s["xgt_copied"], 1)

        def silu(e, k):
            act.wait_ge(s["h_ready"], nth(l, "h_ready", e * 2 + k))
            act.wait_ge(s["gu_mm"], nth(l, "gu_mm", e * 2 + (k + 1)))
            act.activation(m.silu, ps[:, 3, 0:DEXP], ACT.Silu).then_inc(s["silu_done"], 1)

        def rows_back(e, k):
            act.wait_ge((s["y0_stored"], s["y1_stored"])[k], nth(l, f"y{k}_stored", e * 16))
            act.wait_ge(s["down_mm"], nth(l, "down_mm", e * 2 + (k + 1)))
            copy(m.y[k][:, 0:512], ps[:, 5, :]).then_inc(s["y_copied_a"], 1)

        def store(e, k):
            act.wait_ge(s["y_copied_a"], nth(l, "y_copied_a", e * 2 + (k + 1)))
            act.wait_ge(s["y_copied_v"], nth(l, "y_copied_v", e * 2 + (k + 1)))
            act.dma_start(m.rows_out.rearrange("(n p) d -> p n d", p=P)[:, bass.ds(e * 2 + k, 1), :]
                          .rearrange("p n d -> p (n d)"), m.y[k]).then_inc((s["y0_stored"], s["y1_stored"])[k], 16)

        columns_of_rows(0, 0)
        silu(0, 0)
        with act.Fori(0, NEXP // 2 - 1) as e:
            for k in range(2):
                columns_of_rows(e + k, 1 - k)
                rows_back(e, k)
                silu(e + k, 1 - k)
                store(e, k)
        e = NEXP // 2 - 1
        columns_of_rows(e, 1)
        rows_back(e, 0)
        silu(e, 1)
        store(e, 0)
        rows_back(e, 1)
        store(e, 1)
        extra = act.value_load(m.extra_blocks, min_val=0, max_val=BLOCKS - NEXP)
        with act.Fori(NEXP // 2, BLOCKS // 2) as e:
            with act.If(extra > e * 2 - NEXP):
                columns_of_rows(e, 0)
                silu(e, 0)
                columns_of_rows(e, 1)
                rows_back(e, 0)
                silu(e, 1)
                store(e, 0)
                rows_back(e, 1)
                store(e, 1)
            with act.If(extra <= e * 2 - NEXP):
                act.wait_ge(s["down_mm"], nth(l, "down_mm", e * 2 + 2))
                act.wait_ge(s["y0_stored"], nth(l, "y0_stored", e * 16))
                act.wait_ge(s["y1_stored"], nth(l, "y1_stored", e * 16)).then_inc(s["xgt_copied"], 2)
                act.drain().then_inc(s["y_copied_a"], 2)
                act.drain().then_inc(s["y0_stored"], 16)
                act.drain().then_inc(s["y1_stored"], 16)
                act.drain().then_inc(s["silu_done"], 2)

    for name in ("xt_copied", "xgt_copied", "y_copied_a", "y0_stored", "y1_stored", "x_kept"):
        act.drain().then_inc(s[name], 1)
    act.wait_ge(s["const_in"], 64)
    act.wait_ge(s["zeroed"], 1)
    with act.Fori(0, DEPTH) as l:
        softplus_steps(l)
        projections(l)
        column_stage(l)
        rwkv(l)
        attention(l)
        norm(l, 0)
        experts(l)
        norm(l, 5)


def vector_program(dve, s, m, ps):
    tt, ts, stt = dve.tensor_tensor, dve.tensor_scalar, dve.scalar_tensor_tensor
    mul, add, sub = ALU.mult, ALU.add, ALU.subtract
    ident = m.const("ident")

    def seqs(ap):
        return ap.rearrange("p (b t) -> p b t", t=DS)

    def softplus(l):
        L = m.lam
        stt(L[0], m.param("lam"), -1.0, m.param("lam"), mul, ALU.max).then_inc(s["lam_abs"], 1)
        ts(L[7], m.param("lam"), -1.0, 0.0, mul, ALU.max)
        ts(m.omka, m.param("ka"), -1.0, 1.0, mul, add)
        dve.wait_ge(s["lam_exp"], nth(l, "lam_exp", 1))
        ts(L[2], L[1], 1.0, None, add).then_inc(s["lam_sum"], 1)
        dve.wait_ge(s["lam_log"], nth(l, "lam_log", 1))
        ts(L[4], L[2], 1.0, None, ALU.is_equal)
        dve.drain()
        tt(L[3], L[3], L[4], add)
        stt(L[5], L[2], -1.0, L[4], add, add)
        dve.drain()
        dve.reciprocal(L[5], L[5])
        tt(L[6], L[1], L[3], mul)
        dve.drain()
        tt(L[6], L[6], L[5], mul)
        dve.drain()
        tt(L[6], L[6], L[7], add)
        dve.drain()
        ts(L[6], L[6], 8.0, None, mul)

    def rotate(x1, x2, c, sn, t):
        tt(t[0], x1, c, mul)
        tt(t[1], x2, sn, mul)
        tt(t[2], x2, c, mul)
        tt(t[3], x1, sn, mul)
        dve.drain()
        tt(x1, t[0], t[1], sub)
        return tt(x2, t[2], t[3], add)

    def row_stage(l):
        dve.wait_ge(s["rows_copied"], nth(l, "rows_copied", 10))
        ki = m.A[:, :, C_KI:C_KI + 32]
        dve.tensor_reduce(m.kist[0], ki, AX.X, add)
        dve.drain()
        ts(m.kist[0], m.kist[0], 1.0 / 32, None, mul)
        dve.drain()
        tt(m.ki_c, ki, m.kist[0].unsqueeze(2).broadcast_to([P, 5, 32]), sub)
        dve.drain()
        tt(m.ki_2, m.ki_c, m.ki_c, mul)
        dve.drain()
        dve.tensor_reduce(m.kist[1], m.ki_2, AX.X, add).then_inc(s["ki_var"], 1)

        def table(name, half, heads):
            return m.const(name).rearrange("p (i f) -> p i f", f=half).unsqueeze(2).broadcast_to([P, 5, heads, half])

        qk = m.A[:, :, 0:512].rearrange("p i (h d) -> p i h d", d=64)
        rotate(qk[:, :, :, 0:8], qk[:, :, :, 8:16], table("cos_q", 8, 8), table("sin_q", 8, 8), m.rope_q)
        qi = m.A[:, :, C_QI:C_KI].rearrange("p i (h d) -> p i h d", d=32)
        rotate(qi[:, :, :, 0:4], qi[:, :, :, 4:8], table("cos_i", 4, 4), table("sin_i", 4, 4), m.rope_i)
        wi = m.A[:, :, C_WI:ACOLS]
        ts(wi, wi, 0.5, None, mul)
        dve.wait_ge(s["ki_std"], nth(l, "ki_std", 1))
        dve.reciprocal(m.kist[1], m.kist[1])
        dve.drain()
        tt(m.ki_c, m.ki_c, m.kist[1].unsqueeze(2).broadcast_to([P, 5, 32]), mul)
        dve.drain()
        tt(m.ki_c, m.ki_c, m.param("idxg").unsqueeze(1).broadcast_to([P, 5, 32]), mul)
        dve.drain()
        tt(ki, m.ki_c, m.param("idxb").unsqueeze(1).broadcast_to([P, 5, 32]), add)
        dve.drain()
        t = [r[:, :, 0, :] for r in m.rope_i]
        c = m.const("cos_i").rearrange("p (i f) -> p i f", f=4)
        sn = m.const("sin_i").rearrange("p (i f) -> p i f", f=4)
        rotate(ki[:, :, 0:4], ki[:, :, 4:8], c, sn, t).then_inc(s["rows_ready"], 1)
        dve.drain()
        dve.tensor_copy(m.KR[:, 0:NT].rearrange("p i (h d) -> p i h d", d=32),
                        m.A[:, 0:NT, C_KI:C_KI + 32].unsqueeze(2).broadcast_to([P, NT, 4, 32]))
        dve.tensor_copy(m.KR[0:NS, NT].rearrange("p (h d) -> p h d", d=32),
                        m.A[0:NS, NT, C_KI:C_KI + 32].unsqueeze(1).broadcast_to([NS, 4, 32]))
        dve.tensor_copy(m.wb_in[0:NS], m.A[0:NS, NT, C_WI:ACOLS].unsqueeze(2).broadcast_to([NS, 4, P]))
        dve.drain().then_inc(s["kr_ready"], 1)

    def taps(out, src, w, first, bias=None):
        n = len(w)
        width = SEQ if len(src.shape) == 2 else DS

        def at(k):
            return src[:, first + k:first + k + width] if len(src.shape) == 2 else src[:, :, first + k:first + k + width]

        ts(out, at(0), w[0], bias, mul, add) if bias is not None else ts(out, at(0), w[0], None, mul)
        for k in range(1, n):
            dve.drain()
            ins = stt(out, at(k), w[k], out, mul, add)
        return ins

    def columns(l):
        dve.wait_ge(s["rows_mm"], nth(l, "rows_mm", 10))
        dve.memset(m.Z[:, :, T:TP], 0.0)
        for f in m.fm_p:
            dve.memset(f[:, 0:3], 0.0)
        mu = m.param("mu")
        shift = m.param("shift").rearrange("p (n b) -> p n b", b=DB)
        for n in range(7):
            fp, fs = m.fm_p[n % 4], m.fm_s[n % 4]
            dve.tensor_copy(fs[:, :, 2], shift[:, n, :])
            dve.drain()
            dve.wait_ge(s["fm_copied"], nth(l, "fm_copied", n + 1))
            tt(m.diff[:, 0:SEQ], fp[:, 2:2 + SEQ], fp[:, 3:3 + SEQ], sub)
            tt(seqs(m.diff[:, SEQ:T]), fs[:, :, 2:6], fs[:, :, 3:7], sub)
            dve.drain()
            stt(m.Z[:, n, 0:SEQ], m.diff[:, 0:SEQ], mu[:, n:n + 1], fp[:, 3:3 + SEQ], mul, add)
            stt(seqs(m.Z[:, n, SEQ:T]), seqs(m.diff[:, SEQ:T]), mu[:, n:n + 1], fs[:, :, 3:7], mul, add)\
                .then_inc(s["fm_used"], 1)
            if n == 2:
                split_queries(l)
            elif n == 3:
                sample_sums(l)
            elif n >= 4:
                scores(l, 7 - n)
        start_selection(l)
        rounds = iter(range(17))

        def select_rounds(n):
            for _ in range(n):
                selection_round(next(rounds))

        select_rounds(3)
        convc = m.param("convc").rearrange("p (j b t) -> p j b t", j=2, b=DB)
        tail = m.small("convc").rearrange("p (j c) -> p j c", j=2)
        cw = m.param("cw")
        for j in range(2):
            n = 7 + 3 * j
            cg, xin, bg = n % 4, (n + 1) % 4, (n + 2) % 4
            dve.tensor_copy(m.fm_s[cg][:, :, 1:3], convc[:, j, :, :])
            dve.wait_ge(s["fm_copied"], nth(l, "fm_copied", n + 3))
            tt(m.fm_p[cg][:, 3:3 + SEQ], m.fm_p[cg][:, 3:3 + SEQ], m.fm_p[xin][:, 3:3 + SEQ], mul)
            tt(m.fm_s[cg][:, :, 3:7], m.fm_s[cg][:, :, 3:7], m.fm_s[xin][:, :, 3:7], mul)
            dve.drain()
            w = [cw[:, 3 * j + k:3 * j + k + 1] for k in range(3)]
            taps(m.conv[:, 0:SEQ], m.fm_p[cg], w, 1)
            taps(seqs(m.conv[:, SEQ:T]), m.fm_s[cg], w, 1)
            dve.tensor_copy(tail[:, j, 0:2], m.fm_p[cg][:, 1 + SEQ:3 + SEQ])
            dve.tensor_copy(tail[:, j, 2:18].rearrange("p (b t) -> p b t", t=2), m.fm_s[cg][:, :, 5:7])
            dve.drain()
            tt(m.yT[:, 4 + j, 0:SEQ], m.conv[:, 0:SEQ], m.fm_p[bg][:, 3:3 + SEQ], mul)
            tt(seqs(m.yT[:, 4 + j, SEQ:T]), seqs(m.conv[:, SEQ:T]), m.fm_s[bg][:, :, 3:7], mul).then_inc(s["fm_used"], 3)
            select_rounds((5, 4)[j])
        convd = m.param("convd").rearrange("p (j b t) -> p j b t", j=2, b=DB)
        tail = m.small("convd").rearrange("p (j c) -> p j c", j=2)
        dw, db = m.param("dw"), m.param("db")
        for j in range(2):
            n = 13 + 2 * j
            xb, gb = n % 4, (n + 1) % 4
            dve.tensor_copy(m.fm_s[xb][:, :, 0:3], convd[:, j, :, :])
            dve.drain()
            dve.wait_ge(s["fm_copied"], nth(l, "fm_copied", n + 2))
            w = [dw[:, 4 * j + k:4 * j + k + 1] for k in range(4)]
            taps(m.xc[:, j, 0:SEQ], m.fm_p[xb], w, 0, db[:, j:j + 1])
            taps(seqs(m.xc[:, j, SEQ:T]), m.fm_s[xb], w, 0, db[:, j:j + 1]).then_inc(s["conv_done"], 1)
            dve.tensor_copy(tail[:, j, 0:3], m.fm_p[xb][:, SEQ:3 + SEQ])
            dve.tensor_copy(tail[:, j, 3:27].rearrange("p (b t) -> p b t", t=3), m.fm_s[xb][:, :, 4:7])
            dve.tensor_copy(m.gb[:, j, 0:SEQ], m.fm_p[gb][:, 3:3 + SEQ])
            dve.tensor_copy(seqs(m.gb[:, j, SEQ:T]), m.fm_s[gb][:, :, 3:7]).then_inc(s["fm_used"], 2)
            select_rounds((3, 2)[j])
        finish_selection()
        dve.drain().then_inc(s["selected"], 1)

    def column_math(l):
        r, k, v = (m.Z[:, 2 * n:2 * n + 2, :] for n in range(3))
        for p in range(2):
            ts(m.nkk[:, p, :], k[:, p, :], m.param("kkw")[:, p:p + 1], None, mul)
        dve.drain()
        tt(m.bv, m.nkk, m.nkk, mul).then_inc(s["kk_in"], 1)
        dve.wait_ge(s["job_out"], nth(l, "job_out", 8))
        for p in range(2):
            dve.tensor_tensor_scan(m.en[:, p, :], m.const("reset"), m.ea[:, p, :], 0.0, mul, add)
        dve.drain()
        tt(m.ea, m.en, m.ea, sub).then_inc(s["cum_ready"], 1)
        dve.wait_ge(s["job_out"], nth(l, "job_out", 10))
        for p in range(2):
            ts(m.kf[:, p, :], m.aa[:, p, :], m.param("ka")[:, p:p + 1], m.omka[:, p:p + 1], mul, add)
        dve.drain()
        tt(m.kf, m.kf, k, mul)
        dve.drain()
        for p in range(2):
            stt(m.bonus[:, p, :], r[:, p, :], m.param("rk")[:, p:p + 1], m.kf[:, p, :], mul, mul)
        dve.drain().then_inc(s["bonus_in"], 1)
        dve.wait_ge(s["job_out"], nth(l, "job_out", 4))
        for p in range(2):
            ts(m.za[:, p, :], m.za[:, p, :], m.lam[6][:, p:p + 1], None, mul)
        dve.drain().then_inc(s["dz_ready"], 1)
        dve.wait_ge(s["fm_mm"], nth(l, "fm_mm", NCH))
        tt(m.gelu, m.gb, m.gb, mul)
        dve.drain()
        ts(m.gelu, m.gelu, 0.044715, 1.0, mul, add)
        dve.drain()
        tt(m.gelu, m.gelu, m.gb, mul).then_inc(s["gelu_in"], 1)
        dve.wait_ge(s["d_tanh"], nth(l, "d_tanh", 1))
        ts(m.za, m.za_tanh, 1.0, None, add)
        dve.drain()
        dve.reciprocal(m.za, m.za)
        dve.drain()
        stt(m.za, m.za, 2.0, m.za_tanh, mul, mul).then_inc(s["om_ready"], 1)
        tt(m.gx, m.gx, m.xc, mul)
        dve.wait_ge(s["gelu_tanh"], nth(l, "gelu_tanh", 1))
        stt(m.gelu, m.gelu, 1.0, m.gb, add, mul)
        dve.drain()
        dve.wait_ge(s["om_sqrt"], nth(l, "om_sqrt", 1))
        tt(m.gx, m.gx, m.za, mul)
        dve.drain()
        us, as_ = m.gx[:, :, SEQ:T].rearrange("p q (b t) -> p q b t", t=DS), m.a_lru[:, :, SEQ:T].rearrange("p q (b t) -> p q b t", t=DS)
        h0 = m.param("lru").rearrange("p (q b) -> p q b", b=DB)
        tt(m.hs[:, :, 0:DB], as_[:, :, :, 0], h0, mul)
        dve.drain()
        tt(us[:, :, :, 0], us[:, :, :, 0], m.hs[:, :, 0:DB], add)
        dve.memset(as_[:, :, :, 0], 0.0)
        dve.drain()
        for p in range(2):
            dve.tensor_tensor_scan(m.hs[:, p, :], m.a_lru[:, p, :], m.gx[:, p, :], 0.0, mul, add)
        dve.drain()
        tail = m.small("lru").rearrange("p (q c) -> p q c", q=2)
        dve.tensor_copy(tail[:, :, 0:1], m.hs[:, :, SEQ - 1:SEQ])
        dve.tensor_copy(tail[:, :, 1:9], m.hs[:, :, SEQ:T].rearrange("p q (b t) -> p q b t", t=DS)[:, :, :, DS - 1])\
            .then_inc(s["small_ready"], 1)
        for p in range(2):
            stt(m.yT[:, 6 + p, :], m.gelu[:, p, :], 0.5, m.hs[:, p, :], mul, mul)
        dve.drain()
        dve.memset(m.TB, 0.0).then_inc(s["states_zeroed"], 1)
        for t in (m.AE, m.BE, m.KE, m.VE, m.Tst):
            dve.memset(t, 0.0)
        dve.wait_ge(s["job_out"], nth(l, "job_out", 12))
        tt(m.bonus, m.bonus, v, mul)
        dve.wait_ge(s["job_out"], nth(l, "job_out", 14))
        ts(m.bv, m.bv, 1e-12, None, ALU.max)
        dve.drain()
        dve.reciprocal(m.bv, m.bv)
        dve.drain()
        stt(m.nkk, m.nkk, -1.0, m.bv, mul, mul)
        dve.drain()
        dve.drain()
        dve.wait_ge(s["exps_ready"], nth(l, "exps_ready", 1))
        stt(m.bv, m.nkk, -1.0, m.aa, mul, mul)
        dve.drain()

    def chunk_inputs(at, n):
        def chunks(t, rows):
            return t[rows, :, at].rearrange("p q (c t) -> p c q t", t=CH)

        def four(t):
            return t.rearrange("p (c q) n -> p c q n", q=2)[:, 0:n]

        r, v = m.Z[:, 0:2, :], m.Z[:, 4:6, :]
        for h in range(2):
            rows = slice(64 * h, 64 * h + 64)
            for c in range(n):
                def cut(t):
                    return chunks(t, rows)[:, c]

                def put(t):
                    return four(t)[rows, c, :, rows]
                tt(put(m.AE), cut(m.nkk), cut(m.ea), mul)
                tt(put(m.BE), cut(m.bv), cut(m.en), mul)
                tt(put(m.KE), cut(m.kf), cut(m.en), mul)
                dve.tensor_copy(put(m.VE), cut(v))
        everyone = slice(0, P)
        for c in range(n):
            tt(four(m.RC)[:, c], chunks(r, everyone)[:, c], chunks(m.ec, everyone)[:, c], mul)

    def flat(t, n=4):
        return t[:, 0:n, :].rearrange("p k n -> p (k n)")

    def mask(out, bank, name, n):
        w = CONST[name][1]
        k = 8 if w == CH else n
        return tt(out, ps[:, bank, 0:k * w].rearrange("p (k n) -> p k n", n=w),
                  m.const(name).unsqueeze(1).broadcast_to([P, k, w]), mul)

    def rwkv_loop(l):
        eye = ident.unsqueeze(1).broadcast_to([P, 2, P])
        with dve.Fori(0, 4) as g:
            def mm(n):
                dve.wait_ge(s["rw_mm"], nth(l, "rw_mm", g * RW_PE + n))

            dve.drain()
            mm(0)
            chunk_inputs(bass.ds(g * (2 * CH), 2 * CH), 2)
            for c in range(2):
                dve.tensor_copy(m.pc[:, c, :], m.ec[:, :, bass.ds(g * (2 * CH) + (c * CH + CH - 1), 1)]
                                .rearrange("p q z -> p (q z)"))
            dve.drain().then_inc(s["rw_in"], 1)
            mm(1)
            mask(m.D, 0, "strict_near", 4).then_inc(s["rw_v"], 1)
            mask(m.DT, 1, "strict_near_t", 4).then_inc(s["rw_v"], 1)
            mask(m.E, 0, "strict_far", 4).then_inc(s["rw_v"], 1)
            mask(m.Mak, 2, "strict", 4).then_inc(s["rw_v"], 1)
            mask(m.attn.rearrange("p a k t -> p (a k) t"), 3, "incl", 4).then_inc(s["rw_v"], 1)
            for n, bank, to in (((3, 5), 0, m.D2), ((7, 9), 2, m.D4)):
                for c in range(2):
                    mm(n[c])
                    dve.tensor_copy(to[:, 2 * c:2 * c + 2, :].rearrange("p k n -> p (k n)"), ps[:, 4 * c + bank, 0:2 * P])\
                        .then_inc(s["rw_v"], 1)

            def grow(n, bank, to, plus):
                dve.drain()
                for c in range(2):
                    mm(n + c)
                    k = slice(2 * c, 2 * c + 2)
                    tt(to[:, k, :], ps[:, 4 * c + bank, 0:2 * P].rearrange("p (k n) -> p k n", n=P),
                       eye if plus is None else plus[:, k, :], add).then_inc(s["rw_v"], 1)

            grow(11, 0, m.X, None)
            grow(13, 1, m.X, m.X)
            grow(15, 2, m.X, m.X)
            grow(17, 3, m.X, m.X)
            grow(23, 2, m.Zs, m.X)
            grow(25, 3, m.Zs, m.X)
            grow(27, 0, m.Zs, m.X)
            for c in range(2):
                mm(29 + 3 * c)
                dve.tensor_copy(flat(m.W, 2), ps[:, 4, 0:256]).then_inc(s["rwc_v"], 1)
                mm(30 + 3 * c)
                dve.tensor_copy(flat(m.U, 2), ps[:, 5, 0:256]).then_inc(s["rwc_v"], 1)
                mm(31 + 3 * c)
                tt(m.Tst, ps[:, 6, 0:256].rearrange("p (q n) -> p q n", n=P),
                   m.pc[:, c, :].unsqueeze(2).broadcast_to([P, 2, P]), mul).then_inc(s["rwc_v"], 1)

    def rwkv_sample(l):
        chunk_inputs(slice(SEQ, TP), 1)
        dve.drain()
        dve.memset(m.AEb, 0.0)
        dve.drain()
        for p in range(2):
            for h in range(2):
                src = m.AE[:, p, 64 * h:64 * h + NS]
                for b in range(DB):
                    c = 64 * h + DS * b
                    ins = dve.tensor_copy(m.AEb[:, p, b, c:c + DS], src[:, DS * b:DS * b + DS])
        ins.then_inc(s["rws_in"], 1)
        dve.wait_ge(s["rws_mm"], nth(l, "rws_mm", 1))
        mask(m.D[:, 0:2], 0, "s_strict", 2)
        mask(m.DT[:, 0:2], 1, "s_strict_t", 2)
        mask(m.Mak[:, 0:2], 2, "s_strict", 2)
        for a in range(2):
            tt(m.attn[:, a, 0:2, :], ps[:, 3, 256 * a:256 * a + 128].rearrange("p (k n) -> p k n", n=CH),
               m.const("s_incl").unsqueeze(1).broadcast_to([P, 2, CH]), mul)
        dve.drain().then_inc(s["rws_v"], 1)
        dve.wait_ge(s["rws_mm"], nth(l, "rws_mm", 3))
        tt(m.X[:, 0:2], ps[:, 0, 0:256].rearrange("p (k n) -> p k n", n=P), ident.unsqueeze(1).broadcast_to([P, 2, P]), add)\
            .then_inc(s["rws_v"], 1)
        dve.drain()
        dve.wait_ge(s["rws_mm"], nth(l, "rws_mm", 4))
        tt(m.X[:, 0:2], ps[:, 1, 0:256].rearrange("p (k n) -> p k n", n=P), m.X[:, 0:2], add).then_inc(s["rws_v"], 1)
        dve.wait_ge(s["rws_mm"], nth(l, "rws_mm", 5))
        dve.tensor_copy(flat(m.W, 2), ps[:, 4, 0:256]).then_inc(s["rws_v"], 1)
        dve.wait_ge(s["rws_mm"], nth(l, "rws_mm", 6))
        dve.tensor_copy(flat(m.U, 2), ps[:, 5, 0:256]).then_inc(s["rws_v"], 1)
        ec = m.ec[:, :, SEQ:T].rearrange("p q (b t) -> p q b t", t=DS)
        own = m.const("s_rows").unsqueeze(2).broadcast_to([P, DB, P])
        for p in range(2):
            dve.drain()
            dve.wait_ge(s["rws_a"], nth(l, "rws_a", 1))
            if p:
                dve.wait_ge(s["rws_mm"], nth(l, "rws_mm", 8))
            tt(m.UEb, m.U[:, p, :].unsqueeze(1).broadcast_to([P, DB, P]), own, mul)
            tt(m.VEb, m.VEt[:, p, :].unsqueeze(1).broadcast_to([P, DB, P]), own, mul)
            dve.drain().then_inc(s["rws_v"], 1)
            dve.wait_ge(s["rws_mm"], nth(l, "rws_mm", 8 + p))
            for h in range(2):
                ins = tt(m.TB[:, p, 4 * h:4 * h + 4, :], ps[:, 2 * p + h, :].rearrange("p (b n) -> p b n", n=P),
                         ec[:, p, 4 * h:4 * h + 4, DS - 1].unsqueeze(2).broadcast_to([P, 4, P]), mul)
            ins.then_inc(s["rws_v"], 1)

    def rwkv_out(l):
        dve.wait_ge(s["rws_a"], nth(l, "rws_a", 2))
        dve.wait_ge(s["yn_mm"], nth(l, "yn_mm", 1))
        for p in range(2):
            stt(m.yc[:, p, 0:SEQ], ps[:, 2 * p, :], -1.0 / 64, m.yb[:, p, 0:SEQ], mul, add)
            stt(m.yc[:, p, SEQ:TP], ps[:, 2 * p + 1, 0:64], -1.0 / 64, m.yb[:, p, SEQ:TP], mul, add)
        dve.drain()
        tt(m.y2, m.yc, m.yc, mul).then_inc(s["yn_in"], 1)
        dve.wait_ge(s["yn_std"], nth(l, "yn_std", 1))
        dve.reciprocal(m.ec, m.ec)
        dve.drain()
        tt(m.yc, m.yc, m.ec, mul)
        dve.drain()
        for p in range(2):
            ts(m.yc[:, p, :], m.yc[:, p, :], m.param("lnxg")[:, p:p + 1], m.param("lnxb")[:, p:p + 1], mul, add)
        dve.drain()
        tt(m.yc, m.yc, m.bonus, add)
        dve.drain()
        tt(m.yT[:, 2:4, :], m.yc[:, :, 0:T], m.gate[:, :, 0:T], mul).then_inc(s["rw_done"], 1)

    def split_queries(l):
        dve.drain()
        dve.wait_ge(s["tr_sample"], nth(l, "tr_sample", 2))
        for j in range(4):
            for h in range(4):
                src = m.qiT[32 * h:32 * h + 32, SEQ:T].rearrange("p (g j t) -> p g j t", g=2, t=DS)
                dve.tensor_copy(m.QI[32 * j:32 * j + 32, :, h, :], src[:, :, j, :])
        dve.drain().then_inc(s["s_prep"], 1)

    def sample_sums(l):
        dve.wait_ge(s["s_relu"], nth(l, "s_relu", 1))
        R = m.relu[0].rearrange("p (c n) -> p c n", c=4)
        tt(R, R, m.WB.rearrange("p b h t -> p (b h t)").unsqueeze(1).broadcast_to([P, 4, P]), mul)
        dve.drain()
        R = m.relu[0].rearrange("p (c h t) -> p c h t", h=4, t=DS)
        S4 = m.sums.rearrange("p c (b t) -> p (c b) t", t=DS)
        tt(S4, R[:, :, 0, :], R[:, :, 1, :], add)
        for h in (2, 3):
            dve.drain()
            ins = tt(S4, S4, R[:, :, h, :], add)
        ins.then_inc(s["s_sums"], 1)
        new = m.score[3][0:NS, PAST:T]
        ts(new, m.relu_n[0:NS, 0, :], m.A[0:NS, NT, C_WI:C_WI + 1], None, mul)
        for h in range(1, 4):
            dve.drain()
            stt(new, m.relu_n[0:NS, h, :], m.A[0:NS, NT, C_WI + h:C_WI + h + 1], new, mul, add)
        dve.drain()
        tt(new, new, m.const("new_bias")[0:NS], add)
        dve.drain()

    def scores(l, i):
        w, c = P * (i + 1), 3 - i
        for h in range(4):
            dve.drain()
            dve.wait_ge(s["relu_done"], nth(l, "relu_done", 4 * c + h + 1))
            wi = m.A[:, i, C_WI + h:C_WI + h + 1]
            if h:
                ins = stt(m.score[c], m.relu[h % 2][:, 0:w], wi, m.score[c], mul, add)
            else:
                ins = ts(m.score[c], m.relu[0][:, 0:w], wi, None, mul)
            ins.then_inc(s["rl_used"], 1)
        dve.drain()
        tt(m.score[c][:, w - P:w], m.score[c][:, w - P:w], m.const("causal"), add)
        dve.drain()

    CHAINS = [(slice(0, P), TOPK_P)] * 3 + [(slice(0, NS), TOPK_S)]

    def start_selection(l):
        dve.drain()
        dve.wait_ge(s["s_score"], nth(l, "s_score", 1))
        for c, (rows, _) in enumerate(CHAINS):
            dve.tensor_copy(m.work[c][rows], m.score[c][rows])
        dve.drain()

    def selection_round(r):
        for c, (rows, topk) in enumerate(CHAINS):
            if r <= (topk - 1) // 8:
                dve.max(m.top8[c][rows], m.work[c][rows])
        dve.drain()
        for c, (rows, topk) in enumerate(CHAINS):
            if r < (topk - 1) // 8:
                dve.match_replace(m.work[c][rows], m.top8[c][rows], m.work[c][rows], -3e38)
        dve.drain()

    def finish_selection():
        for c, (rows, topk) in enumerate(CHAINS):
            last = (topk - 1) % 8
            thr = m.top8[c][rows, last:last + 1]
            ts(m.work[c][rows], m.score[c][rows], thr, None, ALU.is_gt)
            ts(m.eq[c][rows], m.score[c][rows], thr, None, ALU.is_equal)
        dve.drain()
        for c, (rows, topk) in enumerate(CHAINS):
            dve.tensor_reduce(m.cnt[c][rows, 0:1], m.work[c][rows], AX.X, add)
            dve.tensor_tensor_scan(m.pre[c][rows], m.const("ones")[rows].broadcast_to([rows.stop, m.chain_w[c]]), m.eq[c][rows],
                                   0.0, mul, add)
        dve.drain()
        for c, (rows, topk) in enumerate(CHAINS):
            ts(m.cnt[c][rows, 1:2], m.cnt[c][rows, 0:1], -1.0, float(topk), mul, add)
        dve.drain()
        for c, (rows, topk) in enumerate(CHAINS):
            stt(m.pre[c][rows], m.pre[c][rows], m.cnt[c][rows, 1:2], m.eq[c][rows], ALU.is_le, mul)
        dve.drain()
        for c, (rows, topk) in enumerate(CHAINS):
            tt(m.pre[c][rows], m.pre[c][rows], m.work[c][rows], add)
        dve.drain()
        for c, (rows, topk) in enumerate(CHAINS):
            ts(m.bias[c][rows], m.pre[c][rows], 1.0, -NEG, sub, mul)
        dve.drain()
        for c in range(3):
            w = m.chain_w[c]
            tt(m.bias[c][:, w - P:w], m.bias[c][:, w - P:w], m.const("causal"), add)
        tt(m.bias[3][0:NS, PAST:T], m.bias[3][0:NS, PAST:T], m.const("new_bias")[0:NS], add)
        dve.drain()

    def attention(l):
        dve.memset(m.QB, 0.0)
        dve.drain()
        for p in range(2):
            for h in range(2):
                q = slice(64 * h, 64 * h + 64)
                dve.tensor_copy(m.QB[q, p, :, DS * (2 * p + h):DS * (2 * p + h) + DS], seqs(m.qT[q, p, SEQ:T]))
        dve.drain().then_inc(s["qb_ready"], 1)

        def masked(i):
            w = P * (i + 1)
            x = m.lg[i % 2][:, :, 0:w]
            bias = m.bias[3 - i] if i else m.const("causal")
            dve.wait_ge(s["lg_mm"], nth(l, "lg_mm", i + 1))
            if i >= 2:
                dve.wait_ge(s["pt_mm"], nth(l, "pt_mm", 4 * (i - 1)))
            tt(x, ps[:, 0:4, 0:w], bias.unsqueeze(1).broadcast_to([P, 4, w]), add).then_inc(s["lg_taken"], 1)
            dve.drain()
            dve.tensor_reduce(m.nmax[i % 2], x, AX.X, ALU.max, negate=True).then_inc(s["lg_ready"], 1)

        def normed(i):
            w = P * (i + 1)
            x = m.lg[i % 2][:, :, 0:w]
            dve.wait_ge(s["p_exp"], nth(l, "p_exp", i + 1))
            dve.reciprocal(m.rsum[i % 2], m.ssum[i % 2])
            dve.drain()
            tt(x, x, m.rsum[i % 2].unsqueeze(2).broadcast_to([P, 4, w]), mul).then_inc(s["p_ready"], 1)

        masked(0)
        masked(1)
        normed(0)
        normed(1)
        for i in (2, 3):
            masked(i)
            normed(i)

        for g in range(2):
            dve.wait_ge(s["s_lg"], nth(l, "s_lg", g + 1))
            dve.tensor_reduce(m.nmax[g][:, 0:1], m.s_lg[g], AX.X, ALU.max, negate=True).then_inc(s["s_max"], 1)
        for g in range(2):
            dve.wait_ge(s["s_exp"], nth(l, "s_exp", g + 1))
            dve.reciprocal(m.rsum[g][:, 0:1], m.ssum[g][:, 0:1])
            dve.drain()
            ts(m.s_lg[g], m.s_lg[g], m.rsum[g][:, 0:1], None, mul).then_inc(s["s_p"], 1)

    def norm(l, first, residual):
        def stats(i):
            n = P if i < NT else NS
            if residual:
                dve.wait_ge(s["x_back"], nth(l, "x_back", 32))
                dve.wait_ge(s["mix_mm"], nth(l, "mix_mm", i + 1))
                xr = m.x[0:n, i, :].rearrange("p (h d) -> p h d", h=2)
                stt(xr, xr, ALPHA, ps[0:n, 2 * (i % 2):2 * (i % 2) + 2, :], mul, add)
                dve.drain()
            else:
                dve.wait_ge((s["yg0_in"], s["yg1_in"], s["yg2_in"], s["yg3_in"], s["yg4_in"])[i], nth(l, f"yg{i}_in", 32))
                for k, gate in enumerate((m.gate_hi, m.gate_lo)):
                    stt(m.x[0:n, i, :], m.yg[0:n, i, k, :], gate[0:n, i:i + 1], m.x[0:n, i, :], mul, add)
                    dve.drain()
            for h in range(2):
                dve.bn_stats(m.bn[i % 2][0:n, h, :], m.x[0:n, i, 512 * h:512 * h + 512])
            dve.drain()
            dve.bn_aggr(m.mv[i % 2][0:n], m.bn[i % 2][0:n]).then_inc(s["ln_var"], 1)

        def scale(i):
            n = P if i < NT else NS
            dve.wait_ge(s["ln_std"], nth(l, "ln_std", first + i + 1))
            dve.reciprocal(m.std[i % 2][0:n], m.std[i % 2][0:n])
            dve.drain()
            ts(m.x[0:n, i, :], m.x[0:n, i, :], m.mv[i % 2][0:n, 0:1], m.std[i % 2][0:n], sub, mul)
            dve.drain()
            tt(m.x[0:n, i, :], m.x[0:n, i, :], m.ln[0:n, 0, :], mul).then_inc(s["ln_mid"], 1)

        dve.wait_ge(s["ln_in"], nth(l, "ln_in", 16 + 16 * (first > 0)))
        stats(0)
        for i in range(1, 5):
            stats(i)
            scale(i - 1)
            dve.drain()
        scale(4)

    def router(l):
        G, S_, (a, b, c) = m.gsel, m.gsig, m.g16
        g0, g1, g2, g3 = m.g4
        tt(G, S_, m.router_bias.unsqueeze(1).broadcast_to([P, 5, NEXP]), add)
        dve.drain()
        G4 = G.rearrange("p i (g e) -> p i g e", e=4)
        lo, hi = [G4[:, :, :, k] for k in (0, 2)], [G4[:, :, :, k] for k in (1, 3)]
        tt(g0, lo[0], hi[0], ALU.max)
        tt(g1, lo[0], hi[0], ALU.min)
        tt(g2, lo[1], hi[1], ALU.max)
        tt(g3, lo[1], hi[1], ALU.min)
        dve.drain()
        tt(g1, g1, g3, ALU.max)
        dve.drain()
        tt(g3, g0, g2, ALU.min)
        dve.drain()
        tt(g0, g0, g2, ALU.max)
        dve.drain()
        tt(g1, g1, g3, ALU.max)
        dve.drain()
        tt(g0, g0, g1, add)
        dve.drain()

        def first_best(value, order, scratch, best):
            w = value.shape[2]
            dve.tensor_reduce(best, value, AX.X, ALU.max)
            dve.drain()
            tt(scratch, value, best.unsqueeze(2).broadcast_to([P, 5, w]), ALU.is_equal)
            dve.drain()
            tt(scratch, scratch, m.const(order).unsqueeze(1).broadcast_to([P, 5, w]), mul)
            dve.drain()
            dve.tensor_reduce(best, scratch, AX.X, ALU.max)
            dve.drain()
            tt(scratch, m.const(order).unsqueeze(1).broadcast_to([P, 5, w]), best.unsqueeze(2).broadcast_to([P, 5, w]),
               ALU.is_equal)
            dve.drain()

        first_best(g0, "group_order", g1, m.g1[0])
        ts(g1, g1, 1.0, -NEG, sub, mul)
        dve.drain()
        tt(G4, G4, g1.unsqueeze(3).broadcast_to([P, 5, 4, 4]), add)
        dve.drain()
        first_best(G, "expert_order", a, m.g1[0])
        stt(G, a, NEG, G, mul, add)
        dve.drain()
        first_best(G, "expert_order", b, m.g1[0])
        tt(a, a, b, add)
        ts(m.before, m.const("causal"), 0.0, None, ALU.is_lt)
        dve.memset(m.all1, 1.0)
        dve.drain()
        dve.tensor_copy(m.chosen, a)
        dve.drain().then_inc(s["chosen"], 1)
        tt(a, a, S_, mul)
        dve.drain()
        dve.tensor_reduce(m.g1[1], a, AX.X, add)
        dve.drain()
        dve.reciprocal(m.g1[2], m.g1[1])
        dve.drain()
        tt(m.gates, a, m.g1[2].unsqueeze(2).broadcast_to([P, 5, NEXP]), mul)

    def dispatch(l):
        order = m.const("expert_order")
        dve.wait_ge(s["slots_mm"], nth(l, "slots_mm", 1))
        pos = ps[:, 6, 0:5 * NEXP].rearrange("p (i e) -> p i e", e=NEXP)
        total = ps[:, 6, 5 * NEXP:6 * NEXP]
        ts(m.extra, total, float(P), None, ALU.is_gt)
        for k in range(2, -(-T // P)):
            dve.drain()
            stt(m.extra, total, float(P * k), m.extra, ALU.is_gt, add)
        dve.drain()
        dve.tensor_tensor_scan(m.extra_sum, m.const("ones").broadcast_to([P, NEXP]), m.extra, 0.0, mul, add)
        ts(m.own, order, -float(P), float(P * NEXP), mul, add)
        dve.drain()
        tt(m.shift_to, m.extra_sum, m.extra, sub)
        dve.drain()
        ts(m.shift_to, m.shift_to, float(NEXP - 1), float(P), add, mul)
        dve.drain()
        tt(m.shift_to, m.shift_to, m.own, sub)
        ts(m.slot, pos, float(P), None, ALU.is_ge)
        dve.drain()
        tt(m.slot, m.slot, m.shift_to.unsqueeze(1).broadcast_to([P, 5, NEXP]), mul)
        dve.drain()
        tt(m.slot, m.slot, pos, add)
        dve.drain()
        tt(m.slot, m.slot, m.own.unsqueeze(1).broadcast_to([P, 5, NEXP]), add)
        dve.drain()
        stt(m.slot, m.slot, 1.0, m.chosen, add, mul)
        dve.drain()
        dve.tensor_reduce(m.hi, m.slot, AX.X, ALU.max)
        dve.tensor_reduce(m.lo, m.slot, AX.X, add)
        dve.drain()
        tt(m.lo, m.lo, m.hi, sub)
        tt(m.hot_hi, m.slot, m.hi.unsqueeze(2).broadcast_to([P, 5, NEXP]), ALU.is_equal)
        dve.drain()
        tt(m.hot_lo, m.slot, m.lo.unsqueeze(2).broadcast_to([P, 5, NEXP]), ALU.is_equal)
        tt(m.hot_hi, m.hot_hi, m.gates, mul)
        ts(m.slots[:, 0, :], m.hi, -1.0, None, add)
        ts(m.slots[:, 1, :], m.lo, -1.0, None, add)
        dve.drain()
        tt(m.hot_lo, m.hot_lo, m.gates, mul)
        ts(m.extra_blocks, m.extra_sum[0:1, NEXP - 1:NEXP], 0.0, None, add)
        dve.tensor_reduce(m.gate_hi, m.hot_hi, AX.X, add)
        tt(m.beyond[0:1], m.extra_sum[0:1].unsqueeze(1).broadcast_to([1, 8, NEXP]),
           order[0:1, 0:8].unsqueeze(2).broadcast_to([1, 8, NEXP]), add)
        dve.drain()
        dve.tensor_reduce(m.gate_lo, m.hot_lo, AX.X, add)
        ts(m.beyond[0:1], m.beyond[0:1], float(NEXP), None, ALU.is_le)
        dve.drain()
        dve.tensor_reduce(m.count[0:1], m.beyond[0:1], AX.X, add)
        dve.drain()
        ts(m.extra_expert, m.count[0:1], float(NEXP - 1), None, ALU.min)
        dve.drain().then_inc(s["idx_ready"], 1)

    def experts(l):
        dve.wait_ge(s["router_sig"], nth(l, "router_sig", 1))
        router(l)
        dispatch(l)
        dve.wait_ge(s["x_scattered"], nth(l, "x_scattered", 160))
        dve.wait_ge(s["xt_mm"], nth(l, "xt_mm", 5))
        for i in range(5):
            n = P if i < NT else NS
            ts(m.x[0:n, i, :], m.x[0:n, i, :], ALPHA, None, mul)

        def hidden(e, k):
            dve.wait_ge(s["silu_done"], nth(l, "silu_done", e * 2 + (k + 1)))
            tt(m.h, m.silu, ps[:, 3, DEXP:2 * DEXP], mul).then_inc(s["h_ready"], 1)

        def hidden_columns(e, k):
            dve.wait_ge(s["ht_mm"], nth(l, "ht_mm", e * 2 + (k + 1)))
            dve.tensor_copy(m.hT.rearrange("p f n -> p (f n)"), ps[:, 2, 0:DEXP]).then_inc(s["ht_copied"], 1)

        def rows_back(e, k):
            dve.wait_ge((s["y0_stored"], s["y1_stored"])[k], nth(l, f"y{k}_stored", e * 16))
            dve.wait_ge(s["down_mm"], nth(l, "down_mm", e * 2 + (k + 1)))
            dve.tensor_copy(m.y[k][:, 512:DM], ps[:, 6, :]).then_inc(s["y_copied_v"], 1)

        hidden(0, 0)
        with dve.Fori(0, NEXP // 2 - 1) as e:
            for k in range(2):
                hidden_columns(e, k)
                rows_back(e, k)
                hidden(e + k, 1 - k)
        e = NEXP // 2 - 1
        hidden_columns(e, 0)
        rows_back(e, 0)
        hidden(e, 1)
        hidden_columns(e, 1)
        rows_back(e, 1)
        extra = dve.value_load(m.extra_blocks, min_val=0, max_val=BLOCKS - NEXP)
        with dve.Fori(NEXP // 2, BLOCKS // 2) as e:
            with dve.If(extra > e * 2 - NEXP):
                for k in range(2):
                    hidden(e, k)
                    hidden_columns(e, k)
                    rows_back(e, k)
            with dve.If(extra <= e * 2 - NEXP):
                dve.wait_ge(s["ht_mm"], nth(l, "ht_mm", e * 2 + 2))
                dve.wait_ge(s["silu_done"], nth(l, "silu_done", e * 2 + 2)).then_inc(s["h_ready"], 2)
                dve.drain().then_inc(s["ht_copied"], 2)
                dve.drain().then_inc(s["y_copied_v"], 2)

    dve.memset(m.A[:, NT, :], 0.0)
    dve.memset(m.gsig[:, NT, :], 1.0)
    dve.drain().then_inc(s["zeroed"], 1)
    for name in ("h_ready", "ht_copied", "y_copied_v"):
        dve.drain().then_inc(s[name], 1)
    dve.wait_ge(s["const_in"], 64)
    with dve.Fori(0, DEPTH) as l:
        dve.wait_ge(s["params_in"], nth(l, "params_in", 16))
        softplus(l)
        row_stage(l)
        columns(l)
        column_math(l)
        rwkv_loop(l)
        rwkv_sample(l)
        rwkv_out(l)
        attention(l)
        norm(l, 0, True)
        experts(l)
        norm(l, 5, False)


def kernel(x_prompt, x_sample, cache_k, cache_v, cache_ik, page_table, state_rwkv, state_rwkv_shift,
           state_conv_c, state_conv_d, state_lru, w_in, w_out, idx_ln_g, idx_ln_b, rwkv_mu, rwkv_w0,
           rwkv_w2, rwkv_a0, rwkv_a2, rwkv_g2, rwkv_kk, rwkv_ka, rwkv_rk, rwkv_lnx_g, rwkv_lnx_b,
           convc_w, convd_w, convd_b, lru_gx_w, lru_gx_b, lru_ga_w, lru_ga_b, lru_lam,
           ln1_g, ln1_b, ln2_g, ln2_b, w_router, router_bias, moe_w_gate, moe_w_up, moe_w_down):
    import concourse.bacc as bacc
    from concourse.bass_utils import run_bass_kernel_spmd

    def arr(a):
        return np.asarray(a)

    L = DEPTH
    xs = arr(x_sample).reshape(NS, DM)
    xp = arr(x_prompt).reshape(SEQ, DM)
    w_in, w_out = arr(w_in), arr(w_out)

    def by_rows(w):
        *lead, k, n = w.shape
        return np.moveaxis(w.reshape(*lead, k // P, P, n), -3, -2)

    b0, c0, d0 = ACOLS, ACOLS + 896, ACOLS + 896 + 768
    starts = [b0 + P * n for n in range(7)]
    for j in range(2):
        starts += [c0 + WA + P * j, c0 + 2 * WA + P * j, c0 + P * j]
    for j in range(2):
        starts += [d0 + P * j, d0 + WA + P * j]
    wf = np.stack([w_in[:, :, a:a + P] for a in starts], 1)
    gu = np.stack([by_rows(arr(moe_w_gate)), by_rows(arr(moe_w_up))], -2)

    params = np.zeros((L, P, PARAM_W), np.float32)

    def put(name, a, rows=slice(0, P)):
        at, w = PARAM[name]
        params[:, rows, at:at + w] = a.reshape(L, -1, w)

    def cols(a, n=2):
        return np.moveaxis(arr(a).reshape(L, n, P), 1, 2)

    put("mu", cols(rwkv_mu, 7))
    for name, a in (("w0", rwkv_w0), ("a0", rwkv_a0), ("kkw", rwkv_kk), ("ka", rwkv_ka), ("rk", arr(rwkv_rk).reshape(L, WA)),
                    ("lnxg", rwkv_lnx_g), ("lnxb", rwkv_lnx_b), ("db", convd_b), ("gxb", lru_gx_b), ("gab", lru_ga_b),
                    ("lam", lru_lam)):
        put(name, cols(a))
    put("cw", arr(convc_w).reshape(L, 3, 2, P).transpose(0, 3, 2, 1))
    put("dw", arr(convd_w).reshape(L, 4, 2, P).transpose(0, 3, 2, 1))
    put("shift", arr(state_rwkv_shift).reshape(L, DB, 7, P).transpose(0, 3, 2, 1))
    put("convc", arr(state_conv_c).reshape(L, DB, 2, 2, P).transpose(0, 4, 3, 1, 2))
    put("convd", arr(state_conv_d).reshape(L, DB, 3, 2, P).transpose(0, 4, 3, 1, 2))
    put("lru", arr(state_lru).reshape(L, DB, 2, P).transpose(0, 3, 2, 1))
    put("lora", np.concatenate([arr(rwkv_w2), arr(rwkv_a2), arr(rwkv_g2)], 1))
    for name, w in (("gxw", lru_gx_w), ("gaw", lru_ga_w)):
        g = np.zeros((L, P, 2, P), np.float32)
        for h in range(4):
            q = slice(64 * (h % 2), 64 * (h % 2) + 64)
            g[:, q, h // 2, q] = arr(w)[:, h]
        put(name, g)
    put("idxg", np.repeat(arr(idx_ln_g)[:, None], P, 1))
    put("idxb", np.repeat(arr(idx_ln_b)[:, None], P, 1))

    table = arr(page_table)
    arrays = {
        "consts": constants(),
        "page_table": table.reshape(1, DB * NPAGE).astype(np.int32),
        "xT": np.concatenate([xp, xs]).T.reshape(KC, P, T).transpose(1, 0, 2),
        "x": np.concatenate([xp, xs]),
        "w_router": by_rows(arr(w_router)), "router_bias": arr(router_bias),
        "wa": by_rows(w_in[:, :, 0:ACOLS]),
        "wf": by_rows(wf).reshape(L * NCH, P, KC, P),
        "wout": by_rows(w_out),
        "params": params,
        "ln": np.stack([np.stack([arr(ln1_g), arr(ln1_b)], 1), np.stack([arr(ln2_g), arr(ln2_b)], 1)], 1).reshape(2 * L, 2, DM),
        "state_rwkv": arr(state_rwkv).transpose(0, 2, 4, 1, 3).reshape(L, WA, DB, 64),
        "cache_k": arr(cache_k).reshape(L * NPHYS, PAGE, 2, P).transpose(0, 3, 2, 1),
        "cache_v": arr(cache_v).reshape(L * NPHYS, PAGE, WA),
        "cache_ik": arr(cache_ik).reshape(L * NPHYS, PAGE, 32).transpose(0, 2, 1),
        "w_gu": gu.reshape(L * NEXP, P, KC, 2, DEXP),
        "w_dn": by_rows(arr(moe_w_down)).reshape(L * NEXP, P, 2, DM),
    }
    outs = {
        "x": (L + 1, T, DM), "k_p": (L, SEQ, WA), "v_p": (L, SEQ, WA), "ik_p": (L, SEQ, 32),
        "k_s": (L, NS, WA), "v_s": (L, NS, WA), "ik_s": (L, NS, 32), "small": (L, P, SMALL_W),
        "state_p": (L, WA, 64), "state_s": (L, WA, DB, 64),
    }
    nc = bacc.Bacc("TRN2", target_bir_lowering=False, num_devices=1)
    arrays = {k: np.ascontiguousarray(a) for k, a in arrays.items()}
    din = {k: nc.dram_tensor("in_" + k, a.shape, mybir.dt.from_np(a.dtype), kind="ExternalInput").ap()
           for k, a in arrays.items()}
    dout = {k: nc.dram_tensor("out_" + k, shape, F32, kind="ExternalOutput").ap() for k, shape in outs.items()}
    program(nc, din, dout)
    r = run_bass_kernel_spmd(nc, [{"in_" + k: a for k, a in arrays.items()}], core_ids=[0]).results[0]
    o = {k: np.asarray(r["out_" + k]) for k in outs}

    def piece(name, n):
        at, w = SMALL[name]
        return o["small"][:, :, at:at + w].reshape(L, P, n, w // n)

    shift = piece("shift", 7)
    shift = shift.transpose(0, 3, 2, 1).reshape(L, 9, 1, 896)
    cc = piece("convc", 2).transpose(0, 3, 2, 1).reshape(L, 18, WA)
    cd = piece("convd", 2).transpose(0, 3, 2, 1).reshape(L, 27, WA)
    lru = piece("lru", 2).transpose(0, 3, 2, 1).reshape(L, 9, WA)
    sp = o["state_p"].reshape(L, 1, 4, 64, 64).transpose(0, 1, 2, 4, 3)
    ss = o["state_s"].reshape(L, 4, 64, DB, 64).transpose(0, 3, 1, 4, 2)
    return (
        o["x"][L, 0:SEQ].reshape(1, SEQ, DM), o["x"][L, SEQ:].reshape(DB, DS, DM),
        o["k_p"].reshape(L, 1, SEQ, 4, 64), o["v_p"].reshape(L, 1, SEQ, 4, 64), o["ik_p"].reshape(L, 1, SEQ, 32),
        sp, shift[:, 0:1], cc[:, 0:2].reshape(L, 1, 2, WA), cd[:, 0:3].reshape(L, 1, 3, WA), lru[:, 0:1],
        o["k_s"].reshape(L, DB, DS, 4, 64), o["v_s"].reshape(L, DB, DS, 4, 64), o["ik_s"].reshape(L, DB, DS, 32),
        ss, shift[:, 1:], cc[:, 2:].reshape(L, DB, 2, WA), cd[:, 3:].reshape(L, DB, 3, WA), lru[:, 1:],
    )
```
